# Optimizing a Trainium2 kernel written in Bass

```python
import jax, jax.numpy as jnp
from jax import lax
import numpy as np
import jax
import jax.numpy as jnp

D_MODEL = 1024
BATCH = 1
SEQ = 512
DEPTH = 1

PLE_DIM = 256
EPS = 1e-6
A_HEAD_DIM = 128
A_HEADS = (D_MODEL // 2) // A_HEAD_DIM
A_DIM = A_HEADS * A_HEAD_DIM
QKV_CONV_WIDTH = 4
CHUNK = 64
POOL_WINDOWS = (2, 4, 8, 16)
POOL_GROUPS = len(POOL_WINDOWS)
POOL_DIM = D_MODEL // 4
POOL_GROUP_DIM = POOL_DIM // POOL_GROUPS
CONV_HEADS = 4
CONV_DIM = D_MODEL // 4
CONV_WIDTH = 3
D_MIX = A_DIM + POOL_DIM + CONV_DIM
IN_SIZES = (A_DIM, A_DIM, A_DIM, A_DIM, A_HEADS, A_HEADS, POOL_DIM, CONV_DIM, CONV_DIM, CONV_DIM)
D_IN = sum(IN_SIZES)
D_FF = -(-8 * D_MODEL // (3 * 256)) * 256


def rms_norm(x, g):
    xf = x.astype(jnp.float32)
    y = xf * lax.rsqrt(jnp.mean(xf * xf, axis=-1, keepdims=True) + EPS)
    return (y * g.astype(jnp.float32)).astype(x.dtype)

def causal_dwconv(x, w):
    K, C = w.shape
    return lax.conv_general_dilated(
        x, w[:, None, :].astype(x.dtype), window_strides=(1,), padding=[(K - 1, 0)],
        dimension_numbers=('NWC', 'WIO', 'NWC'), feature_group_count=C)

def l2norm(t):
    return t * lax.rsqrt(jnp.sum(t * t, axis=-1, keepdims=True) + EPS)

def chunk_gated_delta_rule(q, k, v, g, beta):
    Bn, S, H, DK = q.shape
    DV = v.shape[-1]
    N = S // CHUNK

    def to_chunks(t):
        t = t.reshape((Bn, N, CHUNK, H) + t.shape[3:])
        return jnp.moveaxis(t, 3, 1)

    q = to_chunks(q * (DK ** -0.5))
    k = to_chunks(k)
    v = to_chunks(v)
    g = to_chunks(g)
    beta = to_chunks(beta)
    gc = jnp.cumsum(g, axis=-1)
    kb = k * beta[..., None]
    vb = v * beta[..., None]
    causal_incl = jnp.tril(jnp.ones((CHUNK, CHUNK), dtype=bool))
    causal_strict = jnp.tril(jnp.ones((CHUNK, CHUNK), dtype=bool), -1)
    diff = gc[..., :, None] - gc[..., None, :]
    decay = jnp.exp(jnp.where(causal_incl, diff, -jnp.inf))
    lower = jnp.where(causal_strict, jnp.einsum('bhncd,bhnsd->bhncs', kb, k) * decay, 0.0)
    eye = jnp.eye(CHUNK, dtype=jnp.float32)
    tmat = lax.linalg.triangular_solve(eye + lower, jnp.broadcast_to(eye, lower.shape),
                                       left_side=True, lower=True, unit_diagonal=True)
    u = jnp.einsum('bhncs,bhnsv->bhncv', tmat, vb)
    w = jnp.einsum('bhncs,bhnsd->bhncd', tmat, kb * jnp.exp(gc)[..., None])
    attn = jnp.einsum('bhncd,bhnsd->bhncs', q, k) * decay

    def step(state, inp):
        q_i, k_i, u_i, w_i, gc_i, a_i = inp
        v_new = u_i - jnp.einsum('bhck,bhkv->bhcv', w_i, state)
        o_i = (jnp.einsum('bhck,bhkv->bhcv', q_i * jnp.exp(gc_i)[..., None], state)
               + jnp.einsum('bhcs,bhsv->bhcv', a_i, v_new))
        g_last = gc_i[..., -1]
        state = (state * jnp.exp(g_last)[..., None, None]
                 + jnp.einsum('bhck,bhcv->bhkv', k_i * jnp.exp(g_last[..., None] - gc_i)[..., None], v_new))
        return state, o_i

    xs = tuple(jnp.moveaxis(t, 2, 0) for t in (q, k, u, w, gc, attn))
    state0 = jnp.zeros((Bn, H, DK, DV), jnp.float32)
    _, o = lax.scan(step, state0, xs)
    return jnp.transpose(o, (1, 0, 3, 2, 4)).reshape(Bn, S, H, DV)

def gated_deltanet(q, k, v, z, a, b, conv_w, a_log, dt_bias, onorm_g):
    Bn, S, _ = q.shape
    qkv = jax.nn.silu(causal_dwconv(jnp.concatenate([q, k, v], axis=-1), conv_w))
    q, k, v = jnp.split(qkv.astype(jnp.float32), 3, axis=-1)
    hs = (Bn, S, A_HEADS, A_HEAD_DIM)
    q = l2norm(q.reshape(hs))
    k = l2norm(k.reshape(hs))
    v = v.reshape(hs)
    beta = jax.nn.sigmoid(b.astype(jnp.float32))
    g = -jnp.exp(a_log.astype(jnp.float32)) * jax.nn.softplus(a.astype(jnp.float32) + dt_bias.astype(jnp.float32))
    o = chunk_gated_delta_rule(q, k, v, g, beta)
    o = o * lax.rsqrt(jnp.mean(o * o, axis=-1, keepdims=True) + EPS) * onorm_g.astype(jnp.float32)
    o = o * jax.nn.silu(z.astype(jnp.float32).reshape(hs))
    return o.reshape(Bn, S, A_DIM).astype(z.dtype)

def multiscale_pool(h, pool_w, pool_scale):
    Bn, S, _ = h.shape
    hf = h.astype(jnp.float32)
    cs = jnp.cumsum(hf, axis=1)
    count = jnp.arange(1, S + 1, dtype=jnp.float32)[:, None]
    outs = []
    for gi, win in enumerate(POOL_WINDOWS):
        sl = slice(gi * POOL_GROUP_DIM, (gi + 1) * POOL_GROUP_DIM)
        csg = cs[..., sl]
        lag = jnp.pad(csg, ((0, 0), (win, 0), (0, 0)))[:, :S]
        mean = (csg - lag) / jnp.minimum(count, float(win))
        outs.append(mean - hf[..., sl])
    pooled = jnp.stack(outs, axis=2)
    y = jnp.einsum('bsgc,gcd->bsgd', pooled, pool_w.astype(jnp.float32)).reshape(Bn, S, POOL_DIM)
    return (y * pool_scale.astype(jnp.float32)).astype(h.dtype)

def short_gated_conv(gate_b, gate_c, hc, conv_w):
    return gate_b * causal_dwconv(gate_c * hc, conv_w)

def first_inputs(seed: int = 0) -> dict:
    key = jax.random.key(seed)
    ks = jax.random.split(key, 24)
    f32 = jnp.float32
    nrm = lambda k, shape, scale: jax.random.normal(k, shape, f32) * scale
    dt = jnp.exp(jax.random.uniform(ks[5], (DEPTH, A_HEADS), f32, np.log(1e-3), np.log(1e-1)))
    return {
        'x': nrm(ks[0], (BATCH, SEQ, D_MODEL), 1.0),
        'p': nrm(ks[1], (DEPTH, BATCH, SEQ, PLE_DIM), 1.0),
        'norm1_g': 1.0 + nrm(ks[2], (DEPTH, D_MODEL), 0.02),
        'w_in': nrm(ks[3], (DEPTH, D_MODEL, D_IN), D_MODEL ** -0.5),
        'conv_qkv': nrm(ks[4], (DEPTH, QKV_CONV_WIDTH, 3 * A_DIM), QKV_CONV_WIDTH ** -0.5),
        'a_log': jnp.log(jax.random.uniform(ks[6], (DEPTH, A_HEADS), f32, 1.0, 16.0)),
        'dt_bias': jnp.log(jnp.expm1(dt)),
        'onorm_g': 1.0 + nrm(ks[7], (DEPTH, A_HEAD_DIM), 0.02),
        'pool_w': nrm(ks[8], (DEPTH, POOL_GROUPS, POOL_GROUP_DIM, POOL_GROUP_DIM), POOL_GROUP_DIM ** -0.5),
        'pool_scale': 1.0 + nrm(ks[9], (DEPTH, POOL_DIM), 0.02),
        'sconv_w': nrm(ks[10], (DEPTH, CONV_WIDTH, CONV_DIM), CONV_WIDTH ** -0.5),
        'w_out': nrm(ks[11], (DEPTH, D_MIX, D_MODEL), D_MIX ** -0.5),
        'norm2_g': 1.0 + nrm(ks[12], (DEPTH, D_MODEL), 0.02),
        'w_gate': nrm(ks[13], (DEPTH, D_MODEL, D_FF), D_MODEL ** -0.5),
        'w_up': nrm(ks[14], (DEPTH, D_MODEL, D_FF), D_MODEL ** -0.5),
        'w_down': nrm(ks[15], (DEPTH, D_FF, D_MODEL), D_FF ** -0.5),
        'ple_proj': nrm(ks[16], (DEPTH, PLE_DIM, D_MODEL), PLE_DIM ** -0.5),
        'ple_gate': nrm(ks[17], (DEPTH, D_MODEL, D_MODEL), D_MODEL ** -0.5),
        'final_g': 1.0 + nrm(ks[18], (D_MODEL,), 0.02),
    }

def first_block(x, p, norm1_g, w_in, conv_qkv, a_log, dt_bias, onorm_g, pool_w, pool_scale,
              sconv_w, w_out, norm2_g, w_gate, w_up, w_down, ple_proj, ple_gate, final_g):
    offsets = [0]
    for s in IN_SIZES[:-1]:
        offsets.append(offsets[-1] + s)
    for i in range(DEPTH):
        h = rms_norm(x, norm1_g[i])
        proj = jnp.einsum('bsd,de->bse', h, w_in[i])
        q, k, v, z, a, b, hp, cb, cc, ch = jnp.split(proj, offsets[1:], axis=-1)
        o_a = gated_deltanet(q, k, v, z, a, b, conv_qkv[i], a_log[i], dt_bias[i], onorm_g[i])
        o_b = multiscale_pool(hp, pool_w[i], pool_scale[i])
        o_c = short_gated_conv(cb, cc, ch, sconv_w[i])
        mixed = jnp.concatenate([o_a, o_b, o_c], axis=-1)
        x = x + jnp.einsum('bse,ed->bsd', mixed, w_out[i])
        h = rms_norm(x, norm2_g[i])
        ff = jax.nn.silu(jnp.einsum('bsd,df->bsf', h, w_gate[i])) * jnp.einsum('bsd,df->bsf', h, w_up[i])
        x = x + jnp.einsum('bsf,fd->bsd', ff, w_down[i])
        gate = jax.nn.sigmoid(jnp.einsum('bsd,de->bse', x, ple_gate[i]).astype(jnp.float32)).astype(x.dtype)
        x = x + gate * jnp.einsum('bsq,qd->bsd', p[i], ple_proj[i])
    return rms_norm(x, final_g)


ML_HEADS = 4
ML_QK = 64
ML_V = 128
ML_CONV = 4
ML_CHUNK = 64
MLA_HEADS = 8
MLA_NOPE = 64
MLA_ROPE = 32
MLA_V = 64
MLA_Q_RANK = 256
MLA_KV_RANK = 128
ROPE_THETA = 10000.0
Q_BLOCK = 128
D_FF_2 = 4 * D_MODEL

ML_WIDTH = ML_HEADS * ML_V
MLA_WIDTH = MLA_HEADS * MLA_V
MIX_WIDTH = ML_WIDTH + MLA_WIDTH
QK_COLS = 2 * ML_HEADS * ML_QK
GATE_COLS = 2 * ML_HEADS
IN_WIDTH = QK_COLS + 2 * ML_WIDTH + GATE_COLS + MLA_Q_RANK + MLA_KV_RANK + MLA_ROPE


def rmsnorm(x, g):
    xf = x.astype(jnp.float32)
    y = xf * lax.rsqrt(jnp.mean(xf * xf, axis=-1, keepdims=True) + EPS)
    return (y * g.astype(jnp.float32)).astype(x.dtype)

def rope_tables(positions):
    inv = 1.0 / (ROPE_THETA ** (jnp.arange(0, MLA_ROPE, 2, dtype=jnp.float32) / MLA_ROPE))
    ang = positions.astype(jnp.float32)[..., None] * inv
    return jnp.cos(ang), jnp.sin(ang)

def apply_rope(x, cos, sin):
    xf = x.astype(jnp.float32)
    x1, x2 = jnp.split(xf, 2, axis=-1)
    return jnp.concatenate([x1 * cos - x2 * sin, x1 * sin + x2 * cos], axis=-1).astype(x.dtype)

def causal_conv(x, w, b):
    K = w.shape[0]
    S = x.shape[1]
    xp = jnp.pad(x, ((0, 0), (K - 1, 0), (0, 0)))
    return sum(xp[:, k:k + S] * w[k] for k in range(K)) + b

def mlstm_chunkwise(q, k, v, i_pre, f_pre):
    B, S, H, dk = q.shape
    dv = v.shape[-1]
    L = ML_CHUNK
    NC = S // L
    f32 = jnp.float32

    def chunk(t):
        t = t.reshape((B, NC, L, H) + t.shape[3:])
        return jnp.moveaxis(t, 3, 1)

    qc = chunk(q).astype(f32)
    kc = chunk(k).astype(f32) * (dk ** -0.5)
    vc = chunk(v).astype(f32)
    ig = chunk(i_pre).astype(f32)
    logf = jax.nn.log_sigmoid(chunk(f_pre).astype(f32))
    b = jnp.cumsum(logf, axis=-1)
    b_end = b[..., -1]

    a = b_end[..., None] - b + ig
    m_loc = jnp.max(a, axis=-1)
    w_loc = jnp.exp(a - m_loc[..., None])
    C_loc = jnp.einsum('bhcl,bhcld,bhcle->bhcde', w_loc, kc, vc)
    n_loc = jnp.einsum('bhcl,bhcld->bhcd', w_loc, kc)

    def step(carry, xs):
        C, n, m = carry
        Cl, nl, ml, bl = xs
        m_new = jnp.maximum(bl + m, ml)
        s_prev = jnp.exp(bl + m - m_new)
        s_loc = jnp.exp(ml - m_new)
        C_new = s_prev[..., None, None] * C + s_loc[..., None, None] * Cl
        n_new = s_prev[..., None] * n + s_loc[..., None] * nl
        return (C_new, n_new, m_new), (C, n, m)

    init = (jnp.zeros((B, H, dk, dv), f32), jnp.zeros((B, H, dk), f32), jnp.zeros((B, H), f32))
    xs = (jnp.moveaxis(C_loc, 2, 0), jnp.moveaxis(n_loc, 2, 0),
          jnp.moveaxis(m_loc, 2, 0), jnp.moveaxis(b_end, 2, 0))
    _, (C_prev, n_prev, m_prev) = lax.scan(step, init, xs)
    C_prev = jnp.moveaxis(C_prev, 0, 2)
    n_prev = jnp.moveaxis(n_prev, 0, 2)
    m_prev = jnp.moveaxis(m_prev, 0, 2)

    causal = jnp.tril(jnp.ones((L, L), dtype=bool))
    D = b[..., :, None] - b[..., None, :] + ig[..., None, :]
    D = jnp.where(causal, D, -jnp.inf)
    m_inter = b + m_prev[..., None]
    m_comb = jnp.maximum(jnp.max(D, axis=-1), m_inter)
    Dw = jnp.exp(D - m_comb[..., None])
    inter_w = jnp.exp(m_inter - m_comb)
    s = jnp.einsum('bhcid,bhcjd->bhcij', qc, kc) * Dw
    num = jnp.einsum('bhcij,bhcje->bhcie', s, vc) + inter_w[..., None] * jnp.einsum('bhcid,bhcde->bhcie', qc, C_prev)
    den = jnp.sum(s, axis=-1) + inter_w * jnp.einsum('bhcid,bhcd->bhci', qc, n_prev)
    h = num / jnp.maximum(jnp.abs(den), jnp.exp(-m_comb))[..., None]
    return jnp.moveaxis(h, 1, 3).reshape(B, S, H, dv)

def causal_block_attention(q, k, v):
    B, S, H, dq = q.shape
    dv = v.shape[-1]
    nb = S // Q_BLOCK
    scale = dq ** -0.5
    kf = k.astype(jnp.float32)
    vf = v.astype(jnp.float32)
    qb = jnp.transpose(q.reshape(B, nb, Q_BLOCK, H, dq), (1, 0, 3, 2, 4))
    kpos = jnp.arange(S)

    def one_block(args):
        qblk, bi = args
        sc = jnp.einsum('bhqd,bkhd->bhqk', qblk.astype(jnp.float32), kf) * scale
        qpos = bi * Q_BLOCK + jnp.arange(Q_BLOCK)
        sc = jnp.where(kpos[None, :] <= qpos[:, None], sc, -jnp.inf)
        p = jax.nn.softmax(sc, axis=-1)
        return jnp.einsum('bhqk,bkhd->bqhd', p, vf)

    out = lax.map(one_block, (qb, jnp.arange(nb)))
    return jnp.transpose(out, (1, 0, 2, 3, 4)).reshape(B, S, H * dv)

def token_mixer(a, cos, sin, w_in, b_gates, conv_w, conv_b, ml_head_norm,
                q_norm, w_uq, kv_norm, w_ukv, w_out):
    B, S, _ = a.shape
    proj = a @ w_in
    o0 = QK_COLS
    o1 = o0 + ML_WIDTH
    o2 = o1 + ML_WIDTH
    o3 = o2 + GATE_COLS
    o4 = o3 + MLA_Q_RANK
    o5 = o4 + MLA_KV_RANK
    qk_ml = proj[..., :o0]
    v_ml = proj[..., o0:o1]
    o_ml = proj[..., o1:o2]
    gates = proj[..., o2:o3] + b_gates
    c_q = proj[..., o3:o4]
    c_kv = proj[..., o4:o5]
    k_r = proj[..., o5:]

    qk_ml = jax.nn.silu(causal_conv(qk_ml, conv_w, conv_b))
    q_ml = qk_ml[..., :QK_COLS // 2].reshape(B, S, ML_HEADS, ML_QK)
    k_ml = qk_ml[..., QK_COLS // 2:].reshape(B, S, ML_HEADS, ML_QK)
    h_ml = mlstm_chunkwise(q_ml, k_ml, v_ml.reshape(B, S, ML_HEADS, ML_V),
                           gates[..., :ML_HEADS], gates[..., ML_HEADS:])
    h_ml = rmsnorm(h_ml, ml_head_norm.reshape(ML_HEADS, ML_V))
    h_ml = h_ml * jax.nn.sigmoid(o_ml.astype(jnp.float32)).reshape(B, S, ML_HEADS, ML_V)
    h_ml = h_ml.reshape(B, S, ML_WIDTH).astype(a.dtype)

    q = (rmsnorm(c_q, q_norm) @ w_uq).reshape(B, S, MLA_HEADS, MLA_NOPE + MLA_ROPE)
    q = jnp.concatenate([q[..., :MLA_NOPE],
                         apply_rope(q[..., MLA_NOPE:], cos[:, :, None, :], sin[:, :, None, :])], axis=-1)
    kv = (rmsnorm(c_kv, kv_norm) @ w_ukv).reshape(B, S, MLA_HEADS, MLA_NOPE + MLA_V)
    k_rope = apply_rope(k_r, cos, sin)[:, :, None, :]
    k = jnp.concatenate([kv[..., :MLA_NOPE],
                         jnp.broadcast_to(k_rope, (B, S, MLA_HEADS, MLA_ROPE))], axis=-1)
    h_mla = causal_block_attention(q, k, kv[..., MLA_NOPE:]).astype(a.dtype)

    return jnp.concatenate([h_ml, h_mla], axis=-1) @ w_out

def second_inputs(seed: int = 0) -> dict:
    key = jax.random.key(seed)
    ks = jax.random.split(key, 20)

    def nrm(k, shape, scale):
        return jax.random.normal(k, shape, jnp.float32) * scale

    def gain(k, shape):
        return 1.0 + 0.05 * jax.random.normal(k, shape, jnp.float32)

    x = nrm(ks[0], (BATCH, SEQ, D_MODEL), 1.0)
    positions = jnp.broadcast_to(jnp.arange(SEQ, dtype=jnp.int32), (BATCH, SEQ))
    b_gates = jnp.concatenate([nrm(ks[3], (DEPTH, ML_HEADS), 0.1),
                               3.0 + nrm(ks[4], (DEPTH, ML_HEADS), 0.1)], axis=-1)
    return {
        'x': x,
        'positions': positions,
        'norm_pre_mix': gain(ks[1], (DEPTH, D_MODEL)),
        'w_in': nrm(ks[2], (DEPTH, D_MODEL, IN_WIDTH), D_MODEL ** -0.5),
        'b_gates': b_gates,
        'conv_w': nrm(ks[5], (DEPTH, ML_CONV, QK_COLS), ML_CONV ** -0.5),
        'conv_b': nrm(ks[6], (DEPTH, QK_COLS), 0.02),
        'ml_head_norm': gain(ks[7], (DEPTH, ML_WIDTH)),
        'q_norm': gain(ks[8], (DEPTH, MLA_Q_RANK)),
        'w_uq': nrm(ks[9], (DEPTH, MLA_Q_RANK, MLA_HEADS * (MLA_NOPE + MLA_ROPE)), MLA_Q_RANK ** -0.5),
        'kv_norm': gain(ks[10], (DEPTH, MLA_KV_RANK)),
        'w_ukv': nrm(ks[11], (DEPTH, MLA_KV_RANK, MLA_HEADS * (MLA_NOPE + MLA_V)), MLA_KV_RANK ** -0.5),
        'w_out': nrm(ks[12], (DEPTH, MIX_WIDTH, D_MODEL), MIX_WIDTH ** -0.5),
        'norm_post_mix': gain(ks[13], (DEPTH, D_MODEL)),
        'norm_pre_mlp': gain(ks[14], (DEPTH, D_MODEL)),
        'w_up': nrm(ks[15], (DEPTH, D_MODEL, D_FF_2), D_MODEL ** -0.5),
        'w_down': nrm(ks[16], (DEPTH, D_FF_2, D_MODEL), D_FF_2 ** -0.5),
        'norm_post_mlp': gain(ks[17], (DEPTH, D_MODEL)),
    }

def second_block(x, positions, norm_pre_mix, w_in, b_gates, conv_w, conv_b, ml_head_norm,
              q_norm, w_uq, kv_norm, w_ukv, w_out, norm_post_mix, norm_pre_mlp,
              w_up, w_down, norm_post_mlp):
    cos, sin = rope_tables(positions)
    for l in range(DEPTH):
        a = rmsnorm(x, norm_pre_mix[l])
        mix = token_mixer(a, cos, sin, w_in[l], b_gates[l], conv_w[l], conv_b[l], ml_head_norm[l],
                          q_norm[l], w_uq[l], kv_norm[l], w_ukv[l], w_out[l])
        x = x + rmsnorm(mix, norm_post_mix[l])
        m = rmsnorm(x, norm_pre_mlp[l])
        y = jnp.square(jax.nn.relu(m @ w_up[l])) @ w_down[l]
        x = x + rmsnorm(y, norm_post_mlp[l])
    return x


def setup_inputs(seed=0):
    out = dict(first_inputs(seed))
    for name, value in second_inputs(seed + 1).items():
        if name != "x":
            out[name + "_2"] = value
    return out


def reference(
    x, p, norm1_g, w_in, conv_qkv, a_log, dt_bias, onorm_g, pool_w, pool_scale, sconv_w, w_out,
    norm2_g, w_gate, w_up, w_down, ple_proj, ple_gate, final_g, positions_2, norm_pre_mix_2,
    w_in_2, b_gates_2, conv_w_2, conv_b_2, ml_head_norm_2, q_norm_2, w_uq_2, kv_norm_2, w_ukv_2,
    w_out_2, norm_post_mix_2, norm_pre_mlp_2, w_up_2, w_down_2, norm_post_mlp_2,
):
    x = first_block(
        x, p, norm1_g, w_in, conv_qkv, a_log, dt_bias, onorm_g, pool_w, pool_scale, sconv_w,
        w_out, norm2_g, w_gate, w_up, w_down, ple_proj, ple_gate, final_g,
    )
    return second_block(
        x, positions_2, norm_pre_mix_2, w_in_2, b_gates_2, conv_w_2, conv_b_2, ml_head_norm_2,
        q_norm_2, w_uq_2, kv_norm_2, w_ukv_2, w_out_2, norm_post_mix_2, norm_pre_mlp_2, w_up_2,
        w_down_2, norm_post_mlp_2,
    )


_drawn_inputs = setup_inputs


def setup_inputs(seed=0):
    import zlib

    import numpy as np

    out = dict(_drawn_inputs(seed))
    spreads = {}
    factors = {'onorm_g': 5.177,
     'pool_scale': 4.973,
     'norm2_g': 3.13,
     'conv_b_2': 19.083,
     'q_norm_2': 6.027,
     'kv_norm_2': 3.731,
     'ml_head_norm_2': 8.0}
    for name, (base, spread) in spreads.items():
        noise = np.random.default_rng([zlib.crc32(name.encode()), seed]).standard_normal(out[name].shape)
        drawn = base * np.exp(spread * noise) if base else spread * noise
        out[name] = jnp.asarray(drawn.astype(out[name].dtype))
    for name, factor in factors.items():
        out[name] = (out[name] * factor).astype(out[name].dtype)
    return out
```

```python
from contextlib import ExitStack

import numpy as np

import concourse.bass as bass
from concourse import mybir

F32 = mybir.dt.float32
F32R = mybir.dt.float32r
I32 = mybir.dt.int32
ALU = mybir.AluOpType
ACT = mybir.ActivationFunctionType
AX_X = mybir.AxisListType.X

P = 128
T = 512
D = 1024
KD = D // P
NC = T // P
EPS = 1e-6
H = 4
FF1 = 2816
FF2 = 4096
W_IN1, W_IN2 = 3080, 1960
MLA_H, NOPE, ROPE, MLA_V = 8, 64, 32, 64
QR, KVR = 256, 128
LN_EXP_TABLES = 6
NBANK = 4
NAUX = 4
RAW, SPLIT = 3, 3
WB = 1024

PARAMS = [("norm1_g", 8), ("norm2_g", 8), ("final_g", 8), ("conv_qkv", 48), ("onorm_g", 1), ("pool_scale", 2),
          ("sconv_w", 6), ("norm_pre_mix_2", 8), ("norm_post_mix_2", 8), ("norm_pre_mlp_2", 8),
          ("norm_post_mlp_2", 8), ("conv_w_2", 16), ("conv_b_2", 4), ("ml_head_norm_2", 4), ("q_norm_2", 2),
          ("kv_norm_2", 1)]
PCOL = {}
for _name, _rows in PARAMS:
    PCOL[_name] = sum(r for n, r in PARAMS[:len(PCOL)])
NPARAM = sum(r for _, r in PARAMS)
PSPLIT = PCOL["norm_pre_mix_2"]

LEVELS = 7
C_ID = 0
C_UP = C_ID + P
C_LEV = C_UP + P
C_NEG = C_LEV + LEVELS * P
C_INV = C_NEG + P
C_SGN = C_INV + 1
C_CNT = C_SGN + 1
NCST = C_CNT + 32


def constant_table():
    c = np.zeros((P, NCST), np.float32)
    r, q = np.arange(P)[:, None], np.arange(P)[None, :]
    c[:, C_ID:C_ID + P] = r == q
    c[:, C_UP:C_UP + P] = q >= r
    for n in range(LEVELS):
        m = 1 << n
        c[:, C_LEV + n * P:C_LEV + (n + 1) * P] = (r // (2 * m) == q // (2 * m)) & (r // m % 2 == 0) & (q // m % 2 == 1)
    c[:, C_NEG:C_NEG + P] = np.where(q > r, -1e30, 0.0)
    half = ROPE // 2
    inv = 1.0 / (np.float32(10000.0) ** (np.arange(0, ROPE, 2, dtype=np.float32) / np.float32(ROPE)))
    c[:, C_INV] = inv.astype(np.float32)[np.arange(P) % half]
    c[:, C_SGN] = np.where(np.arange(P) % ROPE < half, -1.0, 1.0)
    for t in range(2):
        win = np.where(np.arange(P) < 64, (2, 8)[t], (4, 16)[t])[:, None]
        c[:, C_CNT + 16 * t:C_CNT + 16 * t + 16] = 1.0 / np.minimum(np.arange(1, 17)[None, :], win)
    return c


def plan():
    blocks, tiles = [], []

    def add(kind, idx, what, nk, cols):
        blocks.append(what)
        for j in range(cols // P):
            tiles.append((kind, idx + j, len(blocks) - 1, j * P, nk, cols))

    def wide(kind, weight, col, n, row=0, nk=KD):
        for j in range(n):
            add(kind, j, ("mat", weight, row, nk, col + j * P, P), nk, P)

    wide("ab", "w_in", 2048, 1)
    wide("k", "w_in", 512, 4)
    wide("q", "w_in", 0, 4)
    wide("v", "w_in", 1024, 4)
    wide("hp", "w_in", 2056, 2)
    wide("ch", "w_in", 2824, 2)
    wide("cc", "w_in", 2568, 2)
    wide("cb", "w_in", 2312, 2)
    wide("z", "w_in", 1536, 4)
    wide("wout", "w_out", 0, 8)

    def mlp(widths, up, down):
        rows = [0]
        for w in widths:
            rows.append(rows[-1] + w)
        n = len(widths)
        for c in range(n + 1):
            if c < n:
                for j in range(widths[c]):
                    up(c, rows[c], j)
            if c > 0:
                down(c - 1, rows[c - 1], widths[c - 1])

    def up1(c, row, j):
        blocks.append(("mat", "w_gate", 0, KD, (row + j) * P, P))
        tiles.append(("gate", (c, j), len(blocks) - 1, 0, KD, P))
        blocks.append(("mat", "w_up", 0, KD, (row + j) * P, P))
        tiles.append(("up", (c, j), len(blocks) - 1, 0, KD, P))

    def down1(c, row, w):
        for m in range(KD):
            blocks.append(("mat", "w_down", row * P, w, m * P, P))
            tiles.append(("down", (c, m), len(blocks) - 1, 0, w, P))

    mlp(MLP1, up1, down1)
    for j in range(2):
        add("proj", 4 * j, ("mat", "ple_proj", 0, 2, j * T, T), 2, T)
    wide("pgate", "ple_gate", 0, 8)

    wide("gates2", "w_in_2", 1536, 1)
    wide("qk2", "w_in_2", 0, 4)
    for pair in range(2):
        blocks.append(("mat", "w_in_2", 0, 4, 512 + pair * 256, 256))
        blocks.append(("mat", "w_in_2", 4 * P, 4, 512 + pair * 256, 256))
        for c in range(NC):
            tiles.append(("v2", (pair, c), len(blocks) - 1, 0, KD, 256))
    wide("cq2", "w_in_2", 1544, 2)
    wide("ckv2", "w_in_2", 1800, 1)
    add("kr2", 0, ("krope",), KD, P)
    wide("o2", "w_in_2", 1024, 4)
    for j in range(2):
        add("uq2", 4 * j, ("uq", j), 2, T)
    blocks.append(("ukv",))
    for j in range(4):
        tiles.append(("uk2", j, len(blocks) - 1, j * P, 1, T))
    for c in range(NC):
        tiles.append(("uv2", c, len(blocks) - 1, T, 1, T))
    wide("wout2", "w_out_2", 0, 8)

    def up2(c, row, j):
        blocks.append(("mat", "w_up_2", 0, KD, (row + j) * P, P))
        tiles.append(("up2", (c, j), len(blocks) - 1, 0, KD, P))

    def down2(c, row, w):
        for m in range(KD):
            blocks.append(("mat", "w_down_2", row * P, w, m * P, P))
            tiles.append(("down2", (c, m), len(blocks) - 1, 0, w, P))

    mlp(MLP2, up2, down2)
    return blocks, tiles


MLP1 = (8, 8, 6)
MLP2 = (8, 8, 8, 8)


class Plan:

    READER = dict(ab="dve", k="act", q="act", v="act", hp="act", ch="dve", cc="dve", cb="dve", z="act", wout="dve",
                  gate="act", up="dve", down="dve", proj="act", pgate="act", gates2="dve", qk2="act", v2="act",
                  cq2="act", ckv2="act", kr2="dve", o2="act", uq2="dve", uk2="act", uv2="act", wout2="dve",
                  up2="act", down2="dve")

    def __init__(self):
        self.blocks, self.tiles = plan()
        self.at = {(k, i): t for t, (k, i, *_) in enumerate(self.tiles)}
        self.last = [None] * len(self.blocks)
        for t, tile in enumerate(self.tiles):
            self.last[tile[2]] = t
        for b in range(len(self.blocks) - 2, -1, -1):
            if self.last[b] is None:
                self.last[b] = self.last[b + 1]
        self.read, n = [], {"act": 0, "dve": 0}
        for k, *_ in self.tiles:
            n[self.READER[k]] += 1
            self.read.append((self.READER[k], n[self.READER[k]]))

    def done(self, kind, idx):
        return self.at[kind, idx] + 1


def build(nc, ins, out):
    pl = Plan()
    with ExitStack() as ctx:
        def signal(name):
            return ctx.enter_context(nc.semaphore(name))

        base = (nc.sbuf_base + 31) // 32 * 32
        top = [base]

        def sb(name, shape, dt=F32, at=None):
            size = 4
            for n in shape[1:]:
                size *= n
            if at is None:
                at = top[0]
                top[0] += (size + 31) // 32 * 32
            assert at + size <= nc.sbuf_usable_end, (name, at + size - nc.sbuf_usable_end)
            h = nc.alloc_sbuf_tensor_at(name, shape, dt, offset=at)
            offs[name] = at
            return h

        offs = {}
        x = sb("x", [P, KD, T])
        ah = sb("ah", [P, KD, T], F32R)
        al = sb("al", [P, KD, T], F32R)
        raw = [sb(f"raw{i}", [P, WB]) for i in range(RAW)]
        wh = [sb(f"wh{i}", [P, WB], F32R) for i in range(SPLIT)]
        wl = [sb(f"wl{i}", [P, WB], F32R) for i in range(SPLIT)]
        cst = sb("cst", [P, NCST])
        ones = sb("ones", [P, P])
        par = sb("par", [P, NPARAM])
        sq = sb("sq", [P, 2, T])
        h32 = sb("h32", [P, 3, T])
        rstd = sb("rstd", [P, T])
        cols = sb("cols", [P, 8])
        eps = sb("eps", [P, 1])
        free = top[0]

        kT = sb("kT", [P, H, T])
        qT = sb("qT", [P, H, T])
        qg = sb("qg", [P, H, T])
        bv = sb("bv", [P, NC, H, P])
        kd = sb("kd", [P, NC, H, P])
        AT = sb("AT", [P, NC, H, P])
        U = sb("U", [P, NC, H, P])
        Y = sb("Y", [P, NC, H, P])
        GR = sb("GR", [P, H, T])
        BR = sb("BR", [P, H, T])
        X = sb("X", [P, 2, H, P])
        PS = sb("PS", [P, 2, H, P])
        UM = sb("UM", [P, 2, H, P])
        top[0] += 64
        pin = sb("pin", [P, 2, 16 + T])
        cin = sb("cin", [P, 2, 2 + T])
        gT = sb("gT", [P, NC, 16])
        eg = sb("eg", [P, 4, NC, H])
        xtok = sb("xtok", [P, NC, D], at=offs["U"])
        prow = sb("prow", [P, 2, P], at=offs["pin"])
        craw = [sb(f"craw{i}", [P, 3 + T], at=offs["X"] + i * 2080) for i in range(2)]
        cc = [sb(f"cc{i}", [P, T], at=offs["X"] + 2 * 2080 + i * 2048) for i in range(2)]
        vT = [sb(f"vT{i}", [P, T], at=offs["X"] + 2 * 2080 + 4096 + i * 2048) for i in range(2)]
        gab = sb("gab", [8, T], at=offs["AT"])
        gsp = sb("gsp", [8, T], at=offs["AT"] + 2048)
        gcs = sb("gcs", [8, T], at=offs["AT"] + 4096)
        gbt = sb("gbt", [8, T], at=offs["AT"] + 6144)
        oT = sb("oT", [P, H, T], at=offs["qT"])
        ptmp = sb("ptmp", [P, 2, 16 + T], at=offs["qT"])
        zs = sb("zs", [P, H, T], at=offs["GR"])
        pooled = sb("pooled", [P, 2, T], at=offs["BR"])
        convd = sb("convd", [P, 2, T], at=offs["BR"] + 4096)
        orn = [sb(f"orn{i}", [P, T], at=offs["PS"] + 2048 * i) for i in range(2)]
        S = sb("S", [P, H, P], at=offs["X"])
        vn = sb("vn", [P, H, P], at=offs["X"] + 2048)
        rr = sb("rr", [P, H, P], at=offs["PS"])
        t1 = sb("t1", [P, H, P], at=offs["PS"] + 2048)
        bw = sb("bw", [P, 2, P])

        top[0] = free
        yh = [sb(f"yh{i}", [P, KD, T], F32R) for i in range(2)]
        yl = [sb(f"yl{i}", [P, KD, T], F32R) for i in range(2)]
        sg = sb("sg", [P, 3, T])
        y32 = sb("y32", [P, 2, T])
        hid_top = top[0]
        ptok = sb("ptok", [P, NC, 2 * P])
        ph = sb("ph", [P, 2, T], F32R)
        plo = sb("plo", [P, 2, T], F32R)
        pp = sb("pp", [P, KD, T])

        acc = sb("acc", [P, KD, T], at=hid_top)
        rl = sb("rl", [P, T], at=offs["sg"])
        otok = sb("otok", [P, NC, D], at=free)

        top[0] = free
        q2 = sb("q2", [P, 2, T])
        k2 = sb("k2", [P, 2, T])
        v2 = sb("v2", [P, NC, T])
        og = sb("og", [P, H, T])
        mrow = sb("mrow", [P, T])
        erow = sb("erow", [P, T])
        wt = sb("wt", [P, 2, T])
        st = sb("st", [P, 2, T])
        hm = sb("hm", [P, T])
        dn = sb("dn", [P, T])
        m4 = sb("m4", [H, T])
        em4 = sb("em4", [H, T])
        cT = sb("cT", [P, NC, H])
        trig = sb("trig", [P, 2, T])
        krr = sb("krr", [P, T])
        rtmp = sb("rtmp", [P, T])
        cqh = sb("cqh", [P, 2, T], F32R)
        cql = sb("cql", [P, 2, T], F32R)
        ckh = sb("ckh", [P, 1, T], F32R)
        ckl = sb("ckl", [P, 1, T], F32R)
        am = sb("am", [P, 3, MLA_H * NC])
        qf = sb("qf", [P, MLA_H, T])
        kf = sb("kf", [P, MLA_H, T])
        vt2 = sb("vt2", [P, NC, T])
        craw2 = [sb(f"craw2{i}", [P, 3 + T], at=offs["qf"] + i * 2080) for i in range(2)]
        cc2 = [sb(f"cc2{i}", [P, T], at=offs["qf"] + 4160 + i * 2048) for i in range(2)]
        posi = sb("posi", [P, T], I32, at=offs["qf"] + 8256)
        ang = sb("ang", [P, T], at=offs["qf"] + 10304)
        turn = sb("turn", [P, T], at=offs["qf"] + 12352)
        g2 = sb("g2", [2 * H, T], at=offs["kf"])
        lf = sb("lf", [2 * H, T], at=offs["kf"] + 2048)
        bs = sb("bs", [2 * H, T], at=offs["kf"] + 4096)
        nbs = sb("nbs", [2 * H, T], at=offs["kf"] + 6144)
        c4 = sb("c4", [H, T], at=offs["kf"] + 8192)
        cq = sb("cq", [P, 3, T], at=offs["vt2"])
        pm = sb("pm", [P, 3, T], at=offs["mrow"])
        pT = sb("pT", [P, 2, NC, T], at=free)

        bank = [ctx.enter_context(nc.psum_tensor(f"bank{i}", [P, T], F32)) for i in range(NBANK)]
        aux = [ctx.enter_context(nc.psum_tensor(f"aux{i}", [P, T], F32)) for i in range(NAUX)]
        auxh = [a[:, :].rearrange("p (h n) -> p h n", h=4) for a in aux]

        ident = cst[:, C_ID:C_ID + P]

        def g_of(name, k):
            return par[:, PCOL[name] + k:PCOL[name] + k + 1]

        x_loaded = signal("x_loaded")
        consts_loaded = signal("consts_loaded")
        raw_loaded = [signal(f"raw_loaded{i}") for i in range(RAW)]
        out_stored = signal("out_stored")
        wh_ready = signal("wh_ready")
        wl_ready = signal("wl_ready")
        gemm_done = signal("gemm_done")
        bank_read = {"act": signal("bank_read_act"), "dve": signal("bank_read_dve")}
        ones_set = signal("ones_set")
        par_ps = signal("par_ps")
        par_ready = signal("par_ready")
        xt_ps = signal("xt_ps")
        xt_sq = signal("xt_sq")
        x_ready = signal("x_ready")
        sq_ready = signal("sq_ready")
        ssq_done = signal("ssq_done")
        rstd_ready = signal("rstd_ready")
        h32_ready = signal("h32_ready")
        ah_ready = signal("ah_ready")
        al_ready = signal("al_ready")
        act_step = signal("act_step")
        dve_step = signal("dve_step")
        pool_step = signal("pool_step")

        def landed(b):
            return 16 * sum(len(parts(n)) for n in range(b % RAW, b + 1, RAW))

        def parts(b):
            what, dst = pl.blocks[b], raw[b % RAW]
            if what[0] == "mat":
                _, name, row, nk, col, w = what
                src = ins[name][0, row:row + nk * P, col:col + w].rearrange("(k p) n -> p k n", p=P)
                return [(dst[:, 0:nk * w].rearrange("p (k n) -> p k n", n=w), src)]
            if what[0] == "krope":
                w = ins["w_in_2"][0].rearrange("(k p) n -> p k n", p=P)
                d = dst[:, 0:WB].rearrange("p (k n) -> p k n", n=P)
                end = W_IN2
                return [(d[:, :, 0:96], w[:, :, end - 96:end]), (d[:, :, 96:112], w[:, :, end - 16:end]),
                        (d[:, :, 112:128], w[:, :, end - 32:end - 16])]
            if what[0] == "uq":
                res = []
                for k in range(2):
                    w = ins["w_uq_2"][0, k * P:(k + 1) * P, what[1] * 384:(what[1] + 1) * 384].rearrange(
                        "p (h n) -> p h n", n=NOPE + ROPE)
                    d = dst[:, k * T:(k + 1) * T].rearrange("p (h n) -> p h n", n=P)
                    res += [(d[:, :, 0:96], w), (d[:, :, 96:112], w[:, :, 80:96]), (d[:, :, 112:128], w[:, :, 64:80])]
                return res
            w = ins["w_ukv_2"][0].rearrange("p (h n) -> p h n", n=NOPE + MLA_V)
            return [(dst[:, i * T:(i + 1) * T].rearrange("p (h n) -> p h n", n=64), w[:, :, 64 * i:64 * i + 64])
                    for i in range(2)]

        softplus_ready = signal("softplus_ready")
        decay_sums_ready = signal("decay_sums_ready")
        beta_ready = signal("beta_ready")
        rows_ps = signal("rows_ps")
        rows_ready = signal("rows_ready")
        gt_ps = signal("gt_ps")
        gt_ready = signal("gt_ready")
        eg_args = signal("eg_args")
        eg_exps = signal("eg_exps")
        conv_done = signal("conv_done")
        silu_ready = signal("silu_ready")
        head_sq = signal("head_sq")
        head_ss = signal("head_ss")
        head_rn = signal("head_rn")
        head_normed = signal("head_normed")
        kt_ps = signal("kt_ps")
        kd_ready = signal("kd_ready")
        vt_ps = signal("vt_ps")
        bv_ready = signal("bv_ready")
        gr_exp = signal("gr_exp")
        qg_ready = signal("qg_ready")
        dt_args = signal("dt_args")
        dt_exp = signal("dt_exp")
        gram_ps = signal("gram_ps")
        at_ready = signal("at_ready")
        um_ready = signal("um_ready")
        p_ps = signal("p_ps")
        p_ready = signal("p_ready")
        xy_ps = signal("xy_ps")
        xy_ready = signal("xy_ready")
        ks_ps = signal("ks_ps")
        rr_ready = signal("rr_ready")
        vn_ps = signal("vn_ps")
        vn_ready = signal("vn_ready")
        su_ps = signal("su_ps")
        s_ready = signal("s_ready")
        o_ps = signal("o_ps")
        o_ready = signal("o_ready")
        pooled_ready = signal("pooled_ready")
        pool_ps = signal("pool_ps")
        bw_zero = signal("bw_zero")
        bw_loaded = signal("bw_loaded")
        osq_ready = signal("osq_ready")
        oss_ps = signal("oss_ps")
        orn_ready = signal("orn_ready")
        cols_zero = signal("cols_zero")
        cols_loaded = signal("cols_loaded")
        eps_set = signal("eps_set")
        pads_zero = signal("pads_zero")
        alog_exp = signal("alog_exp")
        y_ready = [signal("y_ready_1"), signal("y_ready_2")]
        ph_ready = signal("ph_ready")
        x_gated = signal("x_gated")
        x_normed = signal("x_normed")
        x_mixed = signal("x_mixed")
        ptok_loaded = signal("ptok_loaded")
        pt_ps = signal("pt_ps")
        pt_ready = signal("pt_ready")

        pads2_zero = signal("pads2_zero")
        pos_loaded = signal("pos_loaded")
        rope_args = signal("rope_args")
        trig_ready = signal("trig_ready")
        logf_ready = signal("logf_ready")
        forget_sums_ready = signal("forget_sums_ready")
        cb_ps = signal("cb_ps")
        c4_ready = signal("c4_ready")
        ct_ps = signal("ct_ps")
        ct_ready = signal("ct_ready")
        em_args = signal("em_args")
        em_ready = signal("em_ready")
        conv2_done = signal("conv2_done")
        silu2_ready = signal("silu2_ready")
        lat_sq = signal("lat_sq")
        lat_ss = signal("lat_ss")
        lat_rn = signal("lat_rn")
        cq_ready = signal("cq_ready")
        kr_ready = signal("kr_ready")
        kf_ready = signal("kf_ready")
        mrow_ps = signal("mrow_ps")
        mrow_ready = signal("mrow_ready")
        wt_args = signal("wt_args")
        wt_ready = signal("wt_ready")
        ms_ps = signal("ms_ps")
        s_done = signal("s_done")
        nd_ps = signal("nd_ps")
        hm_ready = signal("hm_ready")
        ml_sq = signal("ml_sq")
        ml_ss = signal("ml_ss")
        ml_rn = signal("ml_rn")
        as_ps = signal("as_ps")
        max_ready = signal("max_ready")
        prob_ready = signal("prob_ready")
        prob_scaled = signal("prob_scaled")
        at_ps = signal("at_ps")
        pt_evac = signal("pt_evac")
        pv_ps = signal("pv_ps")
        relu_sq = signal("relu_sq")
        x_last = signal("x_last")
        ot_ps = signal("ot_ps")
        out_act = signal("out_act")
        out_dve = signal("out_dve")
        SPLIT_AT = [2 * NC * (t + 1) + 1 for t in range(3)]
        ATT_SCALE = float(NOPE + ROPE) ** -0.5
        TWO_PI = 6.283185307179586
        TURN_PARTS = (6.28125, 0.00193500518798828125, TWO_PI - 6.28125 - 0.00193500518798828125)
        PI_BELOW = 3.1415925
        ROUND = 12582912.0

        F_NORM1, F_MIX1, F_NORM2, F_PLE, F_NORM3, F_MIX2, F_NORM5 = range(7)
        H32_BASE = {F_NORM1: 0, F_MIX1: 8, F_NORM2: 14, F_NORM3: 22}
        H32_BASE[F_MIX2] = 30
        H32_BASE[F_NORM5] = 30 + 4
        LAST_USE = {F_NORM1: pl.done("z", 3), F_MIX1: pl.done("wout", 7), F_NORM2: pl.done("up", (2, 5)),
                    F_PLE: pl.done("pgate", 7), F_NORM3: pl.done("o2", 3), F_MIX2: pl.done("wout2", 7),
                    F_NORM5: pl.done("up2", (3, 7))}
        MIX1_ORDER = [4, 5, 6, 7, 0, 1, 2, 3]
        HEADS = [("k", h) for h in range(H)] + [("q", h) for h in range(H)] + [("v", h) for h in range(H)]
        INV_PAIR = 2 * LEVELS

        RSTD_FREE = {1: (h32_ready, 8), 2: (h32_ready, H32_BASE[F_NORM2] + KD), 3: (x_normed, KD),
                     4: (h32_ready, H32_BASE[F_MIX2] + H), 5: (x_mixed, KD),
                     6: (h32_ready, H32_BASE[F_NORM5] + KD)}

        def when_read(kind, idx):
            eng, n = pl.read[pl.at[kind, idx]]
            return bank_read[eng], n

        def evacuated(eng, kind, idx):
            eng.wait_ge(*when_read(kind, idx))

        def conv_tile(j):
            kind, h = HEADS[j]
            return {"q": 0, "k": 4, "v": 8}[kind] + h

        def block_cols(b):
            what = pl.blocks[b]
            return what[3] * what[5] if what[0] == "mat" else WB

        def multiscale(pool, link):
            for t in range(2):
                evacuated(pool, "hp", t)
                pool.wait_ge(qg_ready, H)
                a, b, n = pin[:, t, :], ptmp[:, 0, :], 16 + T
                c = ptmp[:, 1, :]
                link(nc.gpsimd.tensor_tensor(b[:, 1:n], a[:, 1:n], a[:, 0:n - 1], ALU.add))
                if t == 0:
                    link(nc.gpsimd.tensor_copy(c[0:64, 16:n], b[0:64, 16:n]))
                    link(nc.gpsimd.tensor_tensor(c[64:P, 3:n], b[64:P, 3:n], b[64:P, 1:n - 2], ALU.add))
                    s = c
                else:
                    link(nc.gpsimd.tensor_tensor(c[:, 3:n], b[:, 3:n], b[:, 1:n - 2], ALU.add))
                    link(nc.gpsimd.tensor_tensor(b[:, 7:n], c[:, 7:n], c[:, 3:n - 4], ALU.add))
                    link(nc.gpsimd.tensor_copy(c[0:64, 16:n], b[0:64, 16:n]))
                    link(nc.gpsimd.tensor_tensor(c[64:P, 16:n], b[64:P, 16:n], b[64:P, 8:n - 8], ALU.add))
                    s = c
                cnt = cst[:, C_CNT + 16 * t:C_CNT + 16 * t + 16]
                o = pooled[:, t, :]
                pool.wait_ge(at_ready, NC)
                link(nc.gpsimd.tensor_scalar(o[:, 16:T], s[:, 32:n], cnt[:, 15:16], None, ALU.mult))
                link(nc.gpsimd.tensor_tensor(o[:, 0:16], s[:, 16:32], cnt, ALU.mult))
                nc.gpsimd.tensor_tensor(o, o, a[:, 16:n], ALU.subtract).then_inc(pooled_ready, 1)

        def tensor_rest(pe, gemm, ssq, transpose4, state):
            def mlp(kinds, widths, fill, n):
                up, down = kinds
                for c in range(len(widths) + 1):
                    if c < len(widths):
                        for j in range(widths[c]):
                            for kind in up:
                                first = c == 0 and j == 0 and kind == up[0]
                                gemm(kind, (c, j), ready=(al_ready, KD * fill) if first else None)
                    if c > 0:
                        before = sum(widths[:c - 1])
                        for m in range(KD):
                            gemm(down, (c - 1, m), mov=(yh[(c - 1) % 2], yl[(c - 1) % 2]),
                                 ready=(y_ready[n], before) if m == 0 else None)
                            if c == len(widths) and m >= 2 and n:
                                ssq(6, m - 2)

            mlp((("gate", "up"), "down"), MLP1, F_NORM2, 0)
            pe.wait_ge(ptok_loaded, 16)
            for k in range(2):
                for c in range(NC):
                    last = nc.tensor.transpose(aux[k][:, c * P:(c + 1) * P], ptok[:, c, k * P:(k + 1) * P], ident)
                last.then_inc(pt_ps, 1)
            for j in range(KD):
                gemm("proj", j, mov=(ph, plo), ready=(pt_ready, 0) if j == 0 else None)
            for m in range(KD):
                gemm("pgate", m, ready=(al_ready, KD * F_PLE) if m == 0 else None)
                if m >= 2:
                    ssq(2, m - 2)
            ssq(2, KD - 2)
            ssq(2, KD - 1)
            for k in range(KD):
                ssq(3, k)
            tensor_second(pe, gemm, ssq, transpose4, mlp, state)

        def scalar_rest(act, link, tables, tile, square, norm, upper):
            def norm_upper(n, fill):
                norm(n)
                for k in range(KD):
                    upper(fill, k, k, h32[:, k % 3, :], (h32_ready, H32_BASE[fill] + k + 1))

            norm_upper(1, F_NORM2)
            act.dma_start(ptok[:, :, :], ins["p"][0, 0].rearrange("(c p) n -> p c n", p=P)).then_inc(ptok_loaded, 16)

            n = [0]

            def gate(c, j):
                slot = n[0] % 3
                if n[0] >= 3:
                    evacuated(act, *hidden[n[0] - 3])
                tile("gate", (c, j), lambda ps: nc.scalar.activation(sg[:, slot, :], ps, ACT.Silu))
                tile("up", (c, j))
                n[0] += 1

            hidden = [("up", (c, j)) for c in range(len(MLP1)) for j in range(MLP1[c])]
            for c in range(len(MLP1) + 1):
                if c < len(MLP1):
                    for j in range(MLP1[c]):
                        gate(c, j)
                if c > 0:
                    for m in range(KD):
                        tile("down", (c - 1, m))
                        if c == len(MLP1) and m > 0:
                            upper(F_PLE, m - 1, m - 1, x[:, m - 1, :], when_read("down", (c - 1, m - 1)))
            for k in range(2):
                act.wait_ge(pt_ps, k + 1)
                nc.scalar.copy(ph[:, k, :], aux[k][:, :]).then_inc(ph_ready, 1)
            upper(F_PLE, KD - 1, KD - 1, x[:, KD - 1, :], when_read("down", (len(MLP1) - 1, KD - 1)))
            for j in range(KD):
                tile("proj", j, lambda ps: nc.scalar.copy(pp[:, j, :], ps))
            for m in range(KD):
                if m >= 3:
                    act.wait_ge(x_gated, m - 2)
                tile("pgate", m, lambda ps: nc.scalar.activation(sg[:, m % 3, :], ps, ACT.Sigmoid))
                if m > 0:
                    act.wait_ge(x_gated, m)
                    square(2, m - 1, x[:, m - 1, :])
            act.wait_ge(x_gated, KD)
            square(2, KD - 1, x[:, KD - 1, :])
            norm(2)
            for k in range(KD):
                act.wait_ge(x_normed, k + 1)
                square(3, k, x[:, k, :])
            act.wait_ge(x_gated, KD)
            act.dma_start(posi[:, :], ins["positions_2"][0:1, :].partition_broadcast(P)).then_inc(pos_loaded, 16)
            norm_upper(3, F_NORM3)
            scalar_second(act, link, tables, tile, square, norm, upper, norm_upper)

        def vector_rest(dve, link, tile, freed, lower, norm_fill):
            norm_fill(1, F_NORM2, "norm2_g", 0)
            hidden = [(c, j) for c in range(len(MLP1)) for j in range(MLP1[c])]

            def product(c, j):
                i = hidden.index((c, j))
                ps = tile("up", (c, j))
                if c >= 2 and j == 0:
                    dve.wait_ge(gemm_done, pl.done("down", (c - 2, KD - 1)))
                if i >= 2:
                    dve.wait_ge(y_ready[0], i - 1)
                evacuated(dve, "gate", (c, j))
                y = y32[:, i % 2, :]
                freed(nc.vector.tensor_tensor(y, ps, sg[:, i % 3, :], ALU.mult))
                evacuated(dve, "up", (c, j))
                link(nc.vector.tensor_copy(yh[c % 2][:, j, :], y))
                nc.vector.tensor_tensor(yl[c % 2][:, j, :], y, yh[c % 2][:, j, :].bitcast(F32),
                                        ALU.subtract).then_inc(y_ready[0], 1)

            for c in range(len(MLP1) + 1):
                if c < len(MLP1):
                    for j in range(MLP1[c]):
                        product(c, j)
                if c > 0:
                    for m in range(KD):
                        ps = tile("down", (c - 1, m))
                        if c > 1:
                            evacuated(dve, "down", (c - 2, m))
                        freed(nc.vector.tensor_tensor(x[:, m, :], ps, x[:, m, :], ALU.add))
                        if c == len(MLP1) and m > 1:
                            lower(F_PLE, m - 2, m - 2, x[:, m - 2, :])
            for k in range(2):
                dve.wait_ge(ph_ready, k + 1)
                nc.vector.tensor_tensor(plo[:, k, :], aux[k][:, :], ph[:, k, :].bitcast(F32), ALU.subtract).then_inc(
                    pt_ready, 1)
            lower(F_PLE, KD - 2, KD - 2, x[:, KD - 2, :])
            lower(F_PLE, KD - 1, KD - 1, x[:, KD - 1, :])
            for m in range(KD):
                evacuated(dve, "pgate", m)
                g = sg[:, m % 3, :]
                link(nc.vector.tensor_tensor(g, g, pp[:, m, :], ALU.mult))
                dve.wait_ge(al_ready, KD * F_PLE + KD)
                nc.vector.tensor_tensor(x[:, m, :], x[:, m, :], g, ALU.add).then_inc(x_gated, 1)
            dve.wait_ge(rstd_ready, 3)
            dve.wait_ge(x_gated, KD)
            for k in range(KD):
                nc.vector.scalar_tensor_tensor(x[:, k, :], x[:, k, :], g_of("final_g", k), rstd[:, :], ALU.mult,
                                               ALU.mult).then_inc(x_normed, 1)
            dve.wait_ge(x_normed, KD)
            norm_fill(3, F_NORM3, "norm_pre_mix_2", 0)
            vector_second(dve, link, tile, freed, lower, norm_fill)

        def tensor_second(pe, gemm, ssq, transpose4, mlp, state):
            gemm("gates2", 0, ready=(al_ready, KD * F_NORM3))
            gemm("qk2", 0)
            pe.wait_ge(forget_sums_ready, 1)
            pe.wait_ge(rstd_ready, 4)
            nc.tensor.matmul(aux[0][0:H, :], ident[0:8, 0:H], g2[:, :], start=True, stop=False)
            nc.tensor.matmul(aux[0][0:H, :], ident[0:8, H:2 * H], nbs[:, :], start=False, stop=True)
            nc.tensor.matmul(aux[1][0:H, :], ident[0:8, H:2 * H], bs[:, :], start=True, stop=True).then_inc(cb_ps, 1)
            gemm("qk2", 1)
            gemm("qk2", 2)
            pe.wait_ge(c4_ready, 1)
            for c in range(NC):
                last = nc.tensor.transpose(aux[2][:, H * c:H * c + H], c4[:, c * P:(c + 1) * P], ident[0:H, 0:H])
            last.then_inc(ct_ps, 1)
            gemm("qk2", 3)

            def by_token(kinds, idx, mh, ml, blocks, nk, at, width):
                for c in range(NC):
                    t = pe_tile(pe, kinds, idx(c))
                    ps = bank[t % NBANK][:, 0:width]
                    s = slice(c * P, (c + 1) * P)
                    for k in range(nk):
                        b = blocks[k * len(blocks) // nk]
                        o = at + k % (nk // len(blocks)) * width
                        h, l = wh[b % SPLIT][:, o:o + width], wl[b % SPLIT][:, o:o + width]
                        nc.tensor.matmul(ps, mh[:, k, s], h, start=(k == 0), stop=False)
                        nc.tensor.matmul(ps, mh[:, k, s], l, start=False, stop=False)
                        last = nc.tensor.matmul(ps, ml[:, k, s], h, start=False, stop=(k == nk - 1))
                    last.then_inc(gemm_done, 1)

            def pe_tile(pe, kind, idx):
                t = state["t"]
                assert pl.tiles[t][:2] == (kind, idx)
                state["t"] += 1
                pe.wait_ge(wl_ready, pl.tiles[t][2] + 1)
                eng, n = pl.read[t - NBANK]
                pe.wait_ge(bank_read[eng], n)
                return t

            for pair in range(2):
                b = pl.tiles[pl.at["v2", (pair, 0)]][2]
                by_token("v2", lambda c: (pair, c), ah, al, [b - 1, b], KD, 0, 256)
            gemm("cq2", 0)
            gemm("cq2", 1)
            gemm("ckv2", 0)
            gemm("kr2", 0)
            for j in range(3):
                pe.wait_ge(lat_sq, j + 1)
                if j == 0:
                    pe.wait_ge(ct_ready, 1)
                nc.tensor.matmul(aux[2 + j // 2][:, :], ones[:, :], sq[:, j % 2, :], start=(j != 1),
                                 stop=(j != 0)).then_inc(lat_ss, 1)
            for h in range(H):
                gemm("o2", h)

            def latents(j):
                if j < 4:
                    for h in (2 * j, 2 * j + 1):
                        gemm("uq2", h, mov=(cqh, cql), ready=(cq_ready, 0) if h == 0 else None)
                elif j == 4:
                    pe.wait_ge(cq_ready, 3)
                    for i in range(4):
                        gemm("uk2", i, mov=(ckh, ckl))
                elif j == 5:
                    b = pl.tiles[pl.at["uv2", 0]][2]
                    by_token("uv2", lambda c: c, ckh, ckl, [b], 1, T, T)

            pe.wait_ge(lat_rn, 2)
            for h in range(H):
                r, t = 64 * (h % 2), h // 2
                pe.wait_ge(em_ready, 1)
                if h > 0:
                    pe.wait_ge(ml_rn, h)
                row = ident[0:H, h:h + 1].to_broadcast([H, P])
                nc.tensor.matmul(aux[0][:, :], row, m4[:, :], start=True, stop=True).then_inc(mrow_ps, 1)
                if h > 0:
                    pe.wait_ge(s_done, 4 * h)
                nc.tensor.matmul(aux[1][:, :], row, em4[:, :], start=True, stop=True).then_inc(mrow_ps, 1)

                def scores(j):
                    if j < 2:
                        pe.wait_ge(mrow_ready, 2 * h + j + 1)
                    else:
                        pe.wait_ge(s_done, 4 * h + j - 1)
                    if h == 0 and j == 0:
                        pe.wait_ge(silu2_ready, 4)
                    nc.tensor.matmul(aux[j % 2][:, 0:T - j * P], k2[r:r + 64, t, j * P:(j + 1) * P],
                                     q2[r:r + 64, t, j * P:T], start=True, stop=True).then_inc(ms_ps, 1)

                scores(0)
                scores(1)
                for j in range(NC):
                    if j == 0 or j == 2:
                        latents(2 * h + j // 2)
                    pe.wait_ge(s_done, 4 * h + j + 1)
                    if j == 0 and h == 0:
                        evacuated(pe, "v2", (1, NC - 1))
                    if j == 0 and h > 0:
                        pe.wait_ge(hm_ready, h)
                    n = T - j * P
                    nc.tensor.matmul(aux[2][:, j * P:T], v2[:, j, h * P:(h + 1) * P], st[:, j % 2, 0:n],
                                     start=(j == 0), stop=(j == NC - 1), skip_group_check=True)
                    nc.tensor.matmul(aux[3][:, j * P:T], ones[:, :], st[:, j % 2, 0:n], start=(j == 0),
                                     stop=(j == NC - 1), skip_group_check=True).then_inc(nd_ps, 1)
                    if j < 2:
                        scores(j + 2)
                pe.wait_ge(ml_sq, h + 1)
                pe.wait_ge(s_done, 4 * h + 3)
                nc.tensor.matmul(aux[0][:, :], ones[:, :], sq[:, h % 2, :], start=True, stop=True).then_inc(ml_ss, 1)

            NI = MLA_H * NC
            tb = [bank[0], bank[1]]
            pv = [bank[2], aux[3]]

            def att_scores(i):
                h, ib = i // NC, i % NC
                if i == 0:
                    evacuated(pe, "uq2", MLA_H - 1)
                    evacuated(pe, "uk2", 3)
                    pe.wait_ge(kf_ready, 1)
                    evacuated(pe, "uv2", NC - 1)
                    pe.wait_ge(ml_rn, H)
                    pe.wait_ge(s_done, 4 * H)
                    pe.wait_ge(hm_ready, H)
                if i >= 2:
                    pe.wait_ge(prob_ready, i - 1)
                n = (ib + 1) * P
                ps = aux[i % 2]
                nc.tensor.matmul(ps[:, 0:n], qf[0:96, h, ib * P:n], kf[0:96, h, 0:n], start=True, stop=False,
                                 skip_group_check=True)
                nc.tensor.matmul(ps[:, ib * P:n], ident, cst[:, C_NEG:C_NEG + P], start=False, stop=True,
                                 skip_group_check=True).then_inc(as_ps, 1)

            def att_values(h):
                pe.wait_ge(pt_evac, NC * (h + 1))
                if h >= 4 and h % 2 == 0:
                    pe.wait_ge(al_ready, KD * F_MIX2 + 4 + h // 2 - 1)
                r = 64 * (h % 2)
                for j in range(NC):
                    last = nc.tensor.matmul(pv[h // 2 % 2][r:r + 64, j * P:T], vt2[:, j, h * 64:(h + 1) * 64],
                                            pT[:, h % 2, j, j * P:T], start=(j == 0), stop=(j == NC - 1),
                                            skip_group_check=True)
                last.then_inc(pv_ps, 1)

            att_scores(0)
            att_scores(1)
            for i in range(NI):
                h, ib = i // NC, i % NC
                pe.wait_ge(prob_scaled, i + 1)
                if i >= 2:
                    pe.wait_ge(pt_evac, i - 1)
                for j in range(ib + 1):
                    last = nc.tensor.transpose(tb[i % 2][:, j * P:(j + 1) * P], pm[:, i % 3, j * P:(j + 1) * P], ident)
                last.then_inc(at_ps, 1)
                if i + 2 < NI:
                    att_scores(i + 2)
                if ib == 0 and h > 0:
                    att_values(h - 1)
            att_values(MLA_H - 1)
            pe.wait_ge(pt_evac, NI)
            pe.wait_ge(al_ready, KD * F_MIX2 + 7)
            for m in range(KD):
                gemm("wout2", m, ready=(al_ready, KD * F_MIX2) if m == 0 else None)
                if m == 2:
                    pe.wait_ge(al_ready, KD * F_MIX2 + 8)
                if m >= 2:
                    ssq(4, m - 2)
            ssq(4, KD - 2)
            ssq(4, KD - 1)
            for k in range(KD):
                ssq(5, k)
            mlp((("up2",), "down2"), MLP2, F_NORM5, 1)
            ssq(6, KD - 2)
            ssq(6, KD - 1)
            for k in range(KD):
                pe.wait_ge(x_last, k + 1)
                if k >= 3:
                    pe.wait_ge(*out_evac(k - 3))
                transpose4(aux[k % 3], x[:, k, :]).then_inc(ot_ps, 1)

        def scalar_second(act, link, tables, tile, square, norm, upper, norm_upper):
            tile("gates2", 0)
            evacuated(act, "gates2", 0)
            link(nc.scalar.activation(lf[:, :], g2[:, :], ACT.Abs))
            link(nc.scalar.activation(lf[:, :], lf[:, :], ACT.Exp, scale=-1.0))
            nc.scalar.activation(lf[:, :], lf[:, :], ACT.Ln, bias=1.0).then_inc(logf_ready, 1)

            def conv_evac(j):
                if j >= 2:
                    act.wait_ge(conv2_done, j - 1)
                    act.wait_ge(silu2_ready, j - 1)
                act.wait_ge(gemm_done, pl.done("qk2", j))
                act.wait_ge(pads2_zero, 1)
                t = pl.at["qk2", j]
                nc.scalar.copy(craw2[j % 2][:, 3:3 + T], bank[t % NBANK][:, :])
                tile("qk2", j, lambda ps: nc.scalar.activation(cc2[j % 2][:, :], ps, ACT.Copy,
                                                               scale=g_of("conv_w_2", 12 + j)))

            def conv_silu(j):
                act.wait_ge(conv2_done, j + 1)
                dst = (q2 if j < 2 else k2)[:, j % 2, :]
                nc.scalar.activation(dst, cc2[j % 2][:, :], ACT.Silu, bias=g_of("conv_b_2", j)).then_inc(silu2_ready, 1)

            conv_evac(0)
            conv_evac(1)
            conv_silu(0)
            conv_evac(2)
            conv_silu(1)
            conv_evac(3)
            conv_silu(2)
            conv_silu(3)
            act.wait_ge(em_args, 1)
            tables(LN_EXP_TABLES)
            nc.scalar.activation(em4[:, :], em4[:, :], ACT.Exp, scale=-1.0).then_inc(em_ready, 1)
            for i in range(2):
                act.wait_ge(rope_args, i + 1)
                nc.scalar.activation(trig[:, i, :], trig[:, i, :], ACT.Sin).then_inc(trig_ready, 1)
            for pair in range(2):
                for c in range(NC):
                    tile("v2", (pair, c), lambda ps: nc.scalar.copy(v2[:, c, pair * 256:(pair + 1) * 256],
                                                                    ps[:, 0:256]))
            for j in range(2):
                tile("cq2", j, lambda ps: nc.scalar.copy(cq[:, j, :], ps))
            tile("ckv2", 0, lambda ps: nc.scalar.copy(cq[:, 2, :], ps))
            for j in range(3):
                evacuated(act, "ckv2", 0)
                if j == 2:
                    act.wait_ge(lat_ss, 1)
                nc.scalar.activation(sq[:, j % 2, :], cq[:, j, :], ACT.Square).then_inc(lat_sq, 1)
            tile("kr2", 0)
            tables(LN_EXP_TABLES)
            for j in range(2):
                act.wait_ge(lat_ss, 2 + j)
                link(nc.scalar.activation(wt[:, j, :], aux[2 + j][:, :], ACT.Ln, bias=eps[:, 0:1],
                                          scale=(1.0 / QR, 1.0 / KVR)[j]))
                nc.scalar.activation(wt[:, j, :], wt[:, j, :], ACT.Exp, scale=-0.5).then_inc(lat_rn, 1)
            act.wait_ge(kr_ready, 1)
            nc.scalar.copy(kf[64:96, :, :], krr[64:96, :].unsqueeze(1).to_broadcast([32, MLA_H, T])).then_inc(kf_ready, 1)
            for h in range(H):
                tile("o2", h, lambda ps: nc.scalar.activation(og[:, h, :], ps, ACT.Sigmoid))
            tables(LN_EXP_TABLES)

            def keys(j):
                def read(ps):
                    nc.scalar.copy(kf[0:64, 2 * j, :], ps[0:64, :])
                    return nc.scalar.copy(kf[0:64, 2 * j + 1, :], ps[64:P, :])
                tile("uk2", j, read)

            def latents(j):
                if j < 4:
                    tile("uq2", 2 * j)
                    tile("uq2", 2 * j + 1)
                elif j == 4:
                    for i in range(4):
                        keys(i)
                elif j == 5:
                    for c in range(NC):
                        tile("uv2", c, lambda ps: nc.scalar.copy(vt2[:, c, :], ps))

            for h in range(H):
                if h > 0:
                    act.wait_ge(hm_ready, h)
                act.wait_ge(mrow_ps, 2 * h + 1)
                nc.scalar.copy(mrow[:, :], aux[0][:, :]).then_inc(mrow_ready, 1)
                act.wait_ge(mrow_ps, 2 * h + 2)
                nc.scalar.copy(erow[:, :], aux[1][:, :]).then_inc(mrow_ready, 1)
                for j in range(NC):
                    act.wait_ge(wt_args, 4 * h + j + 1)
                    n = T - j * P
                    nc.scalar.activation(wt[:, j % 2, 0:n], wt[:, j % 2, 0:n], ACT.Exp, scale=-1.0).then_inc(wt_ready, 1)
                    if j == 1 or j == 3:
                        latents(2 * h + j // 2)
                act.wait_ge(hm_ready, h + 1)
                if h >= 2:
                    act.wait_ge(ml_ss, h - 1)
                else:
                    act.wait_ge(lat_ss, 3)
                nc.scalar.activation(sq[:, h % 2, :], hm[:, :], ACT.Square).then_inc(ml_sq, 1)
                act.wait_ge(ml_ss, h + 1)
                if h > 0:
                    act.wait_ge(h32_ready, H32_BASE[F_MIX2] + h)
                link(nc.scalar.activation(rstd[:, :], aux[0][:, :], ACT.Ln, bias=eps[:, 0:1], scale=1.0 / P))
                nc.scalar.activation(rstd[:, :], rstd[:, :], ACT.Exp, scale=-0.5).then_inc(ml_rn, 1)
                upper(F_MIX2, h, h, h32[:, h % 3, :], (h32_ready, H32_BASE[F_MIX2] + h + 1))

            NI = MLA_H * NC
            tb = [bank[0], bank[1]]
            pv = [bank[2], aux[3]]

            def turned(i):
                h, ib = i // NC, i % NC
                act.wait_ge(at_ps, i + 1)
                if i >= 2 * NC:
                    act.wait_ge(pv_ps, h - 1)
                nc.scalar.copy(pT[:, h % 2, 0:ib + 1, ib * P:(ib + 1) * P],
                               tb[i % 2][:, 0:(ib + 1) * P].rearrange("p (j n) -> p j n", n=P)).then_inc(pt_evac, 1)

            def exps(i):
                n = (i % NC + 1) * P
                act.wait_ge(max_ready, i + 1)
                if i >= 3:
                    act.wait_ge(at_ps, i - 2)
                nc.scalar.activation(pm[:, i % 3, 0:n], aux[i % 2][:, 0:n], ACT.Exp, bias=am[:, 0, i:i + 1],
                                     accum_out=am[:, 1, i:i + 1]).then_inc(prob_ready, 1)

            exps(0)
            exps(1)
            for i in range(NI):
                turned(i)
                if i + 2 < NI:
                    exps(i + 2)
                if i in SPLIT_AT:
                    t = SPLIT_AT.index(i)
                    upper(F_MIX2, 4 + t, 4 + t, pv[t % 2][:, :], (pv_ps, 2 * t + 2))
            upper(F_MIX2, 7, 7, pv[1][:, :], (pv_ps, MLA_H))
            for m in range(KD):
                tile("wout2", m)
                if m > 0:
                    evacuated(act, "wout2", m - 1)
                    square(4, m - 1, acc[:, m - 1, :])
            evacuated(act, "wout2", KD - 1)
            square(4, KD - 1, acc[:, KD - 1, :])
            norm(4)
            for k in range(KD):
                act.wait_ge(x_mixed, k + 1)
                square(5, k, x[:, k, :])
            norm_upper(5, F_NORM5)
            n = [0]
            for c in range(len(MLP2) + 1):
                if c < len(MLP2):
                    for j in range(MLP2[c]):
                        i = n[0]
                        n[0] += 1
                        if i >= 1:
                            act.wait_ge(relu_sq, i)
                        tile("up2", (c, j), lambda ps: nc.scalar.activation(rl[:, :], ps, ACT.Relu))
                        evacuated(act, "up2", (c, j))
                        if i >= 2:
                            act.wait_ge(y_ready[1], i - 1)
                        nc.scalar.activation(y32[:, i % 2, :], rl[:, :], ACT.Square).then_inc(relu_sq, 1)
                if c > 0:
                    for m in range(KD):
                        tile("down2", (c - 1, m))
                        if c == len(MLP2) and m > 0:
                            evacuated(act, "down2", (c - 1, m - 1))
                            square(6, m - 1, acc[:, m - 1, :])
            evacuated(act, "down2", (len(MLP2) - 1, KD - 1))
            square(6, KD - 1, acc[:, KD - 1, :])
            norm(6)
            for k in range(0, KD, 2):
                act.wait_ge(ot_ps, k + 1)
                nc.scalar.copy(otok[:, :, k * P:(k + 1) * P], auxh[k % 3][:, :, :]).then_inc(out_act, 1)

        def vector_second(dve, link, tile, freed, lower, norm_fill):
            for i in range(2):
                nc.vector.memset(craw2[i][:, 0:3], 0.0)
            nc.vector.memset(rtmp[:, :], 0.0).then_inc(pads2_zero, 1)
            dve.wait_ge(pos_loaded, 16)
            link(nc.vector.tensor_copy(ang[:, :], posi[:, :]))
            link(nc.vector.tensor_scalar(ang[:, :], ang[:, :], cst[:, C_INV:C_INV + 1], None, ALU.mult))
            for i, turns in enumerate((0.0, 0.25)):
                r = trig[:, i, :]
                link(nc.vector.tensor_scalar(turn[:, :], ang[:, :], 1.0 / TWO_PI, turns, ALU.mult, ALU.add))
                link(nc.vector.tensor_scalar(turn[:, :], turn[:, :], ROUND, None, ALU.add))
                link(nc.vector.tensor_scalar(turn[:, :], turn[:, :], -ROUND, None, ALU.add))
                link(nc.vector.scalar_tensor_tensor(r, turn[:, :], -TURN_PARTS[0], ang[:, :], ALU.mult, ALU.add))
                link(nc.vector.scalar_tensor_tensor(r, turn[:, :], -TURN_PARTS[1], r, ALU.mult, ALU.add))
                link(nc.vector.scalar_tensor_tensor(r, turn[:, :], -TURN_PARTS[2], r, ALU.mult, ALU.add))
                link(nc.vector.tensor_scalar(r, r, turns * TWO_PI, None, ALU.add))
                nc.vector.tensor_scalar(r, r, PI_BELOW, -PI_BELOW, ALU.min, ALU.max).then_inc(rope_args, 1)
            ps = tile("gates2", 0)
            freed(nc.vector.tensor_scalar(g2[:, :], ps[0:8, :], cols[0:8, 3:4], None, ALU.add))
            evacuated(dve, "gates2", 0)
            dve.wait_ge(logf_ready, 1)
            link(nc.vector.scalar_tensor_tensor(lf[:, :], g2[:, :], 0.0, lf[:, :], ALU.min, ALU.subtract))
            for c in range(NC):
                s = slice(c * P, (c + 1) * P)
                link(nc.vector.tensor_tensor_scan(bs[:, s], ones[0:8, :], lf[:, s],
                                                  bs[:, c * P - 1:c * P] if c else 0.0, ALU.mult, ALU.add))
            nc.vector.tensor_scalar(nbs[:, :], bs[:, :], -1.0, None, ALU.mult).then_inc(forget_sums_ready, 1)

            def conv(j):
                r, c = craw2[j % 2], cc2[j % 2]
                evacuated(dve, "qk2", j)
                for tap in (2, 1, 0):
                    i = nc.vector.scalar_tensor_tensor(c[:, :], r[:, tap:tap + T], g_of("conv_w_2", 4 * tap + j),
                                                       c[:, :], ALU.mult, ALU.add)
                    if tap:
                        link(i)
                i.then_inc(conv2_done, 1)

            conv(0)
            dve.wait_ge(cb_ps, 1)
            nc.vector.tensor_copy(c4[:, :], aux[0][0:H, :]).then_inc(c4_ready, 1)
            dve.wait_ge(c4_ready, 1)
            link(nc.vector.tensor_tensor_scan(m4[:, :], c4[:, :], c4[:, :], 0.0, ALU.max, ALU.max))
            nc.vector.tensor_tensor(em4[:, :], aux[1][0:H, :], m4[:, :], ALU.add).then_inc(em_args, 1)
            conv(1)
            conv(2)
            dve.wait_ge(ct_ps, 1)
            nc.vector.tensor_copy(cT[:, :, :], aux[2][:, 0:NC * H].rearrange("p (c h) -> p c h", h=H)).then_inc(
                ct_ready, 1)
            conv(3)
            dve.wait_ge(trig_ready, 2)
            link(nc.vector.tensor_scalar(trig[:, 0, :], trig[:, 0, :], cst[:, C_SGN:C_SGN + 1], None, ALU.mult))

            def rope(dst, ps, scale):
                nc.vector.scalar_tensor_tensor(dst, ps[64:96, :], scale, trig[64:96, 1, :], ALU.mult, ALU.mult)
                return nc.vector.scalar_tensor_tensor(rtmp[64:96, :], ps[96:P, :], scale, trig[96:P, 0, :], ALU.mult,
                                                      ALU.mult)

            ps = tile("kr2", 0)
            dve.wait_ge(pads2_zero, 1)
            freed(rope(krr[64:96, :], ps, 1.0))
            evacuated(dve, "kr2", 0)
            nc.vector.tensor_tensor(krr[64:96, :], krr[64:96, :], rtmp[64:96, :], ALU.add).then_inc(kr_ready, 1)
            dve.wait_ge(kr_ready, 1)
            for j in range(3):
                dve.wait_ge(lat_rn, 1 + j // 2)
                gain = g_of("q_norm_2", j) if j < 2 else g_of("kv_norm_2", 0)
                hi, lo = (cqh[:, j, :], cql[:, j, :]) if j < 2 else (ckh[:, 0, :], ckl[:, 0, :])
                c = cq[:, j, :]
                link(nc.vector.scalar_tensor_tensor(c, c, gain, wt[:, j // 2, :], ALU.mult, ALU.mult))
                link(nc.vector.tensor_copy(hi, c))
                nc.vector.tensor_tensor(lo, c, hi.bitcast(F32), ALU.subtract).then_inc(cq_ready, 1)
            dve.wait_ge(cq_ready, 3)

            def query(h):
                ps = tile("uq2", h)
                nc.vector.tensor_scalar(qf[0:64, h, :], ps[0:64, :], ATT_SCALE, None, ALU.mult)
                freed(rope(qf[64:96, h, :], ps, ATT_SCALE))
                evacuated(dve, "uq2", h)
                link(nc.vector.tensor_tensor(qf[64:96, h, :], qf[64:96, h, :], rtmp[64:96, :], ALU.add))

            parts = {(0, 1): 0, (0, 3): 1, (1, 1): 2, (1, 3): 3}
            for h in range(H):
                def args(j):
                    n = T - j * P
                    if 4 * h + j >= 2:
                        dve.wait_ge(s_done, 4 * h + j - 1)
                    nc.vector.tensor_scalar(wt[:, j % 2, 0:n], mrow[:, j * P:T], cT[:, j, h:h + 1], 0.0, ALU.subtract,
                                            ALU.max).then_inc(wt_args, 1)

                dve.wait_ge(mrow_ready, 2 * h + 1)
                args(0)
                args(1)
                for j in range(NC):
                    n = T - j * P
                    dve.wait_ge(wt_ready, 4 * h + j + 1)
                    dve.wait_ge(ms_ps, 4 * h + j + 1)
                    if 4 * h + j >= 2:
                        dve.wait_ge(nd_ps, 4 * h + j - 1)
                    link(nc.vector.scalar_tensor_tensor(st[:, j % 2, 0:n], aux[j % 2][:, 0:n], 0.125,
                                                        wt[:, j % 2, 0:n], ALU.mult, ALU.mult))
                    nc.vector.tensor_tensor(st[:, j % 2, 0:P], st[:, j % 2, 0:P], cst[:, C_UP:C_UP + P],
                                            ALU.mult).then_inc(s_done, 1)
                    if j + 2 < NC:
                        args(j + 2)
                    if (h, j) in parts:
                        query(2 * parts[h, j])
                        query(2 * parts[h, j] + 1)
                dve.wait_ge(nd_ps, 4 * (h + 1))
                dve.wait_ge(mrow_ready, 2 * h + 2)
                link(nc.vector.scalar_tensor_tensor(dn[:, :], aux[3][:, :], -1.0, erow[:, :], ALU.mult, ALU.max))
                link(nc.vector.tensor_tensor(dn[:, :], aux[3][:, :], dn[:, :], ALU.max))
                link(nc.vector.reciprocal(dn[:, :], dn[:, :]))
                nc.vector.tensor_tensor(hm[:, :], aux[2][:, :], dn[:, :], ALU.mult).then_inc(hm_ready, 1)
                dve.wait_ge(hm_ready, h + 1)
                dve.wait_ge(ml_rn, h + 1)
                link(nc.vector.scalar_tensor_tensor(hm[:, :], hm[:, :], g_of("ml_head_norm_2", h), rstd[:, :],
                                                    ALU.mult, ALU.mult))
                evacuated(dve, "o2", h)
                dve.wait_ge(al_ready, KD * F_MIX2 + max(0, h - 2))
                nc.vector.tensor_tensor(h32[:, h % 3, :], hm[:, :], og[:, h, :], ALU.mult).then_inc(h32_ready, 1)
                lower(F_MIX2, h, h, h32[:, h % 3, :])

            NI = MLA_H * NC
            pv = [bank[2], aux[3]]

            def maxima(i):
                n = (i % NC + 1) * P
                dve.wait_ge(as_ps, i + 1)
                nc.vector.tensor_reduce(am[:, 0, i:i + 1], aux[i % 2][:, 0:n], AX_X, ALU.max, negate=True).then_inc(
                    max_ready, 1)

            maxima(0)
            maxima(1)
            for i in range(NI):
                n = (i % NC + 1) * P
                dve.wait_ge(prob_ready, i + 1)
                link(nc.vector.reciprocal(am[:, 2, i:i + 1], am[:, 1, i:i + 1]))
                nc.vector.tensor_scalar(pm[:, i % 3, 0:n], pm[:, i % 3, 0:n], am[:, 2, i:i + 1], None,
                                        ALU.mult).then_inc(prob_scaled, 1)
                if i + 2 < NI:
                    maxima(i + 2)
                if i in SPLIT_AT:
                    t = SPLIT_AT.index(i)
                    lower(F_MIX2, 4 + t, 4 + t, pv[t % 2][:, :])
            lower(F_MIX2, 7, 7, pv[1][:, :])

            for m in range(KD):
                ps = tile("wout2", m)
                freed(nc.vector.tensor_copy(acc[:, m, :], ps))

            def add_normed(n, gain, done):
                dve.wait_ge(rstd_ready, n + 1)
                for k in range(KD):
                    if k >= 3:
                        dve.wait_ge(done, k - 2)
                    link(nc.vector.scalar_tensor_tensor(h32[:, k % 3, :], acc[:, k, :], g_of(gain, k), rstd[:, :],
                                                        ALU.mult, ALU.mult))
                    nc.vector.tensor_tensor(x[:, k, :], x[:, k, :], h32[:, k % 3, :], ALU.add).then_inc(done, 1)

            evacuated(dve, "wout2", KD - 1)
            dve.wait_ge(al_ready, KD * (F_MIX2 + 1))
            add_normed(4, "norm_post_mix_2", x_mixed)
            dve.wait_ge(x_mixed, KD)
            norm_fill(5, F_NORM5, "norm_pre_mlp_2", 0)
            n = 0
            for c in range(len(MLP2) + 1):
                if c < len(MLP2):
                    for j in range(MLP2[c]):
                        if c >= 2 and j == 0:
                            dve.wait_ge(gemm_done, pl.done("down2", (c - 2, KD - 1)))
                        dve.wait_ge(relu_sq, n + 1)
                        y = y32[:, n % 2, :]
                        link(nc.vector.tensor_copy(yh[c % 2][:, j, :], y))
                        nc.vector.tensor_tensor(yl[c % 2][:, j, :], y, yh[c % 2][:, j, :].bitcast(F32),
                                                ALU.subtract).then_inc(y_ready[1], 1)
                        n += 1
                if c > 0:
                    for m in range(KD):
                        ps = tile("down2", (c - 1, m))
                        if c == 1:
                            freed(nc.vector.tensor_copy(acc[:, m, :], ps))
                        else:
                            evacuated(dve, "down2", (c - 2, m))
                            freed(nc.vector.tensor_tensor(acc[:, m, :], ps, acc[:, m, :], ALU.add))
            evacuated(dve, "down2", (len(MLP2) - 1, KD - 1))
            dve.wait_ge(al_ready, KD * (F_NORM5 + 1))
            add_normed(6, "norm_post_mlp_2", x_last)
            for k in range(1, KD, 2):
                dve.wait_ge(ot_ps, k + 1)
                nc.vector.tensor_copy(otok[:, :, k * P:(k + 1) * P], auxh[k % 3][:, :, :]).then_inc(out_dve, 1)

        def out_evac(k):
            return (out_dve if k % 2 else out_act), k // 2 + 1

        def stores(sp):
            for half in range(2):
                sp.wait_ge(out_act, 2 * half + 2)
                sp.wait_ge(out_dve, 2 * half + 2)
                s = slice(half * (D // 2), (half + 1) * (D // 2))
                sp.dma_start(out[0].rearrange("(c p) n -> p c n", p=P)[:, :, s], otok[:, :, s]).then_inc(out_stored, 16)
            sp.wait_ge(out_stored, 32)

        block = ctx.enter_context(nc.Block())

        @block.sync
        def _(sp):
            for c in range(NC):
                sp.dma_start(xtok[:, c, :], ins["x"][0, c * P:(c + 1) * P, :]).then_inc(x_loaded, 16)
            for b in range(len(pl.blocks)):
                if b >= RAW:
                    sp.wait_ge(wl_ready, b - RAW + 1)
                for dst, src in parts(b):
                    sp.dma_start(dst, src).then_inc(raw_loaded[b % RAW], 16)
            stores(sp)

        @block.gpsimd
        def _(pool):
            count = [0]

            def link(i):
                count[0] += 1
                i.then_inc(pool_step, 1)
                pool.wait_ge(pool_step, count[0])

            nc.gpsimd.memset(bw[:, :, :], 0.0).then_inc(bw_zero, 1)
            pool.wait_ge(bw_zero, 1)
            for g in range(4):
                r = 64 * (g % 2)
                pool.dma_start(bw[r:r + 64, g // 2, r:r + 64], ins["pool_w"][0, g]).then_inc(bw_loaded, 16)
            pool_at = pl.tiles[pl.at["hp", 1]][2] + SPLIT
            for b in range(len(pl.blocks)):
                pool.wait_ge(wh_ready, b + 1)
                w = block_cols(b)
                nc.gpsimd.tensor_tensor(wl[b % SPLIT][:, 0:w], raw[b % RAW][:, 0:w],
                                        wh[b % SPLIT][:, 0:w].bitcast(F32), ALU.subtract).then_inc(wl_ready, 1)
                if b == pool_at:
                    multiscale(pool, link)

        @block.tensor
        def _(pe):
            state = dict(t=0)

            def gemm(kind, idx, mov=None, ready=None, order=None):
                t = state["t"]
                k_, i_, b, col, nk, stride = pl.tiles[t]
                assert (k_, i_) == (kind, idx), (k_, i_, kind, idx)
                state["t"] += 1
                pe.wait_ge(wl_ready, b + 1)
                if t >= NBANK:
                    eng, n = pl.read[t - NBANK]
                    pe.wait_ge(bank_read[eng], n)
                mh, ml = mov or (ah, al)
                h, l = wh[b % SPLIT], wl[b % SPLIT]
                ps = bank[t % NBANK][:, :]
                for n, k in enumerate(order or range(nk)):
                    if ready:
                        pe.wait_ge(ready[0], ready[1] + n + 1)
                    c = k * stride + col
                    nc.tensor.matmul(ps, h[:, c:c + P], mh[:, k, :], start=(n == 0), stop=False)
                    nc.tensor.matmul(ps, l[:, c:c + P], mh[:, k, :], start=False, stop=False)
                    last = nc.tensor.matmul(ps, h[:, c:c + P], ml[:, k, :], start=False, stop=(n == nk - 1))
                last.then_inc(gemm_done, 1)

            def ssq(n, k):
                pe.wait_ge(sq_ready, KD * n + k + 1)
                if k == 0 and n > 0:
                    pe.wait_ge(rstd_ready, n)
                nc.tensor.matmul(aux[3][:, :], ones[:, :], sq[:, k % 2, :], start=(k == 0),
                                 stop=(k == KD - 1)).then_inc(ssq_done, 1)

            def transpose4(dst, src):
                for c in range(NC):
                    last = nc.tensor.transpose(dst[:, c * P:(c + 1) * P], src[:, c * P:(c + 1) * P], ident)
                return last

            pe.wait_ge(consts_loaded, 16 * (len(PARAMS) + 1))
            pe.wait_ge(ones_set, 1)
            nc.tensor.transpose(aux[3][:, 0:PSPLIT], prow[0:PSPLIT, 0, :], ident[0:PSPLIT, 0:PSPLIT])
            n2 = NPARAM - PSPLIT
            nc.tensor.transpose(aux[3][:, P:P + n2], prow[0:n2, 1, :], ident[0:n2, 0:n2]).then_inc(par_ps, 1)
            pe.wait_ge(x_loaded, 16 * NC)
            for k in range(KD):
                if k >= 3:
                    pe.wait_ge(x_ready, k - 2)
                for c in range(NC):
                    last = nc.tensor.transpose(aux[k % 3][:, c * P:(c + 1) * P], xtok[:, c, k * P:(k + 1) * P], ident)
                last.then_inc(xt_ps, 1)
                if k == 0:
                    pe.wait_ge(par_ready, 1)
                if k > 0:
                    ssq(0, k - 1)
            ssq(0, KD - 1)

            gemm("ab", 0, ready=(al_ready, 0))
            gemm("k", 0)
            gemm("k", 1)
            pe.wait_ge(decay_sums_ready, 1)
            pe.wait_ge(beta_ready, 1)
            for r in range(2 * H):
                if r >= 2:
                    pe.wait_ge(rows_ready, r - 1)
                row = ident[0:8, r:r + 1].to_broadcast([8, P])
                nc.tensor.matmul(aux[r % 2][:, :], row, (gcs if r < H else gbt)[:, :], start=True,
                                 stop=True).then_inc(rows_ps, 1)
            for c in range(NC):
                nc.tensor.transpose(aux[2][:, 16 * c:16 * c + 8], gcs[:, c * P:(c + 1) * P], ident[0:8, 0:8])
                last = nc.tensor.transpose(aux[2][:, 16 * c + 8:16 * c + 16], gbt[:, c * P:(c + 1) * P],
                                           ident[0:8, 0:8])
            last.then_inc(gt_ps, 1)
            gemm("k", 2)
            gemm("k", 3)
            gemm("q", 0)
            gemm("q", 1)

            def head_sums(j0):
                for j in range(j0, j0 + H):
                    pe.wait_ge(head_sq, j + 1)
                    if j == 0:
                        pe.wait_ge(rows_ready, 2 * H)
                        pe.wait_ge(gt_ready, 1)
                        pe.wait_ge(rstd_ready, 1)
                    if j >= H:
                        pe.wait_ge(head_rn, j - H + 1)
                        if j % H >= 2:
                            pe.wait_ge(kd_ready, H)
                    nc.tensor.matmul(aux[j % 4][:, :], ones[:, :], sq[:, j % 2, :], start=True,
                                     stop=True).then_inc(head_ss, 1)

            head_sums(0)
            gemm("q", 2)
            for h in range(H):
                pe.wait_ge(head_normed, h + 1)
                pe.wait_ge(head_rn, H)
                if h >= 2:
                    pe.wait_ge(kd_ready, h - 1)
                transpose4(aux[2 + h % 2], kT[:, h, :]).then_inc(kt_ps, 1)
            gemm("q", 3)
            gemm("v", 0)
            gemm("v", 1)
            head_sums(H)

            def v_transposes(h):
                pe.wait_ge(silu_ready, 2 * H + h + 1)
                pe.wait_ge(head_rn, 2 * H)
                if h >= 2:
                    pe.wait_ge(bv_ready, h - 1)
                transpose4(aux[2 + h % 2], vT[h % 2][:, :]).then_inc(vt_ps, 1)

            gemm("v", 2)
            v_transposes(0)
            v_transposes(1)
            gemm("v", 3)
            v_transposes(2)
            v_transposes(3)
            pe.wait_ge(head_normed, 2 * H)
            for c in range(NC):
                if c < 2:
                    pe.wait_ge(bv_ready, H)
                else:
                    pe.wait_ge(at_ready, c - 1)
                s = slice(c * P, (c + 1) * P)
                for h in range(H):
                    nc.tensor.matmul(auxh[2 * (c % 2)][:, h, :], kT[:, h, s], kT[:, h, s], start=True, stop=True)
                for h in range(H):
                    last = nc.tensor.matmul(auxh[2 * (c % 2) + 1][:, h, :], kT[:, h, s], qT[:, h, s],
                                            start=True, stop=True)
                last.then_inc(gram_ps, 1)
                gemm(*(("hp", 0), ("hp", 1), ("ch", 0), ("ch", 1))[c])

            fill = {(0, 1): ("cc", 0), (0, 3): ("cc", 1), (0, 5): ("cb", 0), (1, 1): ("cb", 1)}
            for pair in range(2):
                for lev in range(LEVELS):
                    n0 = INV_PAIR * pair + 2 * lev
                    m0 = (INV_PAIR - 2) * pair + 2 * (lev - 1)
                    for e in range(2):
                        pe.wait_ge(um_ready, n0 + e + 1)
                        if lev == 0:
                            if pair == 0:
                                pe.wait_ge(at_ready, NC)
                            else:
                                pe.wait_ge(xy_ready, INV_PAIR)
                            for h in range(H):
                                last = nc.tensor.transpose(auxh[2 * e + 1][:, h, :], UM[:, e, h, :], ident)
                            last.then_inc(xy_ps, 1)
                            continue
                        pe.wait_ge(xy_ready, n0 + e - 1)
                        for h in range(H):
                            last = nc.tensor.matmul(auxh[2 * e][:, h, :], UM[:, e, h, :], X[:, e, h, :],
                                                    start=True, stop=True)
                        last.then_inc(p_ps, 1)
                    if lev == 0:
                        continue
                    if (pair, lev) in fill:
                        gemm(*fill[pair, lev])
                    for e in range(2):
                        pe.wait_ge(p_ready, m0 + e + 1)
                        c = 2 * pair + e
                        if lev < LEVELS - 1:
                            for h in range(H):
                                nc.tensor.matmul(auxh[2 * e + 1][:, h, :], Y[:, c, h, :], PS[:, e, h, :],
                                                 start=True, stop=True)
                        for h in range(H):
                            last = nc.tensor.matmul(auxh[2 * e][:, h, :], PS[:, e, h, :], Y[:, c, h, :],
                                                    start=True, stop=True)
                        last.then_inc(xy_ps, 1)

            for c in range(NC):
                s = slice(c * P, (c + 1) * P)
                if c == 0:
                    pe.wait_ge(xy_ready, 2 * INV_PAIR)
                else:
                    pe.wait_ge(s_ready, c)
                    for h in range(H):
                        last = nc.tensor.matmul(auxh[0][:, h, :], kT[:, h, s], S[:, h, :], start=True, stop=True)
                    last.then_inc(ks_ps, 1)
                if c > 0:
                    gemm("z", c - 1)
                    pe.wait_ge(rr_ready, c)
                    pe.wait_ge(vn_ready, c)
                for h in range(H):
                    last = nc.tensor.matmul(auxh[1][:, h, :], Y[:, c, h, :],
                                            bv[:, 0, h, :] if c == 0 else rr[:, h, :], start=True, stop=True)
                last.then_inc(vn_ps, 1)
                if c > 0:
                    pe.wait_ge(o_ready, c)
                pe.wait_ge(vn_ready, c + 1)
                if c < NC - 1:
                    for h in range(H):
                        last = nc.tensor.matmul(auxh[3][:, h, :], kd[:, c, h, :], vn[:, h, :], start=True, stop=True)
                    last.then_inc(su_ps, 1)
                if c == 1:
                    pe.wait_ge(qg_ready, H)
                for h in range(H):
                    if c > 0:
                        nc.tensor.matmul(auxh[2][:, h, :], S[:, h, :], qg[:, h, s], start=True, stop=False)
                    last = nc.tensor.matmul(auxh[2][:, h, :], vn[:, h, :], AT[:, c, h, :], start=(c == 0), stop=True)
                last.then_inc(o_ps, 1)
            gemm("z", 3)
            pe.wait_ge(bw_loaded, 64)
            for t in range(2):
                pe.wait_ge(pooled_ready, t + 1)
                nc.tensor.matmul(aux[t][:, :], bw[:, t, :], pooled[:, t, :], start=True, stop=True).then_inc(pool_ps, 1)
            for h in range(H):
                pe.wait_ge(osq_ready, h + 1)
                if h == 2:
                    pe.wait_ge(h32_ready, H32_BASE[F_MIX1] + 2)
                bk = (2, 3, 0, 1)[h]
                nc.tensor.matmul(aux[bk][:, :], ones[:, :], sq[:, h % 2, :], start=True, stop=True).then_inc(oss_ps, 1)
            for m in range(KD):
                gemm("wout", m, ready=(al_ready, KD * F_MIX1) if m == 0 else None, order=MIX1_ORDER)
                if m == 2:
                    pe.wait_ge(orn_ready, H)
                if m >= 2:
                    ssq(1, m - 2)
            ssq(1, KD - 2)
            ssq(1, KD - 1)
            tensor_rest(pe, gemm, ssq, transpose4, state)

        @block.scalar
        def _(act):
            count = [0]
            nxt = [0]
            tnow = [0]

            def link(i):
                count[0] += 1
                i.then_inc(act_step, 1)
                act.wait_ge(act_step, count[0])

            def tables(n):
                act.add_instruction(mybir.InstLoadActFuncSet(name=nc.get_next_instruction_name(), act_func_set_id=n,
                                                             ins=[], outs=[]))

            def split(upto):
                while nxt[0] < len(pl.blocks) and (nxt[0] < SPLIT or pl.last[nxt[0] - SPLIT] <= upto):
                    b = nxt[0]
                    act.wait_ge(raw_loaded[b % RAW], landed(b))
                    if b >= SPLIT:
                        act.wait_ge(gemm_done, pl.last[b - SPLIT] + 1)
                    w = block_cols(b)
                    nc.scalar.copy(wh[b % SPLIT][:, 0:w], raw[b % RAW][:, 0:w]).then_inc(wh_ready, 1)
                    nxt[0] += 1

            def tile(kind, idx, read=None):
                t = tnow[0]
                assert pl.tiles[t][:2] == (kind, idx), (pl.tiles[t], kind, idx)
                tnow[0] += 1
                if read is not None:
                    assert pl.READER[kind] == "act"
                    act.wait_ge(gemm_done, t + 1)
                    read(bank[t % NBANK][:, :]).then_inc(bank_read["act"], 1)
                split(t)

            def square(n, k, src):
                if k >= 2 or n > 0:
                    act.wait_ge(ssq_done, KD * n + k - 1)
                nc.scalar.activation(sq[:, k % 2, :], src, ACT.Square).then_inc(sq_ready, 1)

            def norm(n, scale=1.0 / D):
                act.wait_ge(ssq_done, KD * (n + 1))
                tables(LN_EXP_TABLES)
                if n in RSTD_FREE:
                    act.wait_ge(*RSTD_FREE[n])
                link(nc.scalar.activation(rstd[:, :], aux[3][:, :], ACT.Ln, bias=eps[:, 0:1], scale=scale))
                nc.scalar.activation(rstd[:, :], rstd[:, :], ACT.Exp, scale=-0.5).then_inc(rstd_ready, 1)

            def upper(fill, i, k, src, wait):
                if i == 0 and fill > 0:
                    act.wait_ge(gemm_done, LAST_USE[fill - 1])
                    act.wait_ge(al_ready, KD * fill)
                act.wait_ge(*wait)
                nc.scalar.copy(ah[:, k, :], src).then_inc(ah_ready, 1)

            for i, (name, rows) in enumerate(PARAMS):
                second = PCOL[name] >= PSPLIT
                r = PCOL[name] - (PSPLIT if second else 0)
                v = ins[name]
                if len(v.shape) == 3:
                    v = v.rearrange("a b c -> (a b c)")
                elif len(v.shape) == 2:
                    v = v.rearrange("a b -> (a b)")
                act.dma_start(prow[r:r + rows, int(second), :], v.rearrange("(r c) -> r c", c=P)).then_inc(
                    consts_loaded, 16)
            act.dma_start(cst[:, :], ins["constants"]).then_inc(consts_loaded, 16)
            act.wait_ge(cols_zero, 1)
            act.dma_start(cols[0:H, 0:1], ins["dt_bias"].rearrange("a h -> h a")).then_inc(cols_loaded, 16)
            act.dma_start(cols[0:H, 1:2], ins["a_log"].rearrange("a h -> h a")).then_inc(cols_loaded, 16)
            act.dma_start(cols[0:2 * H, 3:4], ins["b_gates_2"].rearrange("a h -> h a")).then_inc(cols_loaded, 16)
            split(-1)
            for k in range(KD):
                act.wait_ge(x_ready, k + 1)
                square(0, k, x[:, k, :])
            act.wait_ge(eps_set, 1)
            norm(0)
            act.wait_ge(cols_loaded, 48)
            nc.scalar.activation(cols[0:8, 2:3], cols[0:8, 1:2], ACT.Exp).then_inc(alog_exp, 1)
            for k in range(KD):
                upper(F_NORM1, k, k, h32[:, k % 3, :], (h32_ready, k + 1))

            tile("ab", 0)
            evacuated(act, "ab", 0)
            link(nc.scalar.activation(gsp[:, :], gab[:, :], ACT.Abs))
            link(nc.scalar.activation(gsp[:, :], gsp[:, :], ACT.Exp, scale=-1.0))
            nc.scalar.activation(gsp[:, :], gsp[:, :], ACT.Ln, bias=1.0).then_inc(softplus_ready, 1)
            nc.scalar.activation(gbt[:, :], gab[:, :], ACT.Sigmoid).then_inc(beta_ready, 1)

            def conv_evac(j):
                kind, h = HEADS[j]
                if j >= 2:
                    act.wait_ge(conv_done, j - 1)
                    act.wait_ge(silu_ready, j - 1)
                tap = g_of("conv_qkv", 3 * 12 + conv_tile(j))
                t = tnow[0]
                act.wait_ge(gemm_done, t + 1)
                act.wait_ge(pads_zero, 1)
                nc.scalar.copy(craw[j % 2][:, 3:3 + T], bank[t % NBANK][:, :])
                tile(kind, h, lambda ps: nc.scalar.activation(cc[j % 2][:, :], ps, ACT.Copy, scale=tap))

            def conv_silu(j):
                kind, h = HEADS[j]
                act.wait_ge(conv_done, j + 1)
                if kind == "v" and h >= 2:
                    act.wait_ge(vt_ps, h - 1)
                dst = vT[h % 2][:, :] if kind == "v" else {"k": kT, "q": qT}[kind][:, h, :]
                nc.scalar.activation(dst, cc[j % 2][:, :], ACT.Silu).then_inc(silu_ready, 1)

            conv_evac(0)
            conv_evac(1)
            conv_silu(0)
            for r in range(2 * H):
                act.wait_ge(rows_ps, r + 1)
                nc.scalar.copy((GR if r < H else BR)[:, r % H, :], aux[r % 2][:, :]).then_inc(rows_ready, 1)
            conv_evac(2)
            conv_silu(1)
            act.wait_ge(eg_args, 1)
            tables(LN_EXP_TABLES)
            nc.scalar.activation(eg[:, 0, :, :], gT[:, :, 0:H], ACT.Exp)
            nc.scalar.activation(eg[:, 1, :, :], eg[:, 3, :, :], ACT.Exp)
            nc.scalar.activation(eg[:, 2, :, :], GR[:, :, :].rearrange("p h (c t) -> p c h t", c=NC)[:, :, :, P - 1],
                                 ACT.Exp).then_inc(eg_exps, 1)
            conv_evac(3)
            conv_silu(2)
            conv_evac(4)
            conv_silu(3)

            def head_norm(j0):
                src = kT if j0 == 0 else qT
                for j in range(j0, j0 + H):
                    if j >= 2:
                        act.wait_ge(head_ss, j - 1)
                    act.wait_ge(silu_ready, j + 1)
                    nc.scalar.activation(sq[:, j % 2, :], src[:, j % H, :], ACT.Square).then_inc(head_sq, 1)
                tables(LN_EXP_TABLES)
                for j in range(j0, j0 + H):
                    act.wait_ge(head_ss, j + 1)
                    if j == 0:
                        act.wait_ge(al_ready, KD)
                    if j >= 2:
                        act.wait_ge(head_normed, j - 1)
                    link(nc.scalar.activation(h32[:, j % 2, :], aux[j % 4][:, :], ACT.Ln, bias=eps[:, 0:1]))
                    nc.scalar.activation(h32[:, j % 2, :], h32[:, j % 2, :], ACT.Exp, scale=-0.5).then_inc(head_rn, 1)

            act.wait_ge(ssq_done, KD)
            conv_evac(5)
            head_norm(0)
            conv_silu(4)
            conv_evac(6)
            conv_silu(5)
            conv_evac(7)
            conv_silu(6)
            conv_evac(8)
            conv_silu(7)
            conv_evac(9)
            head_norm(H)
            conv_silu(8)
            conv_evac(10)
            conv_silu(9)
            conv_evac(11)
            conv_silu(10)
            conv_silu(11)
            tables(LN_EXP_TABLES)
            for c in range(NC):
                act.wait_ge(dt_args, c + 1)
                nc.scalar.activation(AT[:, c], AT[:, c], ACT.Exp).then_inc(dt_exp, 1)
            for h in range(H):
                nc.scalar.activation(GR[:, h, :], GR[:, h, :], ACT.Exp).then_inc(gr_exp, 1)
            for t in range(2):
                tile("hp", t, lambda ps: nc.scalar.copy(pin[:, t, 16:16 + T], ps))
            tile("ch", 0)
            tile("ch", 1)
            fill = {(0, 1): ("cc", 0), (0, 3): ("cc", 1), (0, 5): ("cb", 0), (1, 1): ("cb", 1)}
            for pair in range(2):
                for lev in range(1, LEVELS):
                    m0 = (INV_PAIR - 2) * pair + 2 * (lev - 1)
                    for e in range(2):
                        act.wait_ge(p_ps, m0 + e + 1)
                        nc.scalar.copy(PS[:, e], auxh[2 * e][:, :, :]).then_inc(p_ready, 1)
                    if (pair, lev) in fill:
                        tile(*fill[pair, lev])

            def z_tile(h):
                act.wait_ge(qg_ready, H)
                tile("z", h, lambda ps: nc.scalar.activation(zs[:, h, :], ps, ACT.Silu))

            for c in range(NC):
                act.wait_ge(vn_ps, c + 1)
                if c > 0:
                    act.wait_ge(o_ps, c)
                else:
                    act.wait_ge(xy_ready, 2 * INV_PAIR)
                nc.scalar.copy(vn[:, :, :], auxh[1][:, :, :]).then_inc(vn_ready, 1)
                if c > 0:
                    z_tile(c - 1)
                act.wait_ge(o_ps, c + 1)
                if c == 0:
                    act.wait_ge(qg_ready, H)
                    act.wait_ge(pooled_ready, 2)
                nc.scalar.copy(oT[:, :, c * P:(c + 1) * P], auxh[2][:, :, :]).then_inc(o_ready, 1)
            act.wait_ge(o_ready, NC)
            for h in range(H):
                if h >= 2:
                    act.wait_ge(oss_ps, h - 1)
                nc.scalar.activation(sq[:, h % 2, :], oT[:, h, :], ACT.Square).then_inc(osq_ready, 1)
                if h == 1:
                    z_tile(3)
            for i in range(2):
                upper(F_MIX1, i, MIX1_ORDER[i], h32[:, i % 3, :], (h32_ready, H32_BASE[F_MIX1] + i + 1))
            for i in range(2):
                upper(F_MIX1, 2 + i, MIX1_ORDER[2 + i], convd[:, i, :], when_read("cb", i))
            tables(LN_EXP_TABLES)
            for h in range(H):
                act.wait_ge(oss_ps, h + 1)
                if h >= 2:
                    act.wait_ge(h32_ready, H32_BASE[F_MIX1] + 2 + h - 1)
                rn = orn[h % 2]
                link(nc.scalar.activation(rn[:, :], aux[(2, 3, 0, 1)[h]][:, :], ACT.Ln, bias=eps[:, 0:1],
                                          scale=1.0 / P))
                nc.scalar.activation(rn[:, :], rn[:, :], ACT.Exp, scale=-0.5).then_inc(orn_ready, 1)
                if h > 0:
                    upper(F_MIX1, 3 + h, h - 1, h32[:, (1 + h) % 3, :], (h32_ready, H32_BASE[F_MIX1] + 2 + h))
            upper(F_MIX1, 7, 3, h32[:, 5 % 3, :], (h32_ready, H32_BASE[F_MIX1] + 6))
            for m in range(KD):
                tile("wout", m)
                if m > 0:
                    evacuated(act, "wout", m - 1)
                    square(1, m - 1, x[:, m - 1, :])
            evacuated(act, "wout", KD - 1)
            square(1, KD - 1, x[:, KD - 1, :])
            scalar_rest(act, link, tables, tile, square, norm, upper)

        @block.vector
        def _(dve):
            count = [0]
            tnow = [0]

            def link(i):
                count[0] += 1
                i.then_inc(dve_step, 1)
                dve.wait_ge(dve_step, count[0])

            def tile(kind, idx):
                while pl.READER[pl.tiles[tnow[0]][0]] != "dve":
                    tnow[0] += 1
                t = tnow[0]
                assert pl.tiles[t][:2] == (kind, idx), (pl.tiles[t], kind, idx)
                tnow[0] += 1
                dve.wait_ge(gemm_done, t + 1)
                return bank[t % NBANK][:, :]

            def freed(i):
                return i.then_inc(bank_read["dve"], 1)

            def lower(fill, i, k, src):
                dve.wait_ge(ah_ready, KD * fill + i + 1)
                nc.vector.tensor_tensor(al[:, k, :], src, ah[:, k, :].bitcast(F32), ALU.subtract).then_inc(al_ready, 1)

            def norm_fill(n, fill, gain, base):
                dve.wait_ge(rstd_ready, n + 1)
                for k in range(KD):
                    if fill or k >= 3:
                        dve.wait_ge(al_ready, KD * fill + max(0, k - 2))
                    i = nc.vector.scalar_tensor_tensor(h32[:, k % 3, :], x[:, k, :], g_of(gain, k), rstd[:, :],
                                                       ALU.mult, ALU.mult)
                    i.then_inc(h32_ready, 1)
                    if k > 0:
                        lower(fill, k - 1, k - 1, h32[:, (k - 1) % 3, :])
                lower(fill, KD - 1, KD - 1, h32[:, (KD - 1) % 3, :])

            nc.vector.memset(ones[:, :], 1.0).then_inc(ones_set, 1)
            nc.vector.memset(eps[:, :], EPS).then_inc(eps_set, 1)
            nc.vector.memset(cols[:, :], 0.0).then_inc(cols_zero, 1)
            for i in range(2):
                nc.vector.memset(craw[i][:, 0:3], 0.0)
                nc.vector.memset(cin[:, i, 0:2], 0.0)
            dve.wait_ge(par_ps, 1)
            nc.vector.tensor_copy(par[:, 0:PSPLIT], aux[3][:, 0:PSPLIT])
            nc.vector.tensor_copy(par[:, PSPLIT:NPARAM], aux[3][:, P:P + NPARAM - PSPLIT]).then_inc(par_ready, 1)
            nc.vector.memset(pin[:, 0, 0:16], 0.0)
            nc.vector.memset(pin[:, 1, 0:16], 0.0).then_inc(pads_zero, 1)
            for k in range(KD):
                dve.wait_ge(xt_ps, k + 1)
                nc.vector.tensor_copy(x[:, k, :], aux[k % 3][:, :]).then_inc(x_ready, 1)
            dve.wait_ge(x_ready, KD)
            norm_fill(0, F_NORM1, "norm1_g", 0)

            ps = tile("ab", 0)
            dve.wait_ge(cols_loaded, 48)
            freed(nc.vector.tensor_scalar(gab[:, :], ps[0:8, :], cols[0:8, 0:1], None, ALU.add))
            evacuated(dve, "ab", 0)
            dve.wait_ge(alog_exp, 1)
            link(nc.vector.tensor_scalar(cols[0:8, 2:3], cols[0:8, 2:3], -1.0, None, ALU.mult))
            dve.wait_ge(softplus_ready, 1)
            link(nc.vector.scalar_tensor_tensor(gsp[:, :], gab[:, :], 0.0, gsp[:, :], ALU.max, ALU.add))
            link(nc.vector.tensor_scalar(gsp[:, :], gsp[:, :], cols[0:8, 2:3], None, ALU.mult))
            for c in range(NC):
                s = slice(c * P, (c + 1) * P)
                last = nc.vector.tensor_tensor_scan(gcs[:, s], ones[0:8, :], gsp[:, s], 0.0, ALU.mult, ALU.add)
            last.then_inc(decay_sums_ready, 1)

            def conv(j):
                r, c = craw[j % 2], cc[j % 2]
                evacuated(dve, *HEADS[j])
                for tap in (2, 1, 0):
                    i = nc.vector.scalar_tensor_tensor(c[:, :], r[:, tap:tap + T],
                                                       g_of("conv_qkv", 12 * tap + conv_tile(j)), c[:, :],
                                                       ALU.mult, ALU.add)
                    if tap:
                        link(i)
                i.then_inc(conv_done, 1)

            def head_norm(j):
                dve.wait_ge(head_rn, j + 1)
                dst = (kT if j < H else qT)[:, j % H, :]
                rn = h32[:, j % 2, :]
                if j < H:
                    i = nc.vector.tensor_tensor(dst, dst, rn, ALU.mult)
                else:
                    i = nc.vector.scalar_tensor_tensor(dst, dst, float(P) ** -0.5, rn, ALU.mult, ALU.mult)
                i.then_inc(head_normed, 1)

            def over_chunks(col):
                return col.unsqueeze(2).to_broadcast([P, NC, P])

            conv(0)
            conv(1)
            dve.wait_ge(gt_ps, 1)
            nc.vector.tensor_copy(gT[:, :, :], aux[2][:, 0:16 * NC].rearrange("p (c n) -> p c n", n=16)).then_inc(
                gt_ready, 1)
            dve.wait_ge(gt_ready, 1)
            dve.wait_ge(rows_ready, H)
            last_g = GR[:, :, :].rearrange("p h (c t) -> p c h t", c=NC)[:, :, :, P - 1]
            nc.vector.tensor_tensor(eg[:, 3, :, :], last_g, gT[:, :, 0:H], ALU.subtract).then_inc(eg_args, 1)
            conv(2)
            dve.wait_ge(eg_exps, 1)
            link(nc.vector.tensor_tensor(eg[:, 0, :, :], eg[:, 0, :, :], gT[:, :, 12:16], ALU.mult))
            conv(3)
            conv(4)
            for j in range(H):
                head_norm(j)
            conv(5)
            for h in range(H):
                dve.wait_ge(kt_ps, h + 1)
                nc.vector.tensor_tensor(kd[:, :, h, :], auxh[2 + h % 2][:, :, :], over_chunks(eg[:, 1, :, h]),
                                        ALU.mult).then_inc(kd_ready, 1)
                if h == 1:
                    conv(6)
            conv(7)
            conv(8)
            conv(9)
            for j in range(H, 2 * H):
                head_norm(j)

            def scaled_v(h):
                dve.wait_ge(vt_ps, h + 1)
                nc.vector.tensor_tensor(bv[:, :, h, :], auxh[2 + h % 2][:, :, :], over_chunks(gT[:, :, 12 + h]),
                                        ALU.mult).then_inc(bv_ready, 1)

            conv(10)
            scaled_v(0)
            scaled_v(1)
            conv(11)
            dve.wait_ge(rows_ready, 2 * H)
            for c in range(NC):
                for h in range(H):
                    i = nc.vector.tensor_scalar(AT[:, c, h, :], GR[:, h, c * P:(c + 1) * P], gT[:, c, h:h + 1], 0.0,
                                                ALU.subtract, ALU.min)
                i.then_inc(dt_args, 1)
                if c == 1:
                    scaled_v(2)
                if c == 2:
                    scaled_v(3)

            def over_heads(m):
                return m.unsqueeze(1).to_broadcast([P, H, P])

            for c in range(NC):
                dve.wait_ge(dt_exp, c + 1)
                link(nc.vector.tensor_tensor(AT[:, c], AT[:, c], over_heads(cst[:, C_UP:C_UP + P]), ALU.mult))
                dve.wait_ge(gram_ps, c + 1)
                link(nc.vector.tensor_tensor(U[:, c], auxh[2 * (c % 2)][:, :, :], AT[:, c], ALU.mult))
                nc.vector.tensor_tensor(U[:, c], U[:, c], BR[:, :, c * P:(c + 1) * P], ALU.mult)
                nc.vector.tensor_tensor(AT[:, c], auxh[2 * (c % 2) + 1][:, :, :], AT[:, c], ALU.mult).then_inc(
                    at_ready, 1)
            dve.wait_ge(at_ready, NC)

            def ch_tile(t):
                ps = tile("ch", t)
                freed(nc.vector.tensor_copy(cin[:, t, 2:2 + T], ps))

            def cc_tile(t):
                ps = tile("cc", t)
                evacuated(dve, "ch", t)
                freed(nc.vector.tensor_tensor(cin[:, t, 2:2 + T], ps, cin[:, t, 2:2 + T], ALU.mult))

            def cb_tile(t):
                evacuated(dve, "cc", t)
                d = convd[:, t, :]
                link(nc.vector.tensor_scalar(d, cin[:, t, 2:2 + T], g_of("sconv_w", 4 + t), None, ALU.mult))
                for tap in (1, 0):
                    link(nc.vector.scalar_tensor_tensor(d, cin[:, t, tap:tap + T], g_of("sconv_w", 2 * tap + t), d,
                                                        ALU.mult, ALU.add))
                ps = tile("cb", t)
                freed(nc.vector.tensor_tensor(d, ps, d, ALU.mult))

            ch_tile(0)
            ch_tile(1)
            for h in range(H):
                dve.wait_ge(gr_exp, h + 1)
                nc.vector.tensor_tensor(qg[:, h, :], qT[:, h, :], GR[:, h, :], ALU.mult).then_inc(qg_ready, 1)
            fills = {(0, 1): (cc_tile, 0), (0, 3): (cc_tile, 1), (0, 5): (cb_tile, 0), (1, 1): (cb_tile, 1)}
            for pair in range(2):
                for lev in range(LEVELS):
                    m0 = (INV_PAIR - 2) * pair + 2 * (lev - 1)
                    n0 = INV_PAIR * pair + 2 * lev
                    mask = over_heads(cst[:, C_LEV + lev * P:C_LEV + (lev + 1) * P])
                    if lev == 0:
                        if pair:
                            dve.wait_ge(p_ps, INV_PAIR - 2)
                        for e in range(2):
                            nc.vector.tensor_tensor(UM[:, e], U[:, 2 * pair + e], mask, ALU.mult).then_inc(um_ready, 1)
                            dve.wait_ge(um_ready, n0 + e + 1)
                            nc.vector.tensor_tensor(Y[:, 2 * pair + e], over_heads(ident), UM[:, e], ALU.subtract)
                    if lev == 0:
                        for e in range(2):
                            dve.wait_ge(xy_ps, n0 + e + 1)
                            nc.vector.tensor_tensor(X[:, e], over_heads(ident), auxh[2 * e + 1][:, :, :],
                                                    ALU.subtract).then_inc(xy_ready, 1)
                        nxt = over_heads(cst[:, C_LEV + P:C_LEV + 2 * P])
                        for e in range(2):
                            dve.wait_ge(xy_ready, n0 + e + 1)
                            nc.vector.tensor_tensor(UM[:, e], U[:, 2 * pair + e], nxt, ALU.mult).then_inc(um_ready, 1)
                        continue
                    if lev < LEVELS - 1:
                        nxt = over_heads(cst[:, C_LEV + (lev + 1) * P:C_LEV + (lev + 2) * P])
                        for e in range(2):
                            dve.wait_ge(p_ps, m0 + e + 1)
                            nc.vector.tensor_tensor(UM[:, e], U[:, 2 * pair + e], nxt, ALU.mult).then_inc(um_ready, 1)
                    if (pair, lev) in fills:
                        f, a = fills[pair, lev]
                        f(a)
                    for e in range(2):
                        c = 2 * pair + e
                        dve.wait_ge(xy_ready, n0 + e - 1)
                        dve.wait_ge(xy_ps, n0 + e + 1)
                        if lev < LEVELS - 1:
                            nc.vector.tensor_tensor(X[:, e], X[:, e], auxh[2 * e + 1][:, :, :], ALU.subtract)
                        nc.vector.tensor_tensor(Y[:, c], Y[:, c], auxh[2 * e][:, :, :], ALU.subtract).then_inc(
                            xy_ready, 1)

            for c in range(NC):
                if c > 0:
                    dve.wait_ge(ks_ps, c)
                    link(nc.vector.tensor_tensor(t1[:, :, :], auxh[0][:, :, :],
                                                 eg[:, 0, c, :].unsqueeze(2).to_broadcast([P, H, P]), ALU.mult))
                    nc.vector.tensor_tensor(rr[:, :, :], bv[:, c], t1[:, :, :], ALU.subtract).then_inc(rr_ready, 1)
                if c < NC - 1:
                    dve.wait_ge(su_ps, c + 1)
                    if c == 0:
                        nc.vector.tensor_copy(S[:, :, :], auxh[3][:, :, :]).then_inc(s_ready, 1)
                        continue
                    dve.wait_ge(o_ps, c + 1)
                    link(nc.vector.tensor_tensor(S[:, :, :], S[:, :, :],
                                                 eg[:, 2, c, :].unsqueeze(2).to_broadcast([P, H, P]), ALU.mult))
                    nc.vector.tensor_tensor(S[:, :, :], auxh[3][:, :, :], S[:, :, :], ALU.add).then_inc(s_ready, 1)
            for i in range(2):
                dve.wait_ge(pool_ps, i + 1)
                nc.vector.tensor_scalar(h32[:, i, :], aux[i][:, :], g_of("pool_scale", i), None, ALU.mult).then_inc(
                    h32_ready, 1)
            for i in range(2):
                lower(F_MIX1, i, MIX1_ORDER[i], h32[:, i, :])
            for i in range(2):
                lower(F_MIX1, 2 + i, MIX1_ORDER[2 + i], convd[:, i, :])
            for h in range(H):
                dve.wait_ge(orn_ready, h + 1)
                o = oT[:, h, :]
                link(nc.vector.scalar_tensor_tensor(o, o, g_of("onorm_g", 0), orn[h % 2][:, :], ALU.mult, ALU.mult))
                evacuated(dve, "z", h)
                nc.vector.tensor_tensor(h32[:, (2 + h) % 3, :], o, zs[:, h, :], ALU.mult).then_inc(h32_ready, 1)
                if h > 0:
                    lower(F_MIX1, 3 + h, h - 1, h32[:, (1 + h) % 3, :])
            lower(F_MIX1, 7, 3, h32[:, 5 % 3, :])
            for m in range(KD):
                ps = tile("wout", m)
                freed(nc.vector.tensor_tensor(x[:, m, :], ps, x[:, m, :], ALU.add))
            vector_rest(dve, link, tile, freed, lower, norm_fill)


INPUTS = ["x", "p", "norm1_g", "w_in", "conv_qkv", "a_log", "dt_bias", "onorm_g", "pool_w", "pool_scale", "sconv_w",
          "w_out", "norm2_g", "w_gate", "w_up", "w_down", "ple_proj", "ple_gate", "final_g", "positions_2",
          "norm_pre_mix_2", "w_in_2", "b_gates_2", "conv_w_2", "conv_b_2", "ml_head_norm_2", "q_norm_2", "w_uq_2",
          "kv_norm_2", "w_ukv_2", "w_out_2", "norm_post_mix_2", "norm_pre_mlp_2", "w_up_2", "w_down_2",
          "norm_post_mlp_2"]


def kernel(**inputs):
    import concourse.bacc as bacc
    from concourse.bass_utils import run_bass_kernel_spmd

    nc = bacc.Bacc("TRN2", target_bir_lowering=False, num_devices=1)
    arrays, aps = {}, {}
    for name in INPUTS:
        a = np.ascontiguousarray(inputs[name])
        arrays[f"in_{name}"] = a
        aps[name] = nc.dram_tensor(f"in_{name}", a.shape, mybir.dt.from_np(a.dtype), kind="ExternalInput").ap()
    arrays["constants"] = constant_table()
    aps["constants"] = nc.dram_tensor("constants", (P, NCST), F32, kind="ExternalInput").ap()
    out = nc.dram_tensor("out", (1, T, D), F32, kind="ExternalOutput").ap()
    build(nc, aps, out)
    r = run_bass_kernel_spmd(nc, [arrays], core_ids=[0])
    return r.results[0]["out"]
```

```python
from contextlib import ExitStack

import numpy as np

import concourse.bass as bass
from concourse import mybir

F32 = mybir.dt.float32
BF16 = mybir.dt.bfloat16
F32R = mybir.dt.float32r
I32 = mybir.dt.int32
ALU = mybir.AluOpType
ACT = mybir.ActivationFunctionType
AX_X = mybir.AxisListType.X

P = 128
T = 512
D = 1024
KD = D // P
NC = T // P
EPS = 1e-6
H = 4
FF1 = 2816
FF2 = 4096
W_IN1, W_IN2 = 3080, 1960
MLA_H, NOPE, ROPE, MLA_V = 8, 64, 32, 64
QR, KVR = 256, 128
LN_EXP_TABLES = 6
NBANK = 4
NAUX = 4
RAW, SPLIT = 3, 3
TRI = P * (NC * (NC + 1) // 2)
WB = 1024

PARAMS = [("norm1_g", 8), ("norm2_g", 8), ("final_g", 8), ("conv_qkv", 48), ("onorm_g", 1), ("pool_scale", 2),
          ("sconv_w", 6), ("norm_pre_mix_2", 8), ("norm_post_mix_2", 8), ("norm_pre_mlp_2", 8),
          ("norm_post_mlp_2", 8), ("conv_w_2", 16), ("conv_b_2", 4), ("ml_head_norm_2", 4), ("q_norm_2", 2),
          ("kv_norm_2", 1)]
PCOL = {}
for _name, _rows in PARAMS:
    PCOL[_name] = sum(r for n, r in PARAMS[:len(PCOL)])
NPARAM = sum(r for _, r in PARAMS)
PSPLIT = PCOL["norm_pre_mix_2"]

LEVELS = 7
C_ID = 0
C_UP = C_ID + P
C_LEV = C_UP + P
C_NEG = C_LEV + LEVELS * P
C_INV = C_NEG + P
C_SGN = C_INV + 1
C_CNT = C_SGN + 1
NCST = C_CNT + 32


def constant_table():
    c = np.zeros((P, NCST), np.float32)
    r, q = np.arange(P)[:, None], np.arange(P)[None, :]
    c[:, C_ID:C_ID + P] = r == q
    c[:, C_UP:C_UP + P] = q >= r
    for n in range(LEVELS):
        m = 1 << n
        c[:, C_LEV + n * P:C_LEV + (n + 1) * P] = (r // (2 * m) == q // (2 * m)) & (r // m % 2 == 0) & (q // m % 2 == 1)
    c[:, C_NEG:C_NEG + P] = np.where(q > r, -1e30, 0.0)
    half = ROPE // 2
    inv = 1.0 / (np.float32(10000.0) ** (np.arange(0, ROPE, 2, dtype=np.float32) / np.float32(ROPE)))
    c[:, C_INV] = inv.astype(np.float32)[np.arange(P) % half]
    c[:, C_SGN] = np.where(np.arange(P) % ROPE < half, -1.0, 1.0)
    for t in range(2):
        win = np.where(np.arange(P) < 64, (2, 8)[t], (4, 16)[t])[:, None]
        c[:, C_CNT + 16 * t:C_CNT + 16 * t + 16] = 1.0 / np.minimum(np.arange(1, 17)[None, :], win)
    return c


def plan():
    blocks, tiles = [], []

    def add(kind, idx, what, nk, cols):
        blocks.append(what)
        for j in range(cols // P):
            tiles.append((kind, idx + j, len(blocks) - 1, j * P, nk, cols))

    def wide(kind, weight, col, n, row=0, nk=KD):
        for j in range(n):
            add(kind, j, ("mat", weight, row, nk, col + j * P, P), nk, P)

    wide("ab", "w_in", 2048, 1)
    wide("k", "w_in", 512, 4)
    wide("q", "w_in", 0, 4)
    wide("v", "w_in", 1024, 4)
    wide("hp", "w_in", 2056, 2)
    wide("ch", "w_in", 2824, 2)
    wide("cc", "w_in", 2568, 2)
    wide("cb", "w_in", 2312, 2)
    wide("z", "w_in", 1536, 4)
    wide("wout", "w_out", 0, 8)

    def mlp(widths, up, down):
        rows = [0]
        for w in widths:
            rows.append(rows[-1] + w)
        n = len(widths)
        for c in range(n + 1):
            if c < n:
                for j in range(widths[c]):
                    up(c, rows[c], j)
            if c > 0:
                down(c - 1, rows[c - 1], widths[c - 1])

    def up1(c, row, j):
        blocks.append(("mat", "w_gate", 0, KD, (row + j) * P, P))
        tiles.append(("gate", (c, j), len(blocks) - 1, 0, KD, P))
        blocks.append(("mat", "w_up", 0, KD, (row + j) * P, P))
        tiles.append(("up", (c, j), len(blocks) - 1, 0, KD, P))

    def down1(c, row, w):
        for m in range(KD):
            blocks.append(("mat", "w_down", row * P, w, m * P, P))
            tiles.append(("down", (c, m), len(blocks) - 1, 0, w, P))

    for j in range(2):
        add("proj", 4 * j, ("mat", "ple_proj", 0, 2, j * T, T), 2, T)
    mlp(MLP1, up1, down1)
    wide("pgate", "ple_gate", 0, 8)

    wide("gates2", "w_in_2", 1536, 1)
    wide("qk2", "w_in_2", 0, 3)
    for pair in range(2):
        if pair == 1:
            add("qk2", 3, ("mat", "w_in_2", 0, KD, 3 * P, P), KD, P)
        blocks.append(("mat", "w_in_2", 0, 4, 512 + pair * 256, 256))
        blocks.append(("mat", "w_in_2", 4 * P, 4, 512 + pair * 256, 256))
        for c in range(NC):
            tiles.append(("v2", (pair, c), len(blocks) - 1, 0, KD, 256))
    for kind, j, col in (("o2", 0, 1024), ("cq2", 0, 1544), ("cq2", 1, 1672), ("ckv2", 0, 1800), ("o2", 1, 1152),
                         ("kr2", 0, None), ("o2", 2, 1280), ("o2", 3, 1408)):
        add(kind, j, ("mat", "w_in_2", 0, KD, col, P) if col else ("krope",), KD, P)
    for j in range(2):
        add("uq2", 4 * j, ("uq", j), 2, T)
    blocks.append(("ukv",))
    for j in range(4):
        tiles.append(("uk2", j, len(blocks) - 1, j * P, 1, T))
    for c in range(NC):
        tiles.append(("uv2", c, len(blocks) - 1, T, 1, T))
    wide("wout2", "w_out_2", 0, 8)

    def up2(c, row, j):
        blocks.append(("mat", "w_up_2", 0, KD, (row + j) * P, P))
        tiles.append(("up2", (c, j), len(blocks) - 1, 0, KD, P))

    def down2(c, row, w):
        for m in range(KD):
            blocks.append(("mat", "w_down_2", row * P, w, m * P, P))
            tiles.append(("down2", (c, m), len(blocks) - 1, 0, w, P))

    mlp(MLP2, up2, down2)
    return blocks, tiles


MLP1 = (8, 8, 6)
MLP2 = (8, 8, 8, 8)


class Plan:

    READER = dict(ab="dve", k="act", q="act", v="act", hp="act", ch="dve", cc="dve", cb="dve", z="act", wout="dve",
                  gate="act", up="dve", down="dve", proj="act", pgate="act", gates2="dve", qk2="act", v2="act",
                  cq2="act", ckv2="act", kr2="dve", o2="act", uq2="dve", uk2="act", uv2="dve", wout2="dve",
                  up2="act", down2="dve")

    def __init__(self):
        self.blocks, self.tiles = plan()
        self.at = {(k, i): t for t, (k, i, *_) in enumerate(self.tiles)}
        self.last = [None] * len(self.blocks)
        for t, tile in enumerate(self.tiles):
            self.last[tile[2]] = t
        for b in range(len(self.blocks) - 2, -1, -1):
            if self.last[b] is None:
                self.last[b] = self.last[b + 1]
        self.read, n = [], {"act": 0, "dve": 0}
        for k, *_ in self.tiles:
            n[self.READER[k]] += 1
            self.read.append((self.READER[k], n[self.READER[k]]))

    def done(self, kind, idx):
        return self.at[kind, idx] + 1


def build(nc, ins, out):
    pl = Plan()
    with ExitStack() as ctx:
        def signal(name):
            return ctx.enter_context(nc.semaphore(name))

        base = (nc.sbuf_base + 31) // 32 * 32
        top = [base]

        def sb(name, shape, dt=F32, at=None):
            size = 4
            for n in shape[1:]:
                size *= n
            if at is None:
                at = top[0]
                top[0] += (size + 31) // 32 * 32
            assert at + size <= nc.sbuf_usable_end, (name, at + size - nc.sbuf_usable_end)
            h = nc.alloc_sbuf_tensor_at(name, shape, dt, offset=at)
            offs[name] = at
            return h

        offs = {}
        x = sb("x", [P, KD, T])
        ah = sb("ah", [P, KD, T], F32R)
        al = sb("al", [P, KD, T], F32R)
        raw = [sb(f"raw{i}", [P, WB]) for i in range(RAW)]
        wh = [sb(f"wh{i}", [P, WB], F32R) for i in range(SPLIT)]
        wl = [sb(f"wl{i}", [P, WB], F32R) for i in range(SPLIT)]
        cst = sb("cst", [P, NCST])
        ones = sb("ones", [P, P])
        par = sb("par", [P, NPARAM])
        sq = sb("sq", [P, 2, T])
        h32 = sb("h32", [P, 3, T])
        rstd = sb("rstd", [P, T])
        cols = sb("cols", [P, 8])
        eps = sb("eps", [P, 1])
        eps2 = sb("eps2", [P, 1])
        identr = sb("identr", [P, 64], F32R)
        ident16 = sb("ident16", [P, P], BF16)
        mask16 = sb("mask16", [P, P], BF16)
        rcol = sb("rcol", [P, NC])
        gains = sb("gains", [P, KD])
        free = top[0]

        kT = sb("kT", [P, H, T])
        qT = sb("qT", [P, H, T])
        qg = sb("qg", [P, H, T])
        bv = sb("bv", [P, NC, H, P])
        kd = sb("kd", [P, NC, H, P])
        AT = sb("AT", [P, NC, H, P])
        U = sb("U", [P, NC, H, P])
        Y = sb("Y", [P, NC, H, P])
        GR = sb("GR", [P, H, T])
        BR = sb("BR", [P, H, T])
        X = sb("X", [P, 2, H, P])
        PS = sb("PS", [P, 2, H, P])
        UM = sb("UM", [P, 2, H, P])
        top[0] += 64
        pin = sb("pin", [P, 2, 16 + T])
        cin = sb("cin", [P, 2, 2 + T])
        gT = sb("gT", [P, NC, 16])
        eg = sb("eg", [P, 4, NC, H])
        xtok = sb("xtok", [P, NC, D], at=offs["U"])
        prow = sb("prow", [P, 2, P], at=offs["pin"])
        craw = [sb(f"craw{i}", [P, 3 + T], at=offs["X"] + i * 2080) for i in range(2)]
        cc = [sb(f"cc{i}", [P, T], at=offs["X"] + 2 * 2080 + i * 2048) for i in range(2)]
        vT = [sb(f"vT{i}", [P, T], at=offs["X"] + 2 * 2080 + 4096 + i * 2048) for i in range(2)]
        gab = sb("gab", [8, T], at=offs["AT"])
        gsp = sb("gsp", [8, T], at=offs["AT"] + 2048)
        gcs = sb("gcs", [8, T], at=offs["AT"] + 4096)
        gbt = sb("gbt", [8, T], at=offs["AT"] + 6144)
        gch = sb("gch", [8, T], F32R, at=offs["U"])
        gcl = sb("gcl", [8, T], F32R, at=offs["U"] + 2048)
        gbh = sb("gbh", [8, T], F32R, at=offs["U"] + 4096)
        gbl = sb("gbl", [8, T], F32R, at=offs["U"] + 6144)
        hsq = sb("hsq", [P, H, T], at=offs["AT"])
        oT = sb("oT", [P, H, T], at=offs["qT"])
        ptmp = sb("ptmp", [P, 2, 16 + T], at=offs["qT"])
        zs = sb("zs", [P, H, T], at=offs["GR"])
        pooled = sb("pooled", [P, 2, T], at=offs["BR"])
        convd = sb("convd", [P, 2, T], at=offs["BR"] + 4096)
        orn = [sb(f"orn{i}", [P, T], at=offs["PS"] + 2048 * i) for i in range(2)]
        S = [sb("S0", [P, H, P], at=offs["X"]), sb("S1", [P, H, P], at=offs["UM"])]
        vn = sb("vn", [P, H, P], at=offs["X"] + 2048)
        rr = sb("rr", [P, H, P], at=offs["PS"])
        t1 = sb("t1", [P, H, P], at=offs["PS"] + 2048)
        bw = sb("bw", [P, 2, P])

        top[0] = free
        yh = [sb(f"yh{i}", [P, KD, T], F32R) for i in range(2)]
        yl = [sb(f"yl{i}", [P, KD, T], F32R) for i in range(2)]
        sg = sb("sg", [P, 3, T])
        y32 = sb("y32", [P, 2, T])
        hid_top = top[0]
        ptok = sb("ptok", [P, NC, 2 * P])
        ph = sb("ph", [P, 2, T], F32R)
        plo = sb("plo", [P, 2, T], F32R)
        pp = sb("pp", [P, KD, T])

        acc = sb("acc", [P, KD, T], at=hid_top)
        rl = sb("rl", [P, T], at=offs["sg"])
        xtok2 = sb("xtok2", [P, NC, D], at=offs["yh0"])
        atok = sb("atok", [P, NC, D], at=offs["yl0"])

        top[0] = free
        q2 = sb("q2", [P, 2, T])
        k2 = sb("k2", [P, 2, T])
        v2 = sb("v2", [P, NC, T])
        og = sb("og", [P, H, T])
        wt = sb("wt", [P, TRI])
        st = sb("st", [P, 2, T])
        hm = sb("hm", [P, T])
        dn = sb("dn", [P, T])
        r4h = sb("r4h", [P, T], F32R)
        r4l = sb("r4l", [P, T], F32R)
        cT = sb("cT", [P, NC, H])
        trig = sb("trig", [P, 2, T])
        krr = sb("krr", [P, T])
        rtmp = sb("rtmp", [P, T])
        cqh = sb("cqh", [P, 2, T], F32R)
        cql = sb("cql", [P, 2, T], F32R)
        ckh = sb("ckh", [P, 1, T], F32R)
        ckl = sb("ckl", [P, 1, T], F32R)
        am = sb("am", [P, 3, MLA_H * NC])
        qf = sb("qf", [P, MLA_H, T])
        kf = sb("kf", [P, MLA_H, T])
        vt2 = sb("vt2", [P, NC, T])
        craw2 = [sb(f"craw2{i}", [P, 3 + T], at=offs["qf"] + i * 2080) for i in range(2)]
        cc2 = [sb(f"cc2{i}", [P, T], at=offs["qf"] + 4160 + i * 2048) for i in range(2)]
        posi = sb("posi", [P, T], I32, at=offs["qf"] + 8256)
        ang = sb("ang", [P, T], at=offs["qf"] + 10304)
        turn = sb("turn", [P, T], at=offs["qf"] + 12352)
        g2 = sb("g2", [2 * H, T], at=offs["kf"])
        lf = sb("lf", [2 * H, T], at=offs["kf"] + 2048)
        bs = sb("bs", [2 * H, T], at=offs["kf"] + 4096)
        nbs = sb("nbs", [2 * H, T], at=offs["kf"] + 6144)
        c4 = sb("c4", [H, T], at=offs["kf"] + 8192)
        m4 = sb("m4", [H, T], at=offs["kf"] + 10240)
        em4 = sb("em4", [32 + H, T], at=offs["kf"] + 12288)
        cq = sb("cq", [P, 3, T], at=offs["vt2"])
        pm = sb("pm", [P, 3, T], at=offs["trig"])
        pT = sb("pT", [P, 2, NC, T], at=free)

        bank = [ctx.enter_context(nc.psum_tensor(f"bank{i}", [P, T], F32)) for i in range(NBANK)]
        aux = [ctx.enter_context(nc.psum_tensor(f"aux{i}", [P, T], F32)) for i in range(NAUX)]
        auxh = [a[:, :].rearrange("p (h n) -> p h n", h=4) for a in aux]

        tb, pv = [bank[3], aux[1]], [aux[3], aux[2]]

        ident = cst[:, C_ID:C_ID + P]

        def g_of(name, k):
            return par[:, PCOL[name] + k:PCOL[name] + k + 1]

        x_loaded = [signal(f"x_loaded{c}") for c in range(NC)]
        ident_loaded = signal("ident_loaded")
        gain_loaded = signal("gain_loaded")
        consts_loaded = signal("consts_loaded")
        raw_loaded = [signal(f"raw_loaded{i}") for i in range(RAW)]
        out_stored = signal("out_stored")
        wh_ready = signal("wh_ready")
        wl_ready = signal("wl_ready")
        gemm_done = signal("gemm_done")
        bank_read = {"act": signal("bank_read_act"), "dve": signal("bank_read_dve")}
        ones_set = signal("ones_set")
        par_ps = signal("par_ps")
        par_ready = signal("par_ready")
        xt_ps = signal("xt_ps")
        x_ready = signal("x_ready")
        sq_ready = signal("sq_ready")
        ssq_done = signal("ssq_done")
        rstd_ready = signal("rstd_ready")
        sum_ready = signal("sum_ready")
        fsq_ready = signal("fsq_ready")
        fsum_ready = signal("fsum_ready")
        fssq_done = signal("fssq_done")
        h32_ready = signal("h32_ready")
        ah_ready = signal("ah_ready")
        al_ready = signal("al_ready")
        act_step = signal("act_step")
        dve_step = signal("dve_step")
        pool_step = signal("pool_step")

        def landed(b):
            return 16 * sum(len(parts(n)) for n in range(b % RAW, b + 1, RAW))

        def parts(b):
            what, dst = pl.blocks[b], raw[b % RAW]
            if what[0] == "mat":
                _, name, row, nk, col, w = what
                src = ins[name][0, row:row + nk * P, col:col + w].rearrange("(k p) n -> p k n", p=P)
                return [(dst[:, 0:nk * w].rearrange("p (k n) -> p k n", n=w), src)]
            if what[0] == "krope":
                w = ins["w_in_2"][0].rearrange("(k p) n -> p k n", p=P)
                d = dst[:, 0:WB].rearrange("p (k n) -> p k n", n=P)
                end = W_IN2
                return [(d[:, :, 0:96], w[:, :, end - 96:end]), (d[:, :, 96:112], w[:, :, end - 16:end]),
                        (d[:, :, 112:128], w[:, :, end - 32:end - 16])]
            if what[0] == "uq":
                res = []
                for k in range(2):
                    w = ins["w_uq_2"][0, k * P:(k + 1) * P, what[1] * 384:(what[1] + 1) * 384].rearrange(
                        "p (h n) -> p h n", n=NOPE + ROPE)
                    d = dst[:, k * T:(k + 1) * T].rearrange("p (h n) -> p h n", n=P)
                    res += [(d[:, :, 0:96], w), (d[:, :, 96:112], w[:, :, 80:96]), (d[:, :, 112:128], w[:, :, 64:80])]
                return res
            w = ins["w_ukv_2"][0].rearrange("p (h n) -> p h n", n=NOPE + MLA_V)
            return [(dst[:, i * T:(i + 1) * T].rearrange("p (h n) -> p h n", n=64), w[:, :, 64 * i:64 * i + 64])
                    for i in range(2)]

        softplus_ready = signal("softplus_ready")
        decay_sums_ready = signal("decay_sums_ready")
        log_beta_ready = signal("log_beta_ready")
        beta_ready = signal("beta_ready")
        rows_split = signal("rows_split")
        rows_ps = signal("rows_ps")
        rows_ready = signal("rows_ready")
        gt_ps = signal("gt_ps")
        gt_ready = signal("gt_ready")
        eg_args = signal("eg_args")
        eg_exps = signal("eg_exps")
        conv_done = signal("conv_done")
        silu_ready = signal("silu_ready")
        head_sq = signal("head_sq")
        head_ss = signal("head_ss")
        head_rn = signal("head_rn")
        head_normed = signal("head_normed")
        kt_ps = signal("kt_ps")
        kd_ready = signal("kd_ready")
        vt_ps = signal("vt_ps")
        bv_ready = signal("bv_ready")
        gr_exp = signal("gr_exp")
        qg_ready = signal("qg_ready")
        dt_args = signal("dt_args")
        dt_exp = signal("dt_exp")
        gram_ps = signal("gram_ps")
        at_ready = signal("at_ready")
        um_ready = signal("um_ready")
        p_ps = signal("p_ps")
        p_ready = signal("p_ready")
        xy_ps = signal("xy_ps")
        xy_ready = signal("xy_ready")
        ks_ps = signal("ks_ps")
        rr_ready = signal("rr_ready")
        vn_ps = signal("vn_ps")
        vn_ready = signal("vn_ready")
        su_ps = signal("su_ps")
        s_ready = signal("s_ready")
        o_ps = signal("o_ps")
        o_ready = signal("o_ready")
        pooled_ready = signal("pooled_ready")
        pool_ps = signal("pool_ps")
        bw_zero = signal("bw_zero")
        bw_loaded = signal("bw_loaded")
        osq_ready = signal("osq_ready")
        oss_ps = signal("oss_ps")
        orn_ready = signal("orn_ready")
        cols_zero = signal("cols_zero")
        cols_loaded = signal("cols_loaded")
        eps_set = signal("eps_set")
        pads_zero = signal("pads_zero")
        alog_exp = signal("alog_exp")
        y_ready = [signal("y_ready_1"), signal("y_ready_2")]
        ph_ready = signal("ph_ready")
        x_gated = signal("x_gated")
        r3_arg = signal("r3_arg")
        x_mixed = signal("x_mixed")
        ptok_loaded = signal("ptok_loaded")
        pt_ps = signal("pt_ps")
        pt_ready = signal("pt_ready")

        pads2_zero = signal("pads2_zero")
        pos_loaded = signal("pos_loaded")
        rope_args = signal("rope_args")
        trig_ready = signal("trig_ready")
        logf_ready = signal("logf_ready")
        forget_sums_ready = signal("forget_sums_ready")
        cb_ps = signal("cb_ps")
        c4_ready = signal("c4_ready")
        ct_ps = signal("ct_ps")
        ct_ready = signal("ct_ready")
        maxima_split = signal("maxima_split")
        floor_split = signal("floor_split")
        em_sums = signal("em_sums")
        em_args = signal("em_args")
        em_ready = signal("em_ready")
        conv2_done = signal("conv2_done")
        silu2_ready = signal("silu2_ready")
        lat_sq = signal("lat_sq")
        lat_ss = signal("lat_ss")
        lat_rn = signal("lat_rn")
        cq_ready = signal("cq_ready")
        kr_ready = signal("kr_ready")
        og_ready = signal("og_ready")
        kf_ready = signal("kf_ready")
        mrow_ps = signal("mrow_ps")
        wt_ready = signal("wt_ready")
        ms_ps = signal("ms_ps")
        s_done = signal("s_done")
        nd_ps = signal("nd_ps")
        hm_ready = signal("hm_ready")
        erow_ready = signal("erow_ready")
        erow_ps = signal("erow_ps")
        dn_ready = signal("dn_ready")
        ml_sq = signal("ml_sq")
        ml_sum = signal("ml_sum")
        ml_ss = signal("ml_ss")
        ml_rn = signal("ml_rn")
        as_ps = signal("as_ps")
        max_ready = signal("max_ready")
        prob_ready = signal("prob_ready")
        mask_ready = signal("mask_ready")
        prob_scaled = signal("prob_scaled")
        at_ps = signal("at_ps")
        pt_evac = signal("pt_evac")
        pv_ps = signal("pv_ps")
        relu_sq = signal("relu_sq")
        acc_gained = signal("acc_gained")
        at_turned = signal("at_turned")
        at_evac = signal("at_evac")
        xt_turned = signal("xt_turned")
        xt_evac = signal("xt_evac")
        out_ready = signal("out_ready")
        SPLIT_AT = [2 * NC * (t + 1) + 1 for t in range(3)]
        ATT_SCALE = float(NOPE + ROPE) ** -0.5
        FLOOR_MIN = -41.0
        TWO_PI = 6.283185307179586
        TURN_PARTS = (6.28125, 0.00193500518798828125, TWO_PI - 6.28125 - 0.00193500518798828125)
        PI_BELOW = 3.1415925
        ROUND = 12582912.0

        F_NORM1, F_MIX1, F_NORM2, F_PLE, F_NORM3, F_MIX2, F_NORM5 = range(7)
        H32_BASE = {F_NORM1: 0, F_MIX1: 8, F_NORM2: 14, F_NORM3: 22}
        H32_BASE[F_MIX2] = 30
        H32_BASE[F_NORM5] = 30 + 4
        LAST_USE = {F_NORM1: pl.done("z", 3), F_MIX1: pl.done("wout", 7), F_NORM2: pl.done("up", (2, 5)),
                    F_PLE: pl.done("pgate", 7), F_NORM3: pl.done("o2", 3), F_MIX2: pl.done("wout2", 7),
                    F_NORM5: pl.done("up2", (3, 7))}
        thirds = [(f"proj{i}", kind, j) for kind, j in (("o2", 0), ("cq2", 0), ("cq2", 1), ("ckv2", 0), ("o2", 1),
                                                        ("kr2", 0), ("o2", 2), ("o2", 3)) for i in range(3)]
        fillers = thirds + [("uq2", j, 0) for j in range(MLA_H)] + [("uk2", 0, 0), ("uv2", 0, 0)]
        MIX2_STEPS, kept = [], []
        for h in range(H):
            for s in range(7):
                MIX2_STEPS.append(("mlstm", h, s))
                if s == 6:
                    kept.append(h)
                if (h, s) == (1, 5):
                    MIX2_STEPS.append(("latent_norms", 0, 0))
                for _ in range((2, 1, 1, 1, 2, 2, 0)[s]):
                    if fillers:
                        MIX2_STEPS.append(fillers.pop(0))
                if (h, s) == (3, 4):
                    MIX2_STEPS.append(("attention_start", 0, 0))
                if len(fillers) <= 10:
                    MIX2_STEPS += [("fill", g, 0) for g in kept]
                    kept = []
        assert not fillers and not kept
        WT = [sum(T - m * P for m in range(j)) for j in range(NC)]
        INV_FILL = {}
        for i, at in enumerate((pair, lev) for pair in range(2) for lev in range(1, LEVELS)):
            INV_FILL[at] = (("cc", 0), ("cc", 1), ("cb", 0), ("cb", 1))[i // 3], i % 3
        MIX1_ORDER = [4, 5, 6, 7, 0, 1, 2, 3]
        HEADS = [("k", h) for h in range(H)] + [("q", h) for h in range(H)] + [("v", h) for h in range(H)]
        INV_PAIR = 2 * LEVELS

        SQ_BASE = {0: 0, 1: KD, 2: 2 * KD, 4: 3 * KD, 5: 4 * KD, 6: 5 * KD}
        SSQ_BASE = {0: 0, 1: 1, 2: 4, 4: 7, 5: 10, 6: 10 + KD}
        SSQ_END = {0: 1, 1: 4, 2: 7, 4: 10, 5: 10 + KD, 6: 11 + KD}
        SUM_BASE = {0: 0, 1: 7, 2: 12, 4: 17, 6: 22}
        RSTD_FREE = {1: (h32_ready, 8), 2: (h32_ready, H32_BASE[F_NORM2] + KD),
                     4: (h32_ready, H32_BASE[F_MIX2] + H), 5: (x_mixed, KD),
                     6: (h32_ready, H32_BASE[F_NORM5] + KD)}

        def when_read(kind, idx):
            eng, n = pl.read[pl.at[kind, idx]]
            return bank_read[eng], n

        def evacuated(eng, kind, idx):
            eng.wait_ge(*when_read(kind, idx))

        def conv_tile(j):
            kind, h = HEADS[j]
            return {"q": 0, "k": 4, "v": 8}[kind] + h

        def block_cols(b):
            what = pl.blocks[b]
            return what[3] * what[5] if what[0] == "mat" else WB

        def split_before(step):
            done = pl.at["v2", (1, NC - 1)]
            for kind, i, s in MIX2_STEPS[:MIX2_STEPS.index(step)]:
                if kind == "proj2":
                    done = pl.at[i, s]
                elif kind in ("uq2", "uk2", "uv2"):
                    done = pl.at[kind, i if kind == "uq2" else 3]
            return max(b for b in range(len(pl.blocks)) if b < SPLIT or pl.last[b - SPLIT] <= done)

        def multiscale(pool, link):
            for t in range(2):
                evacuated(pool, "hp", t)
                pool.wait_ge(qg_ready, H)
                a, b, n = pin[:, t, :], ptmp[:, 0, :], 16 + T
                c = ptmp[:, 1, :]
                link(nc.gpsimd.tensor_tensor(b[:, 1:n], a[:, 1:n], a[:, 0:n - 1], ALU.add))
                if t == 0:
                    link(nc.gpsimd.tensor_copy(c[0:64, 16:n], b[0:64, 16:n]))
                    link(nc.gpsimd.tensor_tensor(c[64:P, 3:n], b[64:P, 3:n], b[64:P, 1:n - 2], ALU.add))
                    s = c
                else:
                    link(nc.gpsimd.tensor_tensor(c[:, 3:n], b[:, 3:n], b[:, 1:n - 2], ALU.add))
                    link(nc.gpsimd.tensor_tensor(b[:, 7:n], c[:, 7:n], c[:, 3:n - 4], ALU.add))
                    link(nc.gpsimd.tensor_copy(c[0:64, 16:n], b[0:64, 16:n]))
                    link(nc.gpsimd.tensor_tensor(c[64:P, 16:n], b[64:P, 16:n], b[64:P, 8:n - 8], ALU.add))
                    s = c
                cnt = cst[:, C_CNT + 16 * t:C_CNT + 16 * t + 16]
                o = pooled[:, t, :]
                pool.wait_ge(at_ready, NC)
                link(nc.gpsimd.tensor_scalar(o[:, 16:T], s[:, 32:n], cnt[:, 15:16], None, ALU.mult))
                link(nc.gpsimd.tensor_tensor(o[:, 0:16], s[:, 16:32], cnt, ALU.mult))
                nc.gpsimd.tensor_tensor(o, o, a[:, 16:n], ALU.subtract).then_inc(pooled_ready, 1)

        def parameters(sp):
            for name, rows in PARAMS:
                second = PCOL[name] >= PSPLIT
                r = PCOL[name] - (PSPLIT if second else 0)
                v = ins[name]
                if len(v.shape) == 3:
                    v = v.rearrange("a b c -> (a b c)")
                elif len(v.shape) == 2:
                    v = v.rearrange("a b -> (a b)")
                sp.dma_start(prow[r:r + rows, int(second), :], v.rearrange("(r c) -> r c", c=P)).then_inc(
                    gain_loaded if name == "norm1_g" else consts_loaded, 16)
            sp.dma_start(cst[:, P:NCST], ins["constants"][:, P:NCST]).then_inc(consts_loaded, 16)
            sp.wait_ge(cols_zero, 1)
            sp.dma_start(cols[0:H, 0:1], ins["dt_bias"].rearrange("a h -> h a")).then_inc(cols_loaded, 16)
            sp.dma_start(cols[0:H, 1:2], ins["a_log"].rearrange("a h -> h a")).then_inc(cols_loaded, 16)
            sp.dma_start(cols[0:2 * H, 3:4], ins["b_gates_2"].rearrange("a h -> h a")).then_inc(cols_loaded, 16)

        def tensor_rest(pe, gemm, gemm_pair, ssq, transpose4, state):
            def mlp(kinds, widths, fill, n, beside_last=None):
                up, down = kinds
                for c in range(len(widths) + 1):
                    if c < len(widths):
                        js = [(kind, (c, j)) for j in range(widths[c]) for kind in up]
                        if c == 0:
                            gemm_pair(js[0], js[1], (al_ready, KD * fill))
                        for kind, j in js[2 if c == 0 else 0:]:
                            gemm(kind, j)
                    if c > 0:
                        before = sum(widths[:c - 1])
                        for m in range(KD):
                            gemm(down, (c - 1, m), mov=(yh[(c - 1) % 2], yl[(c - 1) % 2]),
                                 ready=(y_ready[n], before) if m == 0 else None)
                            if c == len(widths) and beside_last:
                                beside_last(m)

            mlp((("gate", "up"), "down"), MLP1, F_NORM2, 0)
            for m in range(KD):
                if m < KD - 1:
                    gemm("pgate", m, ready=(al_ready, KD * F_PLE) if m == 0 else None)
            gemm("pgate", KD - 1, part=(0, 2))
            ssq(2, early=True)
            pe.wait_ge(fsum_ready, 5)
            nc.tensor.matmul(aux[2][:, :], ones[:, :], h32[:, 0, :], start=True, stop=False)
            pe.wait_ge(fsq_ready, KD - 1)
            nc.tensor.matmul(aux[2][:, :], ones[:, :], h32[:, 1, :], start=False, stop=False).then_inc(fssq_done, 1)
            gemm("pgate", KD - 1, part=(1, 2))
            ssq(2)
            pe.wait_ge(fsq_ready, KD)
            nc.tensor.matmul(aux[2][:, :], ones[:, :], h32[:, 2, :], start=False, stop=True).then_inc(fssq_done, 1)
            tensor_second(pe, gemm, gemm_pair, ssq, transpose4, mlp, state)

        def scalar_rest(act, link, tables, tile, square, norm, upper):
            def norm_upper(n, fill, between=None):
                norm(n)
                for k in range(KD):
                    upper(fill, k, k, h32[:, k % 3, :], (h32_ready, H32_BASE[fill] + k + 1))
                    if between and k < KD - 1:
                        between(k + 1)

            def proj(j):
                tile("proj", j, lambda ps: nc.scalar.copy(pp[:, j, :], ps))

            proj(0)
            norm_upper(1, F_NORM2, between=proj)

            n = [0]

            def gate(c, j):
                slot = n[0] % 3
                if n[0] >= 3:
                    evacuated(act, *hidden[n[0] - 3])
                tile("gate", (c, j), lambda ps: nc.scalar.activation(sg[:, slot, :], ps, ACT.Silu))
                tile("up", (c, j))
                n[0] += 1

            hidden = [("up", (c, j)) for c in range(len(MLP1)) for j in range(MLP1[c])]
            for c in range(len(MLP1) + 1):
                if c < len(MLP1):
                    for j in range(MLP1[c]):
                        gate(c, j)
                if c > 0:
                    for m in range(KD):
                        tile("down", (c - 1, m))
                        if c == len(MLP1) and m > 0:
                            upper(F_PLE, m - 1, m - 1, x[:, m - 1, :], when_read("down", (c - 1, m - 1)))
            upper(F_PLE, KD - 1, KD - 1, x[:, KD - 1, :], when_read("down", (len(MLP1) - 1, KD - 1)))

            def both_squares(k):
                act.wait_ge(x_gated, k + 1)
                square(2, k, x[:, k, :])
                if k >= 3:
                    act.wait_ge(fsum_ready, k - 2)
                dst = h32[:, 1 + k % 2 if k else 0, :]
                nc.scalar.activation(dst, x[:, k, :], ACT.Square, scale=g_of("final_g", k)).then_inc(fsq_ready, 1)

            for m in range(KD):
                if m > 0:
                    both_squares(m - 1)
                tile("pgate", m, lambda ps: nc.scalar.activation(sg[:, m % 3, :], ps, ACT.Sigmoid))
            both_squares(KD - 1)
            tables(LN_EXP_TABLES)
            act.wait_ge(r3_arg, 1)
            link(nc.scalar.activation(sq[:, 0, :], sq[:, 0, :], ACT.Ln, bias=eps2[:, 0:1], scale=1.0 / D))
            nc.scalar.activation(sq[:, 0, :], sq[:, 0, :], ACT.Exp, scale=-0.5).then_inc(rstd_ready, 1)
            act.wait_ge(x_gated, KD)
            act.dma_start(posi[:, :], ins["positions_2"][0:1, :].partition_broadcast(P)).then_inc(pos_loaded, 16)
            for k in range(KD):
                upper(F_NORM3, k, k, h32[:, k % 3, :], (h32_ready, H32_BASE[F_NORM3] + k + 1))
            norm(2)
            scalar_second(act, link, tables, tile, square, norm, upper, norm_upper)

        def vector_rest(dve, link, tile, freed, lower, norm_fill, add_square):
            norm_fill(1, F_NORM2, "norm2_g", 0)
            hidden = [(c, j) for c in range(len(MLP1)) for j in range(MLP1[c])]

            def product(c, j):
                i = hidden.index((c, j))
                ps = tile("up", (c, j))
                if c >= 2 and j == 0:
                    dve.wait_ge(gemm_done, pl.done("down", (c - 2, KD - 1)))
                if i >= 2:
                    dve.wait_ge(y_ready[0], i - 1)
                evacuated(dve, "gate", (c, j))
                y = y32[:, i % 2, :]
                freed(nc.vector.tensor_tensor(y, ps, sg[:, i % 3, :], ALU.mult))
                evacuated(dve, "up", (c, j))
                link(nc.vector.tensor_copy(yh[c % 2][:, j, :], y))
                nc.vector.tensor_tensor(yl[c % 2][:, j, :], y, yh[c % 2][:, j, :].bitcast(F32),
                                        ALU.subtract).then_inc(y_ready[0], 1)

            for c in range(len(MLP1) + 1):
                if c < len(MLP1):
                    for j in range(MLP1[c]):
                        product(c, j)
                if c > 0:
                    for m in range(KD):
                        ps = tile("down", (c - 1, m))
                        if c > 1:
                            evacuated(dve, "down", (c - 2, m))
                        freed(nc.vector.tensor_tensor(x[:, m, :], ps, x[:, m, :], ALU.add))
                        if c == len(MLP1) and m > 1:
                            lower(F_PLE, m - 2, m - 2, x[:, m - 2, :])
            lower(F_PLE, KD - 2, KD - 2, x[:, KD - 2, :])
            lower(F_PLE, KD - 1, KD - 1, x[:, KD - 1, :])
            for m in range(KD):
                evacuated(dve, "pgate", m)
                g = sg[:, m % 3, :]
                link(nc.vector.tensor_tensor(g, g, pp[:, m, :], ALU.mult))
                dve.wait_ge(al_ready, KD * F_PLE + KD)
                nc.vector.tensor_tensor(x[:, m, :], x[:, m, :], g, ALU.add).then_inc(x_gated, 1)
                add_square(2, m - 1)
                if 1 <= m - 1 <= 5:
                    dve.wait_ge(fsq_ready, m)
                    if m > 2:
                        dve.wait_ge(fsum_ready, m - 2)
                    nc.vector.tensor_tensor(h32[:, 0, :], h32[:, 0, :], h32[:, 1 + (m - 1) % 2, :],
                                            ALU.add).then_inc(fsum_ready, 1)
            link(nc.vector.tensor_tensor(gains[:, :], par[:, PCOL["final_g"]:PCOL["final_g"] + KD],
                                         par[:, PCOL["norm_pre_mix_2"]:PCOL["norm_pre_mix_2"] + KD], ALU.mult))
            dve.wait_ge(x_gated, KD)
            dve.wait_ge(fssq_done, 2)
            dve.wait_ge(ssq_done, SSQ_END[2])
            both = sq[:, 0, :]
            link(nc.vector.tensor_scalar(both, aux[3][:, :], EPS, None, ALU.mult))
            nc.vector.tensor_tensor(both, aux[2][:, :], both, ALU.add).then_inc(r3_arg, 1)
            dve.wait_ge(rstd_ready, 3)
            for k in range(KD):
                dve.wait_ge(al_ready, KD * F_NORM3 + max(0, k - 2))
                nc.vector.scalar_tensor_tensor(h32[:, k % 3, :], x[:, k, :], gains[:, k:k + 1], both, ALU.mult,
                                               ALU.mult).then_inc(h32_ready, 1)
                if k > 0:
                    lower(F_NORM3, k - 1, k - 1, h32[:, (k - 1) % 3, :])
            lower(F_NORM3, KD - 1, KD - 1, h32[:, (KD - 1) % 3, :])
            vector_second(dve, link, tile, freed, lower, norm_fill, add_square)

        def tensor_second(pe, gemm, gemm_pair, ssq, transpose4, mlp, state):
            gemm_pair(("gates2", 0), ("qk2", 0), (al_ready, KD * F_NORM3))
            gemm("qk2", 1)
            gemm("qk2", 2)
            pe.wait_ge(forget_sums_ready, 1)
            pe.wait_ge(rstd_ready, 4)
            nc.tensor.matmul(aux[0][0:H, :], ident[0:8, 0:H], g2[:, :], start=True, stop=False)
            nc.tensor.matmul(aux[0][0:H, :], ident[0:8, H:2 * H], nbs[:, :], start=False, stop=True)
            nc.tensor.matmul(aux[1][0:H, :], ident[0:8, H:2 * H], bs[:, :], start=True, stop=True).then_inc(cb_ps, 1)

            def by_token(kinds, idx, mh, ml, blocks, nk, at, width):
                for c in range(NC):
                    t = pe_tile(pe, kinds, idx(c))
                    ps = bank[t % NBANK][:, 0:width]
                    s = slice(c * P, (c + 1) * P)
                    for k in range(nk):
                        b = blocks[k * len(blocks) // nk]
                        o = at + k % (nk // len(blocks)) * width
                        h, l = wh[b % SPLIT][:, o:o + width], wl[b % SPLIT][:, o:o + width]
                        nc.tensor.matmul(ps, mh[:, k, s], h, start=(k == 0), stop=False)
                        nc.tensor.matmul(ps, mh[:, k, s], l, start=False, stop=False)
                        last = nc.tensor.matmul(ps, ml[:, k, s], h, start=False, stop=(k == nk - 1))
                    last.then_inc(gemm_done, 1)

            def pe_tile(pe, kind, idx):
                t = state["t"]
                assert pl.tiles[t][:2] == (kind, idx)
                state["t"] += 1
                pe.wait_ge(wl_ready, pl.tiles[t][2] + 1)
                eng, n = pl.read[t - NBANK]
                pe.wait_ge(bank_read[eng], n)
                return t

            for pair in range(2):
                if pair == 1:
                    gemm("qk2", 3)
                    pe.wait_ge(c4_ready, 1)
                    for c in range(NC):
                        last = nc.tensor.transpose(aux[2][:, H * c:H * c + H], c4[:, c * P:(c + 1) * P],
                                                   ident[0:H, 0:H])
                    last.then_inc(ct_ps, 1)
                b = pl.tiles[pl.at["v2", (pair, 0)]][2]
                by_token("v2", lambda c: (pair, c), ah, al, [b - 1, b], KD, 0, 256)
            def latent_norms():
                pe.wait_ge(ml_rn, 2)
                pe.wait_ge(dn_ready, 2)
                for j in range(3):
                    pe.wait_ge(lat_sq, j + 1)
                    nc.tensor.matmul(aux[j // 2][:, :], ones[:, :], sq[:, j % 2, :], start=(j != 1),
                                     stop=(j != 0)).then_inc(lat_ss, 1)

            def latents(kind, j):
                if kind == "uq2":
                    gemm("uq2", j, mov=(cqh, cql), ready=(cq_ready, 0) if j == 0 else None)
                elif kind == "uk2":
                    pe.wait_ge(cq_ready, 3)
                    for i in range(4):
                        gemm("uk2", i, mov=(ckh, ckl))
                else:
                    b = pl.tiles[pl.at["uv2", 0]][2]
                    by_token("uv2", lambda c: c, ckh, ckl, [b], 1, T, T)

            def scores(h, j):
                r, t = 64 * (h % 2), h // 2
                if h == 0 and j == 0:
                    pe.wait_ge(silu2_ready, 4)
                nc.tensor.matmul(aux[1 - j % 2][:, 0:T - j * P], k2[r:r + 64, t, j * P:(j + 1) * P],
                                 q2[r:r + 64, t, j * P:T], start=True, stop=True).then_inc(ms_ps, 1)

            def values(h, j):
                pe.wait_ge(s_done, 4 * h + j + 1)
                if j == 0 and h == 0:
                    evacuated(pe, "v2", (1, NC - 1))
                if j == 0 and h > 0:
                    pe.wait_ge(hm_ready, h)
                n = T - j * P
                nc.tensor.matmul(aux[2][:, j * P:T], v2[:, j, h * P:(h + 1) * P], st[:, j % 2, 0:n],
                                 start=(j == 0), stop=(j == NC - 1), skip_group_check=True)
                nc.tensor.matmul(aux[3][:, j * P:T], ones[:, :], st[:, j % 2, 0:n], start=(j == 0),
                                 stop=(j == NC - 1), skip_group_check=True).then_inc(nd_ps, 1)

            def mlstm(h, s):
                def spread(dst, r):
                    row = identr[r:r + H, r + h:r + h + 1].to_broadcast([H, P])
                    nc.tensor.matmul(dst[:, :], row, r4h[r:r + H, :], start=True, stop=False)
                    return nc.tensor.matmul(dst[:, :], row, r4l[r:r + H, :], start=False, stop=True)

                if s == 0:
                    pe.wait_ge(maxima_split, 1)
                    if h > 0:
                        pe.wait_ge(ml_rn, h)
                        pe.wait_ge(dn_ready, h)
                    if h == 2:
                        pe.wait_ge(lat_rn, 2)
                    spread(aux[0], 0).then_inc(mrow_ps, 1)
                    scores(h, 0)
                elif s == 1:
                    values(h, 0)
                    pe.wait_ge(wt_ready, 4 * h + 4)
                    scores(h, 1)
                elif s < 4:
                    pe.wait_ge(s_done, 4 * h + s - 1)
                    scores(h, s)
                    values(h, s - 1)
                elif s == 4:
                    pe.wait_ge(s_done, 4 * h + 3)
                    pe.wait_ge(floor_split, 1)
                    spread(aux[1], 32).then_inc(erow_ps, 1)
                    values(h, 3)
                elif s == 5:
                    pe.wait_ge(ml_sum, h + 1)
                    pe.wait_ge(s_done, 4 * h + 4)
                    nc.tensor.matmul(aux[0][:, :], ones[:, :], sq[:, 0, :], start=True, stop=True).then_inc(ml_ss, 1)

            NI = MLA_H * NC

            def att_scores(i):
                h, ib = i // NC, i % NC
                if i == 0:
                    evacuated(pe, "uk2", 3)
                    pe.wait_ge(kf_ready, MLA_H)
                    evacuated(pe, "uv2", NC - 1)
                    evacuated(pe, "uq2", MLA_H - 1)
                    pe.wait_ge(mask_ready, 1)
                if i >= 3:
                    pe.wait_ge(prob_ready, i - 2)
                n = (ib + 1) * P
                ps = bank[i % 3]
                nc.tensor.matmul(ps[:, 0:n], qf[:, h, ib * P:n], kf[:, h, 0:n], start=True, stop=False,
                                 skip_group_check=True)
                nc.tensor.matmul(ps[:, ib * P:n], ident16[:, :], mask16[:, :], start=False, stop=True,
                                 skip_group_check=True).then_inc(as_ps, 1)

            def att_values(h):
                pe.wait_ge(pt_evac, NC * (h + 1))
                if h == 0:
                    pe.wait_ge(hm_ready, H)
                if h >= 4 and h % 2 == 0:
                    pe.wait_ge(al_ready, KD * F_MIX2 + 4 + h // 2 - 1)
                r = 64 * (h % 2)
                for j in range(NC):
                    last = nc.tensor.matmul(pv[h // 2 % 2][r:r + 64, j * P:T], vt2[:, j, h * 64:(h + 1) * 64],
                                            pT[:, h % 2, j, j * P:T], start=(j == 0), stop=(j == NC - 1),
                                            skip_group_check=True)
                last.then_inc(pv_ps, 1)

            def attention(i):
                h, ib = i // NC, i % NC
                pe.wait_ge(prob_scaled, i + 1)
                if i >= 2:
                    pe.wait_ge(pt_evac, i - 1)
                else:
                    pe.wait_ge(dn_ready, H)
                for j in range(ib + 1):
                    last = nc.tensor.transpose(tb[i % 2][:, j * P:(j + 1) * P], pm[:, i % 3, j * P:(j + 1) * P], ident)
                last.then_inc(at_ps, 1)
                if i + 3 < NI:
                    att_scores(i + 3)
                if ib == 0 and h > 0:
                    att_values(h - 1)

            for kind, i, s in MIX2_STEPS:
                if kind == "mlstm":
                    mlstm(i, s)
                elif kind in ("proj0", "proj1", "proj2"):
                    gemm(i, s, part=(int(kind[4]), 3))
                elif kind == "latent_norms":
                    latent_norms()
                elif kind in ("uq2", "uk2", "uv2"):
                    latents(kind, i)
                elif kind == "attention_start":
                    for n in range(3):
                        att_scores(n)
            for i in range(NI):
                attention(i)
            att_values(MLA_H - 1)
            pe.wait_ge(pt_evac, NI)
            pe.wait_ge(prob_ready, NI)
            pe.wait_ge(al_ready, KD * F_MIX2 + 7)
            for m in range(KD - 1):
                gemm("wout2", m, ready=(al_ready, KD * F_MIX2) if m == 0 else None)
            gemm("wout2", KD - 1, part=(0, 2))
            ssq(4, early=True)
            gemm("wout2", KD - 1, part=(1, 2))
            ssq(4)
            ssq(5)

            def turn_acc(k):
                pe.wait_ge(acc_gained, k + 1)
                if k >= 2:
                    pe.wait_ge(at_evac, k - 1)
                transpose4(aux[1 + k % 2], acc[:, k, :]).then_inc(at_turned, 1)

            def turn_x(k):
                if k > 0:
                    pe.wait_ge(xt_evac, k)
                transpose4(aux[0], x[:, k, :]).then_inc(xt_turned, 1)

            def turns(m):
                turn_x(m)
                if m >= 2:
                    turn_acc(m - 2)

            mlp((("up2",), "down2"), MLP2, F_NORM5, 1, turns)
            turn_acc(KD - 2)
            pe.wait_ge(rstd_ready, 6)
            pe.wait_ge(sum_ready, SUM_BASE[6] + KD - 1)
            for c in range(NC):
                last = nc.tensor.matmul(aux[3][:, c:c + 1], rstd[:, c * P:(c + 1) * P], ones[:, 0:1], start=True,
                                        stop=True)
            last.then_inc(ssq_done, 1)
            turn_acc(KD - 1)

        def scalar_second(act, link, tables, tile, square, norm, upper, norm_upper):
            tile("gates2", 0)
            evacuated(act, "gates2", 0)
            link(nc.scalar.activation(lf[:, :], g2[:, :], ACT.Abs))
            link(nc.scalar.activation(lf[:, :], lf[:, :], ACT.Exp, scale=-1.0))
            nc.scalar.activation(lf[:, :], lf[:, :], ACT.Ln, bias=1.0).then_inc(logf_ready, 1)

            def conv_evac(j):
                if j >= 2:
                    act.wait_ge(conv2_done, j - 1)
                    act.wait_ge(silu2_ready, j - 1)
                act.wait_ge(gemm_done, pl.done("qk2", j))
                act.wait_ge(pads2_zero, 1)
                t = pl.at["qk2", j]
                nc.scalar.copy(craw2[j % 2][:, 3:3 + T], bank[t % NBANK][:, :])
                tile("qk2", j, lambda ps: nc.scalar.activation(cc2[j % 2][:, :], ps, ACT.Copy,
                                                               scale=g_of("conv_w_2", 12 + j)))

            def conv_silu(j):
                act.wait_ge(conv2_done, j + 1)
                dst = (q2 if j < 2 else k2)[:, j % 2, :]
                nc.scalar.activation(dst, cc2[j % 2][:, :], ACT.Silu, bias=g_of("conv_b_2", j)).then_inc(silu2_ready, 1)

            conv_evac(0)
            conv_evac(1)
            conv_silu(0)
            conv_evac(2)
            conv_silu(1)
            conv_silu(2)
            for pair in range(2):
                if pair == 1:
                    conv_evac(3)
                for c in range(NC):
                    tile("v2", (pair, c), lambda ps: nc.scalar.copy(v2[:, c, pair * 256:(pair + 1) * 256],
                                                                    ps[:, 0:256]))
                    if pair == 1 and c == 0:
                        conv_silu(3)
                        for i in range(2):
                            act.wait_ge(rope_args, i + 1)
                            nc.scalar.activation(trig[:, i, :], trig[:, i, :], ACT.Sin).then_inc(trig_ready, 1)
                        act.wait_ge(em_args, 1)
                        tables(LN_EXP_TABLES)
                        floor = em4[32:32 + H, :]
                        nc.scalar.activation(floor, floor, ACT.Exp, scale=-1.0).then_inc(em_ready, 1)

            def latent_norms():
                evacuated(act, "ckv2", 0)
                act.wait_ge(ml_ss, 2)
                for j in range(3):
                    if j == 2:
                        act.wait_ge(lat_ss, 1)
                    nc.scalar.activation(sq[:, j % 2, :], cq[:, j, :], ACT.Square).then_inc(lat_sq, 1)
                act.wait_ge(s_done, 8)
                for j in range(2):
                    act.wait_ge(lat_ss, 2 + j)
                    rn = wt[:, j * T:(j + 1) * T]
                    link(nc.scalar.activation(rn, aux[j][:, :], ACT.Ln, bias=eps[:, 0:1],
                                              scale=(1.0 / QR, 1.0 / KVR)[j]))
                    nc.scalar.activation(rn, rn, ACT.Exp, scale=-0.5).then_inc(lat_rn, 1)

            def proj(kind, j):
                if kind == "o2":
                    o = og[:, j, :]
                    tile("o2", j, lambda ps: nc.scalar.activation(o, ps, ACT.Exp, scale=-1.0))
                    evacuated(act, "o2", j)
                    link(nc.scalar.activation(o, o, ACT.Ln, bias=1.0))
                    nc.scalar.activation(o, o, ACT.Exp, scale=-1.0).then_inc(og_ready, 1)
                elif kind == "kr2":
                    tile("kr2", 0)
                else:
                    tile(kind, j, lambda ps: nc.scalar.copy(cq[:, j if kind == "cq2" else 2, :], ps))

            def keys(j):
                def read(ps):
                    nc.scalar.copy(kf[0:64, 2 * j, :], ps[0:64, :])
                    return nc.scalar.copy(kf[0:64, 2 * j + 1, :], ps[64:P, :])
                tile("uk2", j, read)

            def latents(kind, j):
                if kind == "uq2":
                    act.wait_ge(kr_ready, 1)
                    nc.scalar.copy(kf[64:P, j, :], krr[64:P, :]).then_inc(kf_ready, 1)
                    tile("uq2", j)
                elif kind == "uk2":
                    for i in range(4):
                        keys(i)
                else:
                    for c in range(NC):
                        tile("uv2", c)

            def mlstm(h, s):
                if s == 0:
                    act.wait_ge(mrow_ps, h + 1)
                    act.wait_ge(ct_ready, 1)
                    if h > 0:
                        act.wait_ge(s_done, 4 * h)
                    if h == 2:
                        act.wait_ge(cq_ready, 3)
                    for j in range(NC):
                        nc.scalar.activation(wt[:, WT[j]:WT[j] + T - j * P], aux[0][:, j * P:T], ACT.Exp,
                                             bias=cT[:, j, h:h + 1], scale=-1.0).then_inc(wt_ready, 1)
                elif s == 4:
                    act.wait_ge(erow_ps, h + 1)
                    if h > 0:
                        act.wait_ge(h32_ready, H32_BASE[F_MIX2] + h)
                    nc.scalar.copy(hm[:, :], aux[1][:, :]).then_inc(erow_ready, 1)
                    act.wait_ge(nd_ps, 4 * h + 4)
                    if h > 0:
                        act.wait_ge(ml_ss, h)
                        if h == 2:
                            act.wait_ge(lat_ss, 3)
                    else:
                        act.wait_ge(h32_ready, H32_BASE[F_MIX2])
                    act.wait_ge(dn_ready, h + 1)
                    nc.scalar.activation(sq[:, 0, :], aux[2][:, :], ACT.Square).then_inc(ml_sq, 1)
                    nc.scalar.activation(sq[:, 1, :], dn[:, :], ACT.Square, scale=EPS ** 0.5).then_inc(ml_sq, 1)
                elif s == 5:
                    act.wait_ge(ml_ss, h + 1)
                    if h > 0:
                        act.wait_ge(h32_ready, H32_BASE[F_MIX2] + h)
                    link(nc.scalar.activation(rstd[:, :], aux[0][:, :], ACT.Ln, scale=1.0 / P))
                    nc.scalar.activation(rstd[:, :], rstd[:, :], ACT.Exp, scale=-0.5).then_inc(ml_rn, 1)

            NI = MLA_H * NC

            def turned(i):
                h, ib = i // NC, i % NC
                act.wait_ge(at_ps, i + 1)
                if i >= 2 * NC:
                    act.wait_ge(pv_ps, h - 1)
                nc.scalar.copy(pT[:, h % 2, 0:ib + 1, ib * P:(ib + 1) * P],
                               tb[i % 2][:, 0:(ib + 1) * P].rearrange("p (j n) -> p j n", n=P)).then_inc(pt_evac, 1)

            def exps(i):
                n = (i % NC + 1) * P
                act.wait_ge(max_ready, i + 1)
                if i >= 3:
                    act.wait_ge(at_ps, i - 2)
                nc.scalar.activation(pm[:, i % 3, 0:n], bank[i % 3][:, 0:n], ACT.Exp, bias=am[:, 0, i:i + 1],
                                     accum_out=am[:, 1, i:i + 1]).then_inc(prob_ready, 1)

            for kind, i, s in MIX2_STEPS:
                if kind == "mlstm":
                    mlstm(i, s)
                elif kind == "proj2":
                    proj(i, s)
                elif kind == "latent_norms":
                    latent_norms()
                elif kind in ("uq2", "uk2", "uv2"):
                    latents(kind, i)
                elif kind == "fill":
                    upper(F_MIX2, i, i, h32[:, i % 3, :], (h32_ready, H32_BASE[F_MIX2] + i + 1))
                elif kind == "attention_start":
                    exps(0)
                    exps(1)
            for i in range(NI):
                turned(i)
                if i + 2 < NI:
                    exps(i + 2)
                if i in SPLIT_AT:
                    t = SPLIT_AT.index(i)
                    upper(F_MIX2, 4 + t, 4 + t, pv[t % 2][:, :], (pv_ps, 2 * t + 2))
            upper(F_MIX2, 7, 7, pv[1][:, :], (pv_ps, MLA_H))
            for m in range(KD):
                if m > 0:
                    evacuated(act, "wout2", m - 1)
                    square(4, m - 1, acc[:, m - 1, :])
                tile("wout2", m)
            evacuated(act, "wout2", KD - 1)
            square(4, KD - 1, acc[:, KD - 1, :])
            norm(4)
            for k in range(KD):
                act.wait_ge(x_mixed, k + 1)
                square(5, k, x[:, k, :])
            norm_upper(5, F_NORM5)
            def gained(k):
                evacuated(act, "down2", (len(MLP2) - 1, k))
                square(6, k, acc[:, k, :])
                act.wait_ge(sq_ready, SQ_BASE[6] + k + 1)
                nc.scalar.activation(acc[:, k, :], acc[:, k, :], ACT.Copy,
                                     scale=g_of("norm_post_mlp_2", k)).then_inc(acc_gained, 1)

            def acc_turned(k):
                act.wait_ge(at_turned, k + 1)
                if k == 0:
                    act.wait_ge(gemm_done, pl.done("down2", (len(MLP2) - 2, KD - 1)))
                nc.scalar.copy(atok[:, :, k * P:(k + 1) * P], auxh[1 + k % 2][:, :, :]).then_inc(at_evac, 1)

            n = [0]
            for c in range(len(MLP2) + 1):
                if c < len(MLP2):
                    for j in range(MLP2[c]):
                        i = n[0]
                        n[0] += 1
                        if i >= 1:
                            act.wait_ge(relu_sq, i)
                        tile("up2", (c, j), lambda ps: nc.scalar.activation(rl[:, :], ps, ACT.Relu))
                        evacuated(act, "up2", (c, j))
                        if i >= 2:
                            act.wait_ge(y_ready[1], i - 1)
                        nc.scalar.activation(y32[:, i % 2, :], rl[:, :], ACT.Square).then_inc(relu_sq, 1)
                if c > 0:
                    for m in range(KD):
                        if c == len(MLP2) and m > 0:
                            gained(m - 1)
                        if c == len(MLP2) and m > 2:
                            acc_turned(m - 3)
                        tile("down2", (c - 1, m))
            acc_turned(KD - 3)
            gained(KD - 1)
            acc_turned(KD - 2)
            act.wait_ge(ssq_done, SSQ_END[5] + 1)
            link(nc.scalar.activation(rcol[:, :], aux[3][:, 0:NC], ACT.Ln, bias=eps[:, 0:1], scale=1.0 / D))
            nc.scalar.activation(rcol[:, :], rcol[:, :], ACT.Exp, scale=-0.5).then_inc(rstd_ready, 1)
            acc_turned(KD - 1)

        def vector_second(dve, link, tile, freed, lower, norm_fill, add_square):
            for i in range(2):
                nc.vector.memset(craw2[i][:, 0:3], 0.0)
            nc.vector.memset(rtmp[:, :], 0.0).then_inc(pads2_zero, 1)
            ps = tile("gates2", 0)
            freed(nc.vector.tensor_scalar(g2[:, :], ps[0:8, :], cols[0:8, 3:4], None, ALU.add))
            evacuated(dve, "gates2", 0)
            dve.wait_ge(logf_ready, 1)
            link(nc.vector.scalar_tensor_tensor(lf[:, :], g2[:, :], 0.0, lf[:, :], ALU.min, ALU.subtract))
            for c in range(NC):
                s = slice(c * P, (c + 1) * P)
                link(nc.vector.tensor_tensor_scan(bs[:, s], ones[0:8, :], lf[:, s],
                                                  bs[:, c * P - 1:c * P] if c else 0.0, ALU.mult, ALU.add))
            nc.vector.tensor_scalar(nbs[:, :], bs[:, :], -1.0, None, ALU.mult).then_inc(forget_sums_ready, 1)

            def conv(j):
                r, c = craw2[j % 2], cc2[j % 2]
                evacuated(dve, "qk2", j)
                for tap in (2, 1, 0):
                    i = nc.vector.scalar_tensor_tensor(c[:, :], r[:, tap:tap + T], g_of("conv_w_2", 4 * tap + j),
                                                       c[:, :], ALU.mult, ALU.add)
                    if tap:
                        link(i)
                i.then_inc(conv2_done, 1)

            conv(0)
            dve.wait_ge(cb_ps, 1)
            nc.vector.tensor_copy(c4[:, :], aux[0][0:H, :]).then_inc(c4_ready, 1)
            dve.wait_ge(c4_ready, 1)
            link(nc.vector.tensor_tensor_scan(m4[:, :], c4[:, :], c4[:, :], 0.0, ALU.max, ALU.max))
            floor = em4[32:32 + H, :]
            nc.vector.tensor_tensor(floor, aux[1][0:H, :], m4[:, :], ALU.add).then_inc(em_sums, 1)
            link(nc.vector.tensor_copy(r4h[0:H, :], m4[:, :]))
            nc.vector.tensor_tensor(r4l[0:H, :], m4[:, :], r4h[0:H, :].bitcast(F32),
                                    ALU.subtract).then_inc(maxima_split, 1)
            dve.wait_ge(em_sums, 1)
            nc.vector.tensor_scalar(floor, floor, FLOOR_MIN, None, ALU.max).then_inc(em_args, 1)
            conv(1)
            conv(2)
            dve.wait_ge(pos_loaded, 16)
            link(nc.vector.tensor_copy(ang[:, :], posi[:, :]))
            link(nc.vector.tensor_scalar(ang[:, :], ang[:, :], cst[:, C_INV:C_INV + 1], None, ALU.mult))
            for i, turns in enumerate((0.0, 0.25)):
                r = trig[:, i, :]
                link(nc.vector.tensor_scalar(turn[:, :], ang[:, :], 1.0 / TWO_PI, turns, ALU.mult, ALU.add))
                link(nc.vector.tensor_scalar(turn[:, :], turn[:, :], ROUND, None, ALU.add))
                link(nc.vector.tensor_scalar(turn[:, :], turn[:, :], -ROUND, None, ALU.add))
                link(nc.vector.scalar_tensor_tensor(r, turn[:, :], -TURN_PARTS[0], ang[:, :], ALU.mult, ALU.add))
                link(nc.vector.scalar_tensor_tensor(r, turn[:, :], -TURN_PARTS[1], r, ALU.mult, ALU.add))
                link(nc.vector.scalar_tensor_tensor(r, turn[:, :], -TURN_PARTS[2], r, ALU.mult, ALU.add))
                link(nc.vector.tensor_scalar(r, r, turns * TWO_PI, None, ALU.add))
                nc.vector.tensor_scalar(r, r, PI_BELOW, -PI_BELOW, ALU.min, ALU.max).then_inc(rope_args, 1)
            conv(3)
            dve.wait_ge(ct_ps, 1)
            nc.vector.tensor_copy(cT[:, :, :], aux[2][:, 0:NC * H].rearrange("p (c h) -> p c h", h=H)).then_inc(
                ct_ready, 1)
            dve.wait_ge(h32_ready, H32_BASE[F_NORM3] + KD)
            dve.wait_ge(rstd_ready, 4)
            for k in range(KD):
                nc.vector.scalar_tensor_tensor(x[:, k, :], x[:, k, :], g_of("final_g", k), rstd[:, :], ALU.mult,
                                               ALU.mult)
            dve.wait_ge(trig_ready, 2)
            link(nc.vector.tensor_scalar(trig[:, 0, :], trig[:, 0, :], cst[:, C_SGN:C_SGN + 1], None, ALU.mult))

            def rope(dst, ps, scale):
                nc.vector.scalar_tensor_tensor(dst, ps[64:96, :], scale, trig[64:96, 1, :], ALU.mult, ALU.mult)
                return nc.vector.scalar_tensor_tensor(rtmp[64:96, :], ps[96:P, :], scale, trig[96:P, 0, :], ALU.mult,
                                                      ALU.mult)

            def rope_key():
                ps = tile("kr2", 0)
                dve.wait_ge(pads2_zero, 1)
                freed(rope(krr[64:96, :], ps, 1.0))
                evacuated(dve, "kr2", 0)
                link(nc.vector.tensor_tensor(krr[64:96, :], krr[64:96, :], rtmp[64:96, :], ALU.add))
                nc.vector.tensor_copy(krr[96:P, :], krr[64:96, :]).then_inc(kr_ready, 1)
                nc.vector.memset(trig[0:64, 1, :], 1.0)
                link(nc.vector.tensor_copy(trig[96:P, 1, :], trig[96:P, 0, :]))

            def latent_norms():
                for j in range(3):
                    dve.wait_ge(lat_rn, 1 + j // 2)
                    gain = g_of("q_norm_2", j) if j < 2 else g_of("kv_norm_2", 0)
                    hi, lo = (cqh[:, j, :], cql[:, j, :]) if j < 2 else (ckh[:, 0, :], ckl[:, 0, :])
                    c = cq[:, j, :]
                    link(nc.vector.scalar_tensor_tensor(c, c, gain, wt[:, j // 2 * T:j // 2 * T + T], ALU.mult,
                                                        ALU.mult))
                    link(nc.vector.tensor_copy(hi, c))
                    nc.vector.tensor_tensor(lo, c, hi.bitcast(F32), ALU.subtract).then_inc(cq_ready, 1)
                dve.wait_ge(cq_ready, 3)

            def query(h):
                ps = tile("uq2", h)
                freed(nc.vector.scalar_tensor_tensor(qf[:, h, :], ps, ATT_SCALE, trig[:, 1, :], ALU.mult, ALU.mult))

            def weighted(h, j):
                n = T - j * P
                w = wt[:, WT[j]:WT[j] + n]
                dve.wait_ge(wt_ready, 4 * h + j + 1)
                link(nc.vector.scalar_tensor_tensor(w[:, 0:P], w[:, 0:P], 1.0, cst[:, C_UP:C_UP + P], ALU.min,
                                                    ALU.mult))
                dve.wait_ge(ms_ps, 4 * h + j + 1)
                if 4 * h + j >= 2:
                    dve.wait_ge(nd_ps, 4 * h + j - 1)
                nc.vector.scalar_tensor_tensor(st[:, j % 2, 0:n], aux[1 - j % 2][:, 0:n], 0.125, w, ALU.mult,
                                               ALU.mult).then_inc(s_done, 1)

            def mlstm(h, s):
                if s < 4:
                    weighted(h, s)
                elif s == 4:
                    dve.wait_ge(nd_ps, 4 * (h + 1))
                    dve.wait_ge(erow_ready, h + 1)
                    if h > 0:
                        dve.wait_ge(ml_sq, 2 * h)
                    link(nc.vector.scalar_tensor_tensor(hm[:, :], aux[3][:, :], -1.0, hm[:, :], ALU.mult, ALU.max))
                    nc.vector.tensor_tensor(dn[:, :], aux[3][:, :], hm[:, :], ALU.max).then_inc(dn_ready, 1)
                elif s == 6:
                    dve.wait_ge(dn_ready, h + 1)
                    dve.wait_ge(ml_rn, h + 1)
                    nc.vector.scalar_tensor_tensor(hm[:, :], aux[2][:, :], g_of("ml_head_norm_2", h), rstd[:, :],
                                                   ALU.mult, ALU.mult).then_inc(hm_ready, 1)
                    dve.wait_ge(hm_ready, h + 1)
                    dve.wait_ge(og_ready, h + 1)
                    dve.wait_ge(al_ready, KD * F_MIX2 + max(0, h - 2))
                    nc.vector.tensor_tensor(h32[:, h % 3, :], hm[:, :], og[:, h, :], ALU.mult).then_inc(h32_ready, 1)

            NI = MLA_H * NC

            dve.wait_ge(em_ready, 1)
            floor = em4[32:32 + H, :]
            link(nc.vector.tensor_copy(r4h[32:32 + H, :], floor))
            nc.vector.tensor_tensor(r4l[32:32 + H, :], floor, r4h[32:32 + H, :].bitcast(F32),
                                    ALU.subtract).then_inc(floor_split, 1)
            link(nc.vector.tensor_copy(ident16[:, :], ident))
            nc.vector.tensor_copy(mask16[:, :], cst[:, C_NEG:C_NEG + P]).then_inc(mask_ready, 1)

            def maxima(i):
                n = (i % NC + 1) * P
                dve.wait_ge(as_ps, i + 1)
                nc.vector.tensor_reduce(am[:, 0, i:i + 1], bank[i % 3][:, 0:n], AX_X, ALU.max, negate=True).then_inc(
                    max_ready, 1)

            def normed(i):
                n = (i % NC + 1) * P
                dve.wait_ge(prob_ready, i + 1)
                link(nc.vector.reciprocal(am[:, 2, i:i + 1], am[:, 1, i:i + 1]))
                nc.vector.tensor_scalar(pm[:, i % 3, 0:n], pm[:, i % 3, 0:n], am[:, 2, i:i + 1], None,
                                        ALU.mult).then_inc(prob_scaled, 1)

            for kind, i, s in MIX2_STEPS:
                if kind == "mlstm":
                    mlstm(i, s)
                elif kind == "proj2" and i == "kr2":
                    rope_key()
                elif kind == "latent_norms":
                    latent_norms()
                elif kind == "uq2":
                    query(i)
                elif kind == "uv2":
                    for c in range(NC):
                        ps = tile("uv2", c)
                        freed(nc.vector.tensor_copy(vt2[:, c, :], ps))
                elif kind == "fill":
                    lower(F_MIX2, i, i, h32[:, i % 3, :])
                elif kind == "attention_start":
                    for n in range(3):
                        maxima(n)
                    normed(0)
            for i in range(NI):
                if i + 1 < NI:
                    normed(i + 1)
                if i + 3 < NI:
                    maxima(i + 3)
                if i in SPLIT_AT:
                    t = SPLIT_AT.index(i)
                    lower(F_MIX2, 4 + t, 4 + t, pv[t % 2][:, :])
            lower(F_MIX2, 7, 7, pv[1][:, :])

            for m in range(KD):
                ps = tile("wout2", m)
                freed(nc.vector.tensor_copy(acc[:, m, :], ps))
                add_square(4, m - 1)

            def add_normed(n, gain, done):
                dve.wait_ge(rstd_ready, n + 1)
                for k in range(KD):
                    if k >= 3:
                        dve.wait_ge(done, k - 2)
                    link(nc.vector.scalar_tensor_tensor(h32[:, k % 3, :], acc[:, k, :], g_of(gain, k), rstd[:, :],
                                                        ALU.mult, ALU.mult))
                    nc.vector.tensor_tensor(x[:, k, :], x[:, k, :], h32[:, k % 3, :], ALU.add).then_inc(done, 1)

            evacuated(dve, "wout2", KD - 1)
            dve.wait_ge(al_ready, KD * (F_MIX2 + 1))
            add_normed(4, "norm_post_mix_2", x_mixed)
            dve.wait_ge(x_mixed, KD)
            norm_fill(5, F_NORM5, "norm_pre_mlp_2", 0)
            n = 0
            for c in range(len(MLP2) + 1):
                if c < len(MLP2):
                    for j in range(MLP2[c]):
                        if c >= 2 and j == 0:
                            dve.wait_ge(gemm_done, pl.done("down2", (c - 2, KD - 1)))
                        dve.wait_ge(relu_sq, n + 1)
                        y = y32[:, n % 2, :]
                        link(nc.vector.tensor_copy(yh[c % 2][:, j, :], y))
                        nc.vector.tensor_tensor(yl[c % 2][:, j, :], y, yh[c % 2][:, j, :].bitcast(F32),
                                                ALU.subtract).then_inc(y_ready[1], 1)
                        n += 1
                if c > 0:
                    for m in range(KD):
                        ps = tile("down2", (c - 1, m))
                        if c == 1:
                            freed(nc.vector.tensor_copy(acc[:, m, :], ps))
                        else:
                            evacuated(dve, "down2", (c - 2, m))
                            freed(nc.vector.tensor_tensor(acc[:, m, :], ps, acc[:, m, :], ALU.add))
                        if c == len(MLP2):
                            add_square(6, m - 1)
                            if m == 0:
                                dve.wait_ge(gemm_done, pl.done("down2", (len(MLP2) - 2, KD - 1)))
                            dve.wait_ge(xt_turned, m + 1)
                            nc.vector.tensor_copy(xtok2[:, :, m * P:(m + 1) * P], auxh[0][:, :, :]).then_inc(xt_evac, 1)
            add_square(6, KD - 1)
            dve.wait_ge(rstd_ready, 7)
            dve.wait_ge(at_evac, KD)
            dve.wait_ge(xt_evac, KD)
            for c in range(NC):
                nc.vector.scalar_tensor_tensor(xtok2[:, c, :], atok[:, c, :], rcol[:, c:c + 1], xtok2[:, c, :], ALU.mult,
                                               ALU.add).then_inc(out_ready, 1)

        def stores(sp):
            for c in range(NC):
                sp.wait_ge(out_ready, c + 1)
                sp.dma_start(out[0, c * P:(c + 1) * P, :], xtok2[:, c, :]).then_inc(out_stored, 16)
            sp.wait_ge(out_stored, 16 * NC)

        block = ctx.enter_context(nc.Block())

        @block.sync
        def _(sp):
            sp.dma_start(cst[:, C_ID:C_ID + P], ins["constants"][:, C_ID:C_ID + P]).then_inc(ident_loaded, 16)
            for c in range(NC):
                sp.dma_start(xtok[:, c, :], ins["x"][0, c * P:(c + 1) * P, :]).then_inc(x_loaded[c], 16)
            for b in range(len(pl.blocks)):
                if b == RAW:
                    parameters(sp)
                if b >= RAW:
                    sp.wait_ge(wl_ready, b - RAW + 1)
                for dst, src in parts(b):
                    sp.dma_start(dst, src).then_inc(raw_loaded[b % RAW], 16)
            stores(sp)

        @block.gpsimd
        def _(pool):
            count = [0]

            def link(i):
                count[0] += 1
                i.then_inc(pool_step, 1)
                pool.wait_ge(pool_step, count[0])

            nc.gpsimd.memset(bw[:, :, :], 0.0).then_inc(bw_zero, 1)
            pool.wait_ge(bw_zero, 1)
            for g in range(4):
                r = 64 * (g % 2)
                pool.dma_start(bw[r:r + 64, g // 2, r:r + 64], ins["pool_w"][0, g]).then_inc(bw_loaded, 16)
            sum_at = [split_before(("mlstm", h, 4)) for h in range(H)]
            pool_at = pl.tiles[pl.at["cb", 1]][2]
            for b in range(len(pl.blocks)):
                pool.wait_ge(wh_ready, b + 1)
                w = block_cols(b)
                nc.gpsimd.tensor_tensor(wl[b % SPLIT][:, 0:w], raw[b % RAW][:, 0:w],
                                        wh[b % SPLIT][:, 0:w].bitcast(F32), ALU.subtract).then_inc(wl_ready, 1)
                if b == pool_at:
                    multiscale(pool, link)
                for h in range(H):
                    if b == sum_at[h]:
                        pool.wait_ge(ml_sq, 2 * (h + 1))
                        nc.gpsimd.tensor_tensor(sq[:, 0, :], sq[:, 0, :], sq[:, 1, :], ALU.add).then_inc(ml_sum, 1)

        @block.tensor
        def _(pe):
            state = dict(t=0)

            def gemm(kind, idx, mov=None, ready=None, order=None, part=None):
                t = state["t"]
                k_, i_, b, col, nk, stride = pl.tiles[t]
                assert (k_, i_) == (kind, idx), (k_, i_, kind, idx)
                state["t"] += 1
                pe.wait_ge(wl_ready, b + 1)
                if t >= NBANK:
                    eng, n = pl.read[t - NBANK]
                    pe.wait_ge(bank_read[eng], n)
                mh, ml = mov or (ah, al)
                h, l = wh[b % SPLIT], wl[b % SPLIT]
                ps = bank[t % NBANK][:, :]
                if part and part[0] < part[1] - 1:
                    state["t"] -= 1
                for n, k in enumerate(order or range(nk)):
                    if part and n * part[1] // nk != part[0]:
                        continue
                    if ready:
                        pe.wait_ge(ready[0], ready[1] + n + 1)
                    c = k * stride + col
                    nc.tensor.matmul(ps, h[:, c:c + P], mh[:, k, :], start=(n == 0), stop=False)
                    nc.tensor.matmul(ps, l[:, c:c + P], mh[:, k, :], start=False, stop=False)
                    last = nc.tensor.matmul(ps, h[:, c:c + P], ml[:, k, :], start=False, stop=(n == nk - 1))
                if not part or part[0] == part[1] - 1:
                    last.then_inc(gemm_done, 1)

            def gemm_pair(first, second, ready, order=None):
                t = state["t"]
                state["t"] += 2
                assert (pl.tiles[t][:2], pl.tiles[t + 1][:2]) == (first, second)
                pe.wait_ge(wl_ready, pl.tiles[t + 1][2] + 1)
                if t >= NBANK:
                    for u in (t, t + 1):
                        eng, n = pl.read[u - NBANK]
                        pe.wait_ge(bank_read[eng], n)
                for n, k in enumerate(order or range(KD)):
                    pe.wait_ge(ready[0], ready[1] + n + 1)
                    c = slice(k * P, k * P + P)
                    for u in (t, t + 1):
                        b = pl.tiles[u][2] % SPLIT
                        ps = bank[u % NBANK][:, :]
                        nc.tensor.matmul(ps, wh[b][:, c], ah[:, k, :], start=(n == 0), stop=False)
                        nc.tensor.matmul(ps, wl[b][:, c], ah[:, k, :], start=False, stop=False)
                        last = nc.tensor.matmul(ps, wh[b][:, c], al[:, k, :], start=False, stop=(n == KD - 1))
                        if n == KD - 1:
                            last.then_inc(gemm_done, 1)

            def ssq(n, early=None):
                if n > 0:
                    pe.wait_ge(rstd_ready, n)
                if n in SUM_BASE and (early or n < 2):
                    pe.wait_ge(sum_ready, SUM_BASE[n] + (5 if n else KD - 1))
                    nc.tensor.matmul(aux[3][:, :], ones[:, :], rstd[:, :], start=True, stop=(n == 0)).then_inc(ssq_done, 1)
                if n == 0:
                    return
                for k in range(*((6, KD) if n < 2 else (0, KD) if n == 5 else (6, 7) if early else (7, KD))):
                    pe.wait_ge(sq_ready, SQ_BASE[n] + k + 1)
                    nc.tensor.matmul(aux[3][:, :], ones[:, :], sq[:, k % 2, :], start=(n == 5 and k == 0),
                                     stop=(k == KD - 1)).then_inc(ssq_done, 1)

            def transpose4(dst, src):
                for c in range(NC):
                    last = nc.tensor.transpose(dst[:, c * P:(c + 1) * P], src[:, c * P:(c + 1) * P], ident)
                return last

            pe.wait_ge(ident_loaded, 16)
            for c in range(NC):
                pe.wait_ge(x_loaded[c], 16)
                for k in range(KD):
                    last = nc.tensor.transpose((bank + aux)[k][:, c * P:(c + 1) * P], xtok[:, c, k * P:(k + 1) * P],
                                               ident)
                    if c == NC - 1:
                        last.then_inc(xt_ps, 1)
            pe.wait_ge(ones_set, 1)
            pe.wait_ge(x_ready, KD)
            pe.wait_ge(gain_loaded, 16)
            nc.tensor.transpose(aux[2][:, 0:KD], prow[0:KD, 0, :], ident[0:KD, 0:KD]).then_inc(par_ps, 1)
            ssq(0)

            gemm_pair(("ab", 0), ("k", 0), (al_ready, 0))
            pe.wait_ge(consts_loaded, 16 * len(PARAMS))
            nc.tensor.transpose(aux[0][:, 0:PSPLIT], prow[0:PSPLIT, 0, :], ident[0:PSPLIT, 0:PSPLIT])
            n2 = NPARAM - PSPLIT
            nc.tensor.transpose(aux[0][:, P:P + n2], prow[0:n2, 1, :], ident[0:n2, 0:n2]).then_inc(par_ps, 1)
            gemm("k", 1)
            gemm("k", 2)
            pe.wait_ge(par_ready, 2)
            pe.wait_ge(decay_sums_ready, 1)
            pe.wait_ge(beta_ready, 1)
            for r in range(2 * H):
                if r >= 2:
                    pe.wait_ge(rows_ready, r - 1)
                row = identr[0:8, r:r + 1].to_broadcast([8, P])
                if r % H == 0:
                    pe.wait_ge(rows_split, 1 + r // H)
                nc.tensor.matmul(aux[r % 2][:, :], row, (gch if r < H else gbh)[:, :], start=True, stop=False)
                nc.tensor.matmul(aux[r % 2][:, :], row, (gcl if r < H else gbl)[:, :], start=False,
                                 stop=True).then_inc(rows_ps, 1)
            for c in range(NC):
                nc.tensor.transpose(aux[2][:, 16 * c:16 * c + 8], gcs[:, c * P:(c + 1) * P], ident[0:8, 0:8])
                last = nc.tensor.transpose(aux[2][:, 16 * c + 8:16 * c + 16], gbt[:, c * P:(c + 1) * P],
                                           ident[0:8, 0:8])
            last.then_inc(gt_ps, 1)
            gemm("k", 3)
            gemm("q", 0)
            gemm("q", 1)
            gemm("q", 2)

            def head_sums(j0):
                for j in range(j0, j0 + H):
                    pe.wait_ge(head_sq, j + 1)
                    if j == 0:
                        pe.wait_ge(rows_ready, 2 * H)
                        pe.wait_ge(gt_ready, 1)
                        pe.wait_ge(rstd_ready, 1)
                    if j >= H:
                        pe.wait_ge(head_rn, j - H + 1)
                        if j % H >= 2:
                            pe.wait_ge(kd_ready, H)
                    nc.tensor.matmul(aux[j % 4][:, :], ones[:, :], hsq[:, j % H, :], start=True,
                                     stop=True).then_inc(head_ss, 1)

            head_sums(0)
            gemm("q", 3)
            gemm("v", 0)
            for h in range(H):
                pe.wait_ge(head_normed, h + 1)
                pe.wait_ge(head_rn, H)
                if h >= 2:
                    pe.wait_ge(kd_ready, h - 1)
                transpose4(aux[2 + h % 2], kT[:, h, :]).then_inc(kt_ps, 1)
            gemm("v", 1)
            gemm("v", 2)
            head_sums(H)

            def v_transposes(h):
                pe.wait_ge(silu_ready, 2 * H + h + 1)
                pe.wait_ge(head_rn, 2 * H)
                if h >= 2:
                    pe.wait_ge(bv_ready, h - 1)
                transpose4(aux[2 + h % 2], vT[h % 2][:, :]).then_inc(vt_ps, 1)

            gemm("v", 3)
            gemm("hp", 0)
            v_transposes(0)
            v_transposes(1)
            gemm("hp", 1)
            v_transposes(2)
            v_transposes(3)
            pe.wait_ge(head_normed, 2 * H)
            for c in range(NC):
                if c < 2:
                    pe.wait_ge(bv_ready, H)
                else:
                    pe.wait_ge(at_ready, c - 1)
                s = slice(c * P, (c + 1) * P)
                for h in range(H):
                    nc.tensor.matmul(auxh[2 * (c % 2)][:, h, :], kT[:, h, s], kT[:, h, s], start=True, stop=True)
                for h in range(H):
                    last = nc.tensor.matmul(auxh[2 * (c % 2) + 1][:, h, :], kT[:, h, s], qT[:, h, s],
                                            start=True, stop=True)
                last.then_inc(gram_ps, 1)
                gemm("ch", c // 2, part=(c % 2, 2))

            for pair in range(2):
                for lev in range(LEVELS):
                    n0 = INV_PAIR * pair + 2 * lev
                    m0 = (INV_PAIR - 2) * pair + 2 * (lev - 1)
                    if lev > 0:
                        gemm(*INV_FILL[pair, lev][0], part=(INV_FILL[pair, lev][1], 3))
                    for e in range(2):
                        pe.wait_ge(um_ready, n0 + e + 1)
                        if lev == 0:
                            if pair == 0:
                                pe.wait_ge(at_ready, NC)
                            else:
                                pe.wait_ge(xy_ready, INV_PAIR)
                            for h in range(H):
                                last = nc.tensor.transpose(auxh[2 * e + 1][:, h, :], UM[:, e, h, :], ident)
                            last.then_inc(xy_ps, 1)
                            continue
                        pe.wait_ge(xy_ready, n0 + e - 1)
                        for h in range(H):
                            last = nc.tensor.matmul(auxh[2 * e][:, h, :], UM[:, e, h, :], X[:, e, h, :],
                                                    start=True, stop=True)
                        last.then_inc(p_ps, 1)
                    if lev == 0:
                        continue
                    for e in range(2):
                        pe.wait_ge(p_ready, m0 + e + 1)
                        c = 2 * pair + e
                        if lev < LEVELS - 1:
                            for h in range(H):
                                nc.tensor.matmul(auxh[2 * e + 1][:, h, :], Y[:, c, h, :], PS[:, e, h, :],
                                                 start=True, stop=True)
                        for h in range(H):
                            last = nc.tensor.matmul(auxh[2 * e][:, h, :], PS[:, e, h, :], Y[:, c, h, :],
                                                    start=True, stop=True)
                        last.then_inc(xy_ps, 1)

            for c in range(NC):
                s = slice(c * P, (c + 1) * P)
                if c == 0:
                    pe.wait_ge(xy_ready, 2 * INV_PAIR)
                else:
                    pe.wait_ge(s_ready, H * c)
                    for h in range(H):
                        last = nc.tensor.matmul(auxh[0][:, h, :], kT[:, h, s], S[c % 2][:, h, :], start=True, stop=True)
                    last.then_inc(ks_ps, 1)
                if c > 0:
                    gemm("z", c - 1, part=(1, 2))
                    pe.wait_ge(rr_ready, c)
                    pe.wait_ge(vn_ready, c)
                for h in range(H):
                    last = nc.tensor.matmul(auxh[1][:, h, :], Y[:, c, h, :],
                                            bv[:, 0, h, :] if c == 0 else rr[:, h, :], start=True, stop=True)
                last.then_inc(vn_ps, 1)
                gemm("z", c, part=(0, 2))
                if c > 0:
                    pe.wait_ge(o_ready, c)
                pe.wait_ge(vn_ready, c + 1)
                if c < NC - 1:
                    for h in range(H):
                        last = nc.tensor.matmul(auxh[3][:, h, :], kd[:, c, h, :], vn[:, h, :], start=True, stop=True)
                    last.then_inc(su_ps, 1)
                if c == 1:
                    pe.wait_ge(qg_ready, H)
                for h in range(H):
                    if c > 0:
                        nc.tensor.matmul(auxh[2][:, h, :], S[c % 2][:, h, :], qg[:, h, s], start=True, stop=False)
                    last = nc.tensor.matmul(auxh[2][:, h, :], vn[:, h, :], AT[:, c, h, :], start=(c == 0), stop=True)
                last.then_inc(o_ps, 1)
            gemm("z", 3, part=(1, 2))
            pe.wait_ge(bw_loaded, 64)
            for t in range(2):
                pe.wait_ge(pooled_ready, t + 1)
                nc.tensor.matmul(aux[t][:, :], bw[:, t, :], pooled[:, t, :], start=True, stop=True).then_inc(pool_ps, 1)
            for h in range(H):
                pe.wait_ge(osq_ready, h + 1)
                if h == 2:
                    pe.wait_ge(h32_ready, H32_BASE[F_MIX1] + 2)
                bk = (2, 3, 0, 1)[h]
                nc.tensor.matmul(aux[bk][:, :], ones[:, :], sq[:, h % 2, :], start=True, stop=True).then_inc(oss_ps, 1)
            gemm_pair(("wout", 0), ("wout", 1), (al_ready, KD * F_MIX1), order=MIX1_ORDER)
            for m in range(2, KD - 1):
                gemm("wout", m, order=MIX1_ORDER)
            pe.wait_ge(ptok_loaded, 16)
            pe.wait_ge(orn_ready, H)
            for k in range(2):
                for c in range(NC):
                    last = nc.tensor.transpose(aux[k][:, c * P:(c + 1) * P], ptok[:, c, k * P:(k + 1) * P], ident)
                last.then_inc(pt_ps, 1)
            gemm("wout", KD - 1, order=MIX1_ORDER)
            gemm("proj", 0, mov=(ph, plo), ready=(pt_ready, 0))
            ssq(1)
            for j in range(1, KD):
                gemm("proj", j, mov=(ph, plo))
            tensor_rest(pe, gemm, gemm_pair, ssq, transpose4, state)

        @block.scalar
        def _(act):
            count = [0]
            nxt = [0]
            tnow = [0]

            def link(i):
                count[0] += 1
                i.then_inc(act_step, 1)
                act.wait_ge(act_step, count[0])

            def tables(n):
                act.add_instruction(mybir.InstLoadActFuncSet(name=nc.get_next_instruction_name(), act_func_set_id=n,
                                                             ins=[], outs=[]))

            def split(upto):
                while nxt[0] < len(pl.blocks) and (nxt[0] < SPLIT or pl.last[nxt[0] - SPLIT] <= upto):
                    b = nxt[0]
                    act.wait_ge(raw_loaded[b % RAW], landed(b))
                    if b >= SPLIT:
                        act.wait_ge(gemm_done, pl.last[b - SPLIT] + 1)
                    w = block_cols(b)
                    nc.scalar.copy(wh[b % SPLIT][:, 0:w], raw[b % RAW][:, 0:w]).then_inc(wh_ready, 1)
                    nxt[0] += 1

            def tile(kind, idx, read=None):
                t = tnow[0]
                assert pl.tiles[t][:2] == (kind, idx), (pl.tiles[t], kind, idx)
                tnow[0] += 1
                if read is not None:
                    assert pl.READER[kind] == "act"
                    act.wait_ge(gemm_done, t + 1)
                    read(bank[t % NBANK][:, :]).then_inc(bank_read["act"], 1)
                split(t)

            def square(n, k, src):
                if n in SUM_BASE and k == 0:
                    if n in RSTD_FREE:
                        act.wait_ge(*RSTD_FREE[n])
                    nc.scalar.activation(rstd[:, :], src, ACT.Square).then_inc(sq_ready, 1)
                    return
                if n in SUM_BASE and k >= 3:
                    act.wait_ge(sum_ready, SUM_BASE[n] + k - 2)
                elif n not in SUM_BASE and k >= 2:
                    act.wait_ge(ssq_done, SSQ_BASE[n] + k - 1)
                elif SSQ_BASE[n] > 0:
                    act.wait_ge(ssq_done, SSQ_BASE[n])
                nc.scalar.activation(sq[:, k % 2, :], src, ACT.Square).then_inc(sq_ready, 1)

            def norm(n, scale=1.0 / D):
                act.wait_ge(ssq_done, SSQ_END[n])
                if n == 5:
                    act.wait_ge(*RSTD_FREE[n])
                link(nc.scalar.activation(rstd[:, :], aux[3][:, :], ACT.Ln, bias=eps[:, 0:1], scale=scale))
                nc.scalar.activation(rstd[:, :], rstd[:, :], ACT.Exp, scale=-0.5).then_inc(rstd_ready, 1)

            def upper(fill, i, k, src, wait):
                if i == 0 and fill > 0:
                    act.wait_ge(gemm_done, LAST_USE[fill - 1])
                    act.wait_ge(al_ready, KD * fill)
                act.wait_ge(*wait)
                nc.scalar.copy(ah[:, k, :], src).then_inc(ah_ready, 1)

            tables(LN_EXP_TABLES)
            for k in range(KD):
                act.wait_ge(x_ready, k + 1)
                square(0, k, x[:, k, :])
            split(-1)
            act.wait_ge(eps_set, 1)
            norm(0)
            act.wait_ge(cols_loaded, 48)
            nc.scalar.activation(cols[0:8, 2:3], cols[0:8, 1:2], ACT.Exp).then_inc(alog_exp, 1)
            for k in range(KD):
                upper(F_NORM1, k, k, h32[:, k % 3, :], (h32_ready, k + 1))

            tile("ab", 0)
            evacuated(act, "ab", 0)
            link(nc.scalar.activation(gsp[:, :], gab[:, :], ACT.Abs))
            link(nc.scalar.activation(gsp[:, :], gsp[:, :], ACT.Exp, scale=-1.0))
            nc.scalar.activation(gsp[:, :], gsp[:, :], ACT.Ln, bias=1.0).then_inc(softplus_ready, 1)
            act.wait_ge(log_beta_ready, 1)
            nc.scalar.activation(gbt[:, :], gbt[:, :], ACT.Exp).then_inc(beta_ready, 1)

            def conv_evac(j):
                kind, h = HEADS[j]
                if j >= 2:
                    act.wait_ge(conv_done, j - 1)
                    act.wait_ge(silu_ready, j - 1)
                tap = g_of("conv_qkv", 3 * 12 + conv_tile(j))
                t = tnow[0]
                act.wait_ge(gemm_done, t + 1)
                act.wait_ge(pads_zero, 1)
                nc.scalar.copy(craw[j % 2][:, 3:3 + T], bank[t % NBANK][:, :])
                tile(kind, h, lambda ps: nc.scalar.activation(cc[j % 2][:, :], ps, ACT.Copy, scale=tap))

            def conv_silu(j):
                kind, h = HEADS[j]
                act.wait_ge(conv_done, j + 1)
                if kind == "v" and h >= 2:
                    act.wait_ge(vt_ps, h - 1)
                dst = vT[h % 2][:, :] if kind == "v" else {"k": kT, "q": qT}[kind][:, h, :]
                nc.scalar.activation(dst, cc[j % 2][:, :], ACT.Silu).then_inc(silu_ready, 1)

            conv_evac(0)
            conv_evac(1)
            conv_silu(0)
            conv_evac(2)
            for r in range(2 * H):
                act.wait_ge(rows_ps, r + 1)
                nc.scalar.copy((GR if r < H else BR)[:, r % H, :], aux[r % 2][:, :]).then_inc(rows_ready, 1)
            conv_silu(1)
            act.wait_ge(eg_args, 1)
            tables(LN_EXP_TABLES)
            nc.scalar.activation(eg[:, 0, :, :], gT[:, :, 0:H], ACT.Exp)
            nc.scalar.activation(eg[:, 1, :, :], eg[:, 3, :, :], ACT.Exp)
            nc.scalar.activation(eg[:, 2, :, :], GR[:, :, :].rearrange("p h (c t) -> p c h t", c=NC)[:, :, :, P - 1],
                                 ACT.Exp).then_inc(eg_exps, 1)
            conv_evac(3)
            conv_silu(2)
            conv_evac(4)
            conv_silu(3)

            def head_norm(j0):
                src = kT if j0 == 0 else qT
                if j0 == 0:
                    act.wait_ge(rows_ready, 2 * H)
                    act.wait_ge(gt_ps, 1)
                else:
                    act.wait_ge(head_ss, H)
                for j in range(j0, j0 + H):
                    act.wait_ge(silu_ready, j + 1)
                    nc.scalar.activation(hsq[:, j % H, :], src[:, j % H, :], ACT.Square).then_inc(head_sq, 1)
                tables(LN_EXP_TABLES)
                for j in range(j0, j0 + H):
                    act.wait_ge(head_ss, j + 1)
                    if j == 0:
                        act.wait_ge(al_ready, KD)
                    if j >= 2:
                        act.wait_ge(head_normed, j - 1)
                    link(nc.scalar.activation(h32[:, j % 2, :], aux[j % 4][:, :], ACT.Ln, bias=eps[:, 0:1]))
                    nc.scalar.activation(h32[:, j % 2, :], h32[:, j % 2, :], ACT.Exp, scale=-0.5).then_inc(head_rn, 1)

            act.wait_ge(ssq_done, SSQ_END[0])
            conv_evac(5)
            head_norm(0)
            conv_silu(4)
            conv_evac(6)
            conv_silu(5)
            conv_evac(7)
            conv_silu(6)
            conv_evac(8)
            conv_silu(7)
            conv_evac(9)
            head_norm(H)
            conv_silu(8)
            conv_evac(10)
            conv_silu(9)
            conv_evac(11)
            conv_silu(10)
            conv_silu(11)
            tables(LN_EXP_TABLES)
            for c in range(NC):
                act.wait_ge(dt_args, c + 1)
                nc.scalar.activation(AT[:, c], AT[:, c], ACT.Exp).then_inc(dt_exp, 1)
            for h in range(H):
                nc.scalar.activation(GR[:, h, :], GR[:, h, :], ACT.Exp).then_inc(gr_exp, 1)
            for t in range(2):
                tile("hp", t, lambda ps: nc.scalar.copy(pin[:, t, 16:16 + T], ps))
            tile("ch", 0)
            tile("ch", 1)
            for pair in range(2):
                for lev in range(1, LEVELS):
                    m0 = (INV_PAIR - 2) * pair + 2 * (lev - 1)
                    for e in range(2):
                        act.wait_ge(p_ps, m0 + e + 1)
                        nc.scalar.copy(PS[:, e], auxh[2 * e][:, :, :]).then_inc(p_ready, 1)
                    if INV_FILL[pair, lev][1] == 2:
                        tile(*INV_FILL[pair, lev][0])

            def z_tile(h):
                act.wait_ge(qg_ready, H)
                tile("z", h, lambda ps: nc.scalar.activation(zs[:, h, :], ps, ACT.Silu))

            for c in range(NC):
                act.wait_ge(vn_ps, c + 1)
                if c > 0:
                    act.wait_ge(o_ps, c)
                else:
                    act.wait_ge(xy_ready, 2 * INV_PAIR)
                nc.scalar.copy(vn[:, :, :], auxh[1][:, :, :]).then_inc(vn_ready, 1)
                if c > 0:
                    z_tile(c - 1)
                act.wait_ge(o_ps, c + 1)
                if c == 0:
                    act.wait_ge(qg_ready, H)
                    act.wait_ge(pooled_ready, 2)
                nc.scalar.copy(oT[:, :, c * P:(c + 1) * P], auxh[2][:, :, :]).then_inc(o_ready, 1)
            act.wait_ge(o_ready, NC)
            for h in range(H):
                if h >= 2:
                    act.wait_ge(oss_ps, h - 1)
                nc.scalar.activation(sq[:, h % 2, :], oT[:, h, :], ACT.Square).then_inc(osq_ready, 1)
                if h == 1:
                    z_tile(3)
            for i in range(2):
                upper(F_MIX1, i, MIX1_ORDER[i], h32[:, i % 3, :], (h32_ready, H32_BASE[F_MIX1] + i + 1))
            for i in range(2):
                upper(F_MIX1, 2 + i, MIX1_ORDER[2 + i], convd[:, i, :], when_read("cb", i))
            tables(LN_EXP_TABLES)
            for h in range(H):
                act.wait_ge(oss_ps, h + 1)
                if h >= 2:
                    act.wait_ge(h32_ready, H32_BASE[F_MIX1] + 2 + h - 1)
                rn = orn[h % 2]
                link(nc.scalar.activation(rn[:, :], aux[(2, 3, 0, 1)[h]][:, :], ACT.Ln, bias=eps[:, 0:1],
                                          scale=1.0 / P))
                nc.scalar.activation(rn[:, :], rn[:, :], ACT.Exp, scale=-0.5).then_inc(orn_ready, 1)
                if h > 0:
                    upper(F_MIX1, 3 + h, h - 1, h32[:, (1 + h) % 3, :], (h32_ready, H32_BASE[F_MIX1] + 2 + h))
            upper(F_MIX1, 7, 3, h32[:, 5 % 3, :], (h32_ready, H32_BASE[F_MIX1] + 6))
            act.wait_ge(al_ready, KD * (F_MIX1 + 1))
            act.dma_start(ptok[:, :, :], ins["p"][0, 0].rearrange("(c p) n -> p c n", p=P)).then_inc(ptok_loaded, 16)
            for m in range(KD):
                tile("wout", m)
                if m > 0:
                    evacuated(act, "wout", m - 1)
                    square(1, m - 1, x[:, m - 1, :])
                if m == KD - 2:
                    for k in range(2):
                        act.wait_ge(pt_ps, k + 1)
                        nc.scalar.copy(ph[:, k, :], aux[k][:, :]).then_inc(ph_ready, 1)
            evacuated(act, "wout", KD - 1)
            square(1, KD - 1, x[:, KD - 1, :])
            scalar_rest(act, link, tables, tile, square, norm, upper)

        @block.vector
        def _(dve):
            count = [0]
            tnow = [0]

            def link(i):
                count[0] += 1
                i.then_inc(dve_step, 1)
                dve.wait_ge(dve_step, count[0])

            def tile(kind, idx):
                while pl.READER[pl.tiles[tnow[0]][0]] != "dve":
                    tnow[0] += 1
                t = tnow[0]
                assert pl.tiles[t][:2] == (kind, idx), (pl.tiles[t], kind, idx)
                tnow[0] += 1
                dve.wait_ge(gemm_done, t + 1)
                return bank[t % NBANK][:, :]

            def freed(i):
                return i.then_inc(bank_read["dve"], 1)

            def lower(fill, i, k, src):
                dve.wait_ge(ah_ready, KD * fill + i + 1)
                nc.vector.tensor_tensor(al[:, k, :], src, ah[:, k, :].bitcast(F32), ALU.subtract).then_inc(al_ready, 1)

            def add_square(n, k):
                if 1 <= k <= (KD - 1 if n in (0, 6) else 5):
                    dve.wait_ge(sq_ready, SQ_BASE[n] + k + 1)
                    if k > 1:
                        dve.wait_ge(sum_ready, SUM_BASE[n] + k - 1)
                    nc.vector.tensor_tensor(rstd[:, :], rstd[:, :], sq[:, k % 2, :], ALU.add).then_inc(sum_ready, 1)

            def norm_fill(n, fill, gain, base):
                dve.wait_ge(rstd_ready, n + 1)
                for k in range(KD):
                    if fill or k >= 3:
                        dve.wait_ge(al_ready, KD * fill + max(0, k - 2))
                    i = nc.vector.scalar_tensor_tensor(h32[:, k % 3, :], x[:, k, :], g_of(gain, k), rstd[:, :],
                                                       ALU.mult, ALU.mult)
                    i.then_inc(h32_ready, 1)
                    if k > 0:
                        lower(fill, k - 1, k - 1, h32[:, (k - 1) % 3, :])
                lower(fill, KD - 1, KD - 1, h32[:, (KD - 1) % 3, :])

            nc.vector.memset(ones[:, :], 1.0).then_inc(ones_set, 1)
            nc.vector.memset(eps2[:, :], EPS * EPS)
            nc.vector.memset(eps[:, :], EPS).then_inc(eps_set, 1)
            nc.vector.memset(cols[:, :], 0.0).then_inc(cols_zero, 1)
            for i in range(2):
                nc.vector.memset(craw[i][:, 0:3], 0.0)
                nc.vector.memset(cin[:, i, 0:2], 0.0)
            for k in range(KD):
                dve.wait_ge(xt_ps, k + 1)
                nc.vector.tensor_copy(x[:, k, :], (bank + aux)[k][:, :]).then_inc(x_ready, 1)
                if k > 3:
                    add_square(0, k - 3)
            for k in (5, 6, 7):
                add_square(0, k)
            dve.wait_ge(par_ps, 1)
            nc.vector.tensor_copy(par[:, 0:KD], aux[2][:, 0:KD]).then_inc(par_ready, 1)
            dve.wait_ge(par_ready, 1)
            dve.wait_ge(x_ready, KD)
            norm_fill(0, F_NORM1, "norm1_g", 0)
            dve.wait_ge(par_ps, 2)
            nc.vector.tensor_copy(par[:, KD:PSPLIT], aux[0][:, KD:PSPLIT])
            nc.vector.tensor_copy(par[:, PSPLIT:NPARAM], aux[0][:, P:P + NPARAM - PSPLIT]).then_inc(par_ready, 1)
            nc.vector.memset(pin[:, 0, 0:16], 0.0)
            nc.vector.memset(pin[:, 1, 0:16], 0.0).then_inc(pads_zero, 1)
            dve.wait_ge(par_ready, 2)

            ps = tile("ab", 0)
            dve.wait_ge(cols_loaded, 48)
            freed(nc.vector.tensor_scalar(gab[:, :], ps[0:8, :], cols[0:8, 0:1], None, ALU.add))
            evacuated(dve, "ab", 0)
            dve.wait_ge(alog_exp, 1)
            link(nc.vector.tensor_scalar(cols[0:8, 2:3], cols[0:8, 2:3], -1.0, None, ALU.mult))
            dve.wait_ge(softplus_ready, 1)
            nc.vector.scalar_tensor_tensor(gbt[:, :], gab[:, :], 0.0, gsp[:, :], ALU.min,
                                           ALU.subtract).then_inc(log_beta_ready, 1)
            dve.wait_ge(log_beta_ready, 1)
            link(nc.vector.scalar_tensor_tensor(gsp[:, :], gab[:, :], 0.0, gsp[:, :], ALU.max, ALU.add))
            link(nc.vector.tensor_scalar(gsp[:, :], gsp[:, :], cols[0:8, 2:3], None, ALU.mult))
            for c in range(NC):
                s = slice(c * P, (c + 1) * P)
                last = nc.vector.tensor_tensor_scan(gcs[:, s], ones[0:8, :], gsp[:, s], 0.0, ALU.mult, ALU.add)
            last.then_inc(decay_sums_ready, 1)
            dve.wait_ge(decay_sums_ready, 1)
            nc.vector.tensor_copy(identr[:, :], ident[:, 0:64])
            link(nc.vector.tensor_copy(gch[:, :], gcs[:, :]))
            nc.vector.tensor_tensor(gcl[:, :], gcs[:, :], gch[:, :].bitcast(F32), ALU.subtract).then_inc(rows_split, 1)
            dve.wait_ge(beta_ready, 1)
            link(nc.vector.tensor_copy(gbh[:, :], gbt[:, :]))
            nc.vector.tensor_tensor(gbl[:, :], gbt[:, :], gbh[:, :].bitcast(F32), ALU.subtract).then_inc(rows_split, 1)

            def conv(j):
                r, c = craw[j % 2], cc[j % 2]
                evacuated(dve, *HEADS[j])
                for tap in (2, 1, 0):
                    i = nc.vector.scalar_tensor_tensor(c[:, :], r[:, tap:tap + T],
                                                       g_of("conv_qkv", 12 * tap + conv_tile(j)), c[:, :],
                                                       ALU.mult, ALU.add)
                    if tap:
                        link(i)
                i.then_inc(conv_done, 1)

            def head_norm(j):
                dve.wait_ge(head_rn, j + 1)
                dst = (kT if j < H else qT)[:, j % H, :]
                rn = h32[:, j % 2, :]
                if j < H:
                    i = nc.vector.tensor_tensor(dst, dst, rn, ALU.mult)
                else:
                    i = nc.vector.scalar_tensor_tensor(dst, dst, float(P) ** -0.5, rn, ALU.mult, ALU.mult)
                i.then_inc(head_normed, 1)

            def over_chunks(col):
                return col.unsqueeze(2).to_broadcast([P, NC, P])

            conv(0)
            conv(1)
            conv(2)
            dve.wait_ge(gt_ps, 1)
            nc.vector.tensor_copy(gT[:, :, :], aux[2][:, 0:16 * NC].rearrange("p (c n) -> p c n", n=16)).then_inc(
                gt_ready, 1)
            dve.wait_ge(gt_ready, 1)
            dve.wait_ge(rows_ready, H)
            last_g = GR[:, :, :].rearrange("p h (c t) -> p c h t", c=NC)[:, :, :, P - 1]
            nc.vector.tensor_tensor(eg[:, 3, :, :], last_g, gT[:, :, 0:H], ALU.subtract).then_inc(eg_args, 1)
            dve.wait_ge(eg_exps, 1)
            link(nc.vector.tensor_tensor(eg[:, 0, :, :], eg[:, 0, :, :], gT[:, :, 12:16], ALU.mult))
            conv(3)
            conv(4)
            conv(5)
            for j in range(H):
                head_norm(j)
            for h in range(H):
                dve.wait_ge(kt_ps, h + 1)
                nc.vector.tensor_tensor(kd[:, :, h, :], auxh[2 + h % 2][:, :, :], over_chunks(eg[:, 1, :, h]),
                                        ALU.mult).then_inc(kd_ready, 1)
                if h == 1:
                    conv(6)
            conv(7)
            conv(8)
            conv(9)
            for j in range(H, 2 * H):
                head_norm(j)

            def scaled_v(h):
                dve.wait_ge(vt_ps, h + 1)
                nc.vector.tensor_tensor(bv[:, :, h, :], auxh[2 + h % 2][:, :, :], over_chunks(gT[:, :, 12 + h]),
                                        ALU.mult).then_inc(bv_ready, 1)

            conv(10)
            scaled_v(0)
            scaled_v(1)
            conv(11)
            dve.wait_ge(rows_ready, 2 * H)
            for c in range(NC):
                for h in range(H):
                    i = nc.vector.tensor_scalar(AT[:, c, h, :], GR[:, h, c * P:(c + 1) * P], gT[:, c, h:h + 1], 0.0,
                                                ALU.subtract, ALU.min)
                i.then_inc(dt_args, 1)
                if c == 1:
                    scaled_v(2)
                if c == 2:
                    scaled_v(3)

            def over_heads(m):
                return m.unsqueeze(1).to_broadcast([P, H, P])

            for c in range(NC):
                dve.wait_ge(dt_exp, c + 1)
                link(nc.vector.tensor_tensor(AT[:, c], AT[:, c], over_heads(cst[:, C_UP:C_UP + P]), ALU.mult))
                dve.wait_ge(gram_ps, c + 1)
                link(nc.vector.tensor_tensor(U[:, c], auxh[2 * (c % 2)][:, :, :], AT[:, c], ALU.mult))
                nc.vector.tensor_tensor(U[:, c], U[:, c], BR[:, :, c * P:(c + 1) * P], ALU.mult)
                nc.vector.tensor_tensor(AT[:, c], auxh[2 * (c % 2) + 1][:, :, :], AT[:, c], ALU.mult).then_inc(
                    at_ready, 1)
            dve.wait_ge(at_ready, NC)

            def ch_tile(t):
                ps = tile("ch", t)
                freed(nc.vector.tensor_copy(cin[:, t, 2:2 + T], ps))

            def cc_tile(t):
                ps = tile("cc", t)
                evacuated(dve, "ch", t)
                freed(nc.vector.tensor_tensor(cin[:, t, 2:2 + T], ps, cin[:, t, 2:2 + T], ALU.mult))

            def cb_tile(t):
                evacuated(dve, "cc", t)
                d = convd[:, t, :]
                link(nc.vector.tensor_scalar(d, cin[:, t, 2:2 + T], g_of("sconv_w", 4 + t), None, ALU.mult))
                for tap in (1, 0):
                    link(nc.vector.scalar_tensor_tensor(d, cin[:, t, tap:tap + T], g_of("sconv_w", 2 * tap + t), d,
                                                        ALU.mult, ALU.add))
                ps = tile("cb", t)
                freed(nc.vector.tensor_tensor(d, ps, d, ALU.mult))

            for pair in range(2):
                for lev in range(LEVELS):
                    m0 = (INV_PAIR - 2) * pair + 2 * (lev - 1)
                    n0 = INV_PAIR * pair + 2 * lev
                    mask = over_heads(cst[:, C_LEV + lev * P:C_LEV + (lev + 1) * P])
                    if lev == 0:
                        if pair:
                            dve.wait_ge(p_ps, INV_PAIR - 2)
                        for e in range(2):
                            nc.vector.tensor_tensor(UM[:, e], U[:, 2 * pair + e], mask, ALU.mult).then_inc(um_ready, 1)
                            dve.wait_ge(um_ready, n0 + e + 1)
                            nc.vector.tensor_tensor(Y[:, 2 * pair + e], over_heads(ident), UM[:, e], ALU.subtract)
                    if lev == 0:
                        for e in range(2):
                            dve.wait_ge(xy_ps, n0 + e + 1)
                            nc.vector.tensor_tensor(X[:, e], over_heads(ident), auxh[2 * e + 1][:, :, :],
                                                    ALU.subtract).then_inc(xy_ready, 1)
                        nxt = over_heads(cst[:, C_LEV + P:C_LEV + 2 * P])
                        for e in range(2):
                            dve.wait_ge(xy_ready, n0 + e + 1)
                            nc.vector.tensor_tensor(UM[:, e], U[:, 2 * pair + e], nxt, ALU.mult).then_inc(um_ready, 1)
                        if pair == 0:
                            ch_tile(0)
                            ch_tile(1)
                        continue
                    if lev < LEVELS - 1:
                        nxt = over_heads(cst[:, C_LEV + (lev + 1) * P:C_LEV + (lev + 2) * P])
                        for e in range(2):
                            dve.wait_ge(p_ps, m0 + e + 1)
                            nc.vector.tensor_tensor(UM[:, e], U[:, 2 * pair + e], nxt, ALU.mult).then_inc(um_ready, 1)
                    if pair == 0 and lev <= H:
                        h = lev - 1
                        dve.wait_ge(gr_exp, h + 1)
                        nc.vector.tensor_tensor(qg[:, h, :], qT[:, h, :], GR[:, h, :], ALU.mult).then_inc(qg_ready, 1)
                    if INV_FILL[pair, lev][1] == 2:
                        kind, t = INV_FILL[pair, lev][0]
                        (cc_tile if kind == "cc" else cb_tile)(t)
                    for e in range(2):
                        c = 2 * pair + e
                        dve.wait_ge(xy_ready, n0 + e - 1)
                        dve.wait_ge(xy_ps, n0 + e + 1)
                        if lev < LEVELS - 1:
                            nc.vector.tensor_tensor(X[:, e], X[:, e], auxh[2 * e + 1][:, :, :], ALU.subtract)
                        nc.vector.tensor_tensor(Y[:, c], Y[:, c], auxh[2 * e][:, :, :], ALU.subtract).then_inc(
                            xy_ready, 1)

            for c in range(NC):
                if c > 0:
                    dve.wait_ge(ks_ps, c)
                    link(nc.vector.tensor_tensor(t1[:, :, :], auxh[0][:, :, :],
                                                 eg[:, 0, c, :].unsqueeze(2).to_broadcast([P, H, P]), ALU.mult))
                    nc.vector.tensor_tensor(rr[:, :, :], bv[:, c], t1[:, :, :], ALU.subtract).then_inc(rr_ready, 1)
                if c < NC - 1:
                    dve.wait_ge(su_ps, c + 1)
                    if c == 0:
                        nc.vector.tensor_copy(S[1][:, :, :], auxh[3][:, :, :]).then_inc(s_ready, H)
                        continue
                    dve.wait_ge(o_ps, c)
                    dve.wait_ge(s_ready, H * c)
                    for h in range(H):
                        nc.vector.scalar_tensor_tensor(S[(c + 1) % 2][:, h, :], S[c % 2][:, h, :], eg[:, 2, c, h:h + 1],
                                                       auxh[3][:, h, :], ALU.mult, ALU.add).then_inc(s_ready, 1)
            for i in range(2):
                dve.wait_ge(pool_ps, i + 1)
                nc.vector.tensor_scalar(h32[:, i, :], aux[i][:, :], g_of("pool_scale", i), None, ALU.mult).then_inc(
                    h32_ready, 1)
            for i in range(2):
                lower(F_MIX1, i, MIX1_ORDER[i], h32[:, i, :])
            for i in range(2):
                lower(F_MIX1, 2 + i, MIX1_ORDER[2 + i], convd[:, i, :])
            for h in range(H):
                dve.wait_ge(orn_ready, h + 1)
                o = oT[:, h, :]
                link(nc.vector.scalar_tensor_tensor(o, o, g_of("onorm_g", 0), orn[h % 2][:, :], ALU.mult, ALU.mult))
                evacuated(dve, "z", h)
                nc.vector.tensor_tensor(h32[:, (2 + h) % 3, :], o, zs[:, h, :], ALU.mult).then_inc(h32_ready, 1)
                if h > 0:
                    lower(F_MIX1, 3 + h, h - 1, h32[:, (1 + h) % 3, :])
            lower(F_MIX1, 7, 3, h32[:, 5 % 3, :])
            for m in range(KD):
                if m == KD - 1:
                    for k in range(2):
                        dve.wait_ge(ph_ready, k + 1)
                        nc.vector.tensor_tensor(plo[:, k, :], aux[k][:, :], ph[:, k, :].bitcast(F32),
                                                ALU.subtract).then_inc(pt_ready, 1)
                ps = tile("wout", m)
                freed(nc.vector.tensor_tensor(x[:, m, :], ps, x[:, m, :], ALU.add))
                add_square(1, m - 1)
            vector_rest(dve, link, tile, freed, lower, norm_fill, add_square)


INPUTS = ["x", "p", "norm1_g", "w_in", "conv_qkv", "a_log", "dt_bias", "onorm_g", "pool_w", "pool_scale", "sconv_w",
          "w_out", "norm2_g", "w_gate", "w_up", "w_down", "ple_proj", "ple_gate", "final_g", "positions_2",
          "norm_pre_mix_2", "w_in_2", "b_gates_2", "conv_w_2", "conv_b_2", "ml_head_norm_2", "q_norm_2", "w_uq_2",
          "kv_norm_2", "w_ukv_2", "w_out_2", "norm_post_mix_2", "norm_pre_mlp_2", "w_up_2", "w_down_2",
          "norm_post_mlp_2"]


def kernel(**inputs):
    import concourse.bacc as bacc
    from concourse.bass_utils import run_bass_kernel_spmd

    nc = bacc.Bacc("TRN2", target_bir_lowering=False, num_devices=1)
    arrays, aps = {}, {}
    for name in INPUTS:
        a = np.ascontiguousarray(inputs[name])
        arrays[f"in_{name}"] = a
        aps[name] = nc.dram_tensor(f"in_{name}", a.shape, mybir.dt.from_np(a.dtype), kind="ExternalInput").ap()
    arrays["constants"] = constant_table()
    aps["constants"] = nc.dram_tensor("constants", (P, NCST), F32, kind="ExternalInput").ap()
    out = nc.dram_tensor("out", (1, T, D), F32, kind="ExternalOutput").ap()
    build(nc, aps, out)
    r = run_bass_kernel_spmd(nc, [arrays], core_ids=[0])
    return r.results[0]["out"]
```
